# Optimizing a Trainium2 kernel written in Bass

```python
import jax, jax.numpy as jnp
from jax import lax
import numpy as np

D_MODEL = 1024
BATCH = 1
SEQ = 256
DEPTH = 2

GRID_W = 64
CTX_LEN = 256
N_MIXERS = 2
HEAD_SIZE = 64
N_HEADS = D_MODEL // HEAD_SIZE
DECAY_LORA = 64
ICLR_LORA = 64
VRES_LORA = 32
GATE_LORA = 128
GN_EPS = 64e-5
N_DIR = 2
CHUNK = 128
SG_GROUPS = 16
SG_FFN = 4 * D_MODEL
SG_HALF = SG_FFN // 2
N_EXPERTS = 16
N_EXPERT_GROUPS = 4
TOP_K = 2
EXPERT_FFN = 512
N_MOD = 6
NORM_EPS = 1e-6
LN_EPS = 1e-5

kernel_name = "hybrid_rwkv7_chunksgu_groupmoe_prefix"

def rms_norm(x, g):
    xf = x.astype(jnp.float32)
    y = xf * lax.rsqrt(jnp.mean(xf * xf, axis=-1, keepdims=True) + NORM_EPS)
    return (y * g.astype(jnp.float32)).astype(x.dtype)

def layer_norm(x, g, b):
    xf = x.astype(jnp.float32)
    mu = jnp.mean(xf, axis=-1, keepdims=True)
    var = jnp.mean(jnp.square(xf - mu), axis=-1, keepdims=True)
    return ((xf - mu) * lax.rsqrt(var + LN_EPS) * g.astype(jnp.float32) + b.astype(jnp.float32)).astype(x.dtype)

def modulation(cvec, w, b):
    m = jax.nn.silu(cvec) @ w + b
    m = m.reshape(-1, 1, N_MOD, m.shape[-1] // N_MOD)
    return tuple(m[:, :, j, :] for j in range(N_MOD))

def ada_norm(x, g, shift, scale):
    return rms_norm(x, g) * (1 + scale) + shift

def shift_1d(x):
    half = x.shape[-1] // 2
    prev = jnp.pad(x[:, :-1, :half], ((0, 0), (1, 0), (0, 0)))
    nxt = jnp.pad(x[:, 1:, half:], ((0, 0), (0, 1), (0, 0)))
    return jnp.concatenate([prev, nxt], axis=-1)

def shift_grid(x):
    B, L, D = x.shape
    rows = L // GRID_W
    q = D // 4
    g = x.reshape(B, rows, GRID_W, D)
    left = jnp.pad(g[:, :, :-1, :q], ((0, 0), (0, 0), (1, 0), (0, 0)))
    right = jnp.pad(g[:, :, 1:, q:2 * q], ((0, 0), (0, 0), (0, 1), (0, 0)))
    up = jnp.pad(g[:, :-1, :, 2 * q:3 * q], ((0, 0), (1, 0), (0, 0), (0, 0)))
    down = jnp.pad(g[:, 1:, :, 3 * q:], ((0, 0), (0, 1), (0, 0), (0, 0)))
    return jnp.concatenate([left, right, up, down], axis=-1).reshape(B, L, D)

def wkv_scan(decay, k, v, kk, a, r, s0, reverse):
    seq = [decay, k, v, kk, a] + ([] if r is None else [r])
    xs = tuple(jnp.moveaxis(t, 1, 0) for t in seq)

    def step(s, inp):
        w_t, k_t, v_t, kk_t, a_t = inp[:5]
        sa = jnp.einsum('bhvk,bhk->bhv', s, kk_t)
        s = (s * w_t[:, :, None, :]
             - sa[..., None] * (kk_t * a_t)[:, :, None, :]
             + v_t[..., None] * k_t[:, :, None, :])
        y = None if r is None else jnp.einsum('bhvk,bhk->bhv', s, inp[5])
        return s, y

    s_fin, ys = lax.scan(step, s0, xs, reverse=reverse)
    return (None if r is None else jnp.moveaxis(ys, 0, 1)), s_fin

def rwkv7_bidir(h_ctx, h_lat, v_first, ctx_out, mu, w_r, w_k, w_v, w_o, w0, w1, w2, a0, a1, a2, vres,
                g1, g2, k_k, k_a, r_k, lnx_g, lnx_b):
    B, Lc, D = h_ctx.shape
    H, N = N_HEADS, HEAD_SIZE
    lo = 0 if ctx_out else Lc
    h = jnp.concatenate([h_ctx, h_lat], axis=1)
    xx = jnp.concatenate([shift_1d(h_ctx), shift_grid(h_lat)], axis=1) - h
    xw, xk, xv, xa = (h + xx * mu[j] for j in (1, 2, 3, 4))
    xr = h[:, lo:] + xx[:, lo:] * mu[0]
    xg = h[:, lo:] + xx[:, lo:] * mu[5]
    k = xk @ w_k
    v = xv @ w_v
    if v_first is None:
        v_first = v
    else:
        v0, v1, v2 = vres
        v = v + (v_first - v) * jax.nn.sigmoid(v0 + (xv @ v1) @ v2)
    r = xr @ w_r
    g = jax.nn.sigmoid(xg @ g1) @ g2

    heads = lambda t: t.reshape(B, -1, H, N).astype(jnp.float32)
    r_h, v_h, k_h = heads(r), heads(v), heads(k)
    kk = heads(k * k_k)
    kk = kk / jnp.maximum(jnp.sqrt(jnp.sum(kk * kk, axis=-1, keepdims=True)), 1e-12)
    k_a_h = k_a.reshape(H, N).astype(jnp.float32)
    r_k_f = r_k.astype(jnp.float32)
    s_zero = jnp.zeros((B, H, N, N), jnp.float32)
    rc = r_h[:, :Lc] if ctx_out else None
    rl = r_h[:, Lc - lo:]

    y = None
    bonus = None
    for d in range(N_DIR):
        w_log = -jax.nn.softplus(-(w0[d] + jnp.tanh(xw @ w1[d]) @ w2[d])) - 0.5
        decay = jnp.exp(-jnp.exp(heads(w_log)))
        a = heads(jax.nn.sigmoid(a0[d] + (xa @ a1[d]) @ a2[d]))
        k_d = k_h * (1 + (a - 1) * k_a_h)
        rev = d == 1
        yc, s_ctx = wkv_scan(decay[:, :Lc], k_d[:, :Lc], v_h[:, :Lc], kk[:, :Lc], a[:, :Lc], rc, s_zero, rev)
        yl, _ = wkv_scan(decay[:, Lc:], k_d[:, Lc:], v_h[:, Lc:], kk[:, Lc:], a[:, Lc:], rl, s_ctx, rev)
        y_d = jnp.concatenate([yc, yl], axis=1) if ctx_out else yl
        b_d = jnp.sum(r_h * k_d[:, lo:] * r_k_f, axis=-1, keepdims=True) * v_h[:, lo:]
        y = y_d if y is None else y + y_d
        bonus = b_d if bonus is None else bonus + b_d

    mean = jnp.mean(y, axis=-1, keepdims=True)
    var = jnp.mean(jnp.square(y - mean), axis=-1, keepdims=True)
    y = ((y - mean) * lax.rsqrt(var + GN_EPS)).reshape(B, -1, D) * lnx_g + lnx_b + bonus.reshape(B, -1, D)
    out = (y.astype(h.dtype) * g) @ w_o
    if ctx_out:
        return out[:, :Lc], out[:, Lc:], v_first
    return None, out, v_first

def chunk_sgu(h, w_in, b_in, ln_g, ln_b, w_s, b_s, w_out):
    B, L, _ = h.shape
    z = jax.nn.gelu(h @ w_in + b_in, approximate=False)
    u, v = jnp.split(z, 2, axis=-1)
    v = layer_norm(v, ln_g, ln_b)
    vc = v.reshape(B, L // CHUNK, CHUNK, SG_GROUPS, SG_HALF // SG_GROUPS)
    vs = jnp.einsum('gij,bcjgd->bcigd', w_s, vc) + b_s.T[:, :, None]
    return (u * vs.reshape(B, L, SG_HALF)) @ w_out

def moe_ffn(h, w_router, router_bias, w_gate, w_up, w_down):
    shp = h.shape
    t = h.reshape(-1, shp[-1])
    T = t.shape[0]
    scores = jax.nn.sigmoid((t @ w_router).astype(jnp.float32))
    biased = (scores + router_bias.astype(jnp.float32)).reshape(T, N_EXPERT_GROUPS, -1)
    group_score = jnp.sum(lax.top_k(biased, TOP_K)[0], axis=-1)
    best_group = jnp.argmax(group_score, axis=-1)
    in_group = jnp.arange(N_EXPERT_GROUPS)[None, :] == best_group[:, None]
    masked = jnp.where(in_group[:, :, None], biased, -jnp.inf).reshape(T, N_EXPERTS)
    _, idx = lax.top_k(masked, TOP_K)
    wts = jnp.take_along_axis(scores, idx, axis=-1)
    wts = wts / jnp.sum(wts, axis=-1, keepdims=True)
    gates = jnp.sum(jax.nn.one_hot(idx, N_EXPERTS, dtype=jnp.float32) * wts[..., None], axis=1).astype(t.dtype)
    out = jnp.zeros_like(t)
    for e in range(N_EXPERTS):
        he = jax.nn.silu(t @ w_gate[e]) * (t @ w_up[e])
        out = out + gates[:, e:e + 1] * (he @ w_down[e])
    return out.reshape(shp)

def setup_inputs(seed: int = 0) -> dict:
    key = jax.random.key(seed)
    ks = iter(jax.random.split(key, 64))
    D, E, F = D_MODEL, N_EXPERTS, EXPERT_FFN
    n_a = (DEPTH + N_MIXERS - 1) // N_MIXERS
    n_b = DEPTH // N_MIXERS
    n_v = max(n_a - 1, 0)

    def nrm(shape, scale):
        return jax.random.normal(next(ks), shape, jnp.float32) * scale

    def uni(shape, lo, hi):
        return jax.random.uniform(next(ks), shape, jnp.float32, lo, hi)

    return {
        "x": nrm((BATCH, SEQ, D), 1.0),
        "c": nrm((BATCH, D), 1.0),
        "ctx": nrm((BATCH, CTX_LEN, D), 1.0),
        "c_ctx": nrm((D,), 1.0),
        "w_mod": nrm((DEPTH, D, N_MOD * D), 0.5 * D ** -0.5),
        "b_mod": nrm((DEPTH, N_MOD * D), 0.02),
        "norm1_g": 1.0 + nrm((DEPTH, D), 0.05),
        "norm2_g": 1.0 + nrm((DEPTH, D), 0.05),
        "rw_mu": uni((n_a, 6, D), 0.2, 0.8),
        "rw_wr": nrm((n_a, D, D), D ** -0.5),
        "rw_wk": nrm((n_a, D, D), D ** -0.5),
        "rw_wv": nrm((n_a, D, D), D ** -0.5),
        "rw_wo": nrm((n_a, D, D), D ** -0.5),
        "rw_w0": uni((n_a, N_DIR, D), -6.0, 0.0),
        "rw_w1": nrm((n_a, N_DIR, D, DECAY_LORA), D ** -0.5),
        "rw_w2": nrm((n_a, N_DIR, DECAY_LORA, D), 0.1 * DECAY_LORA ** -0.5),
        "rw_a0": nrm((n_a, N_DIR, D), 0.5),
        "rw_a1": nrm((n_a, N_DIR, D, ICLR_LORA), D ** -0.5),
        "rw_a2": nrm((n_a, N_DIR, ICLR_LORA, D), 0.3 * ICLR_LORA ** -0.5),
        "rw_v0": nrm((n_v, D), 0.5),
        "rw_v1": nrm((n_v, D, VRES_LORA), D ** -0.5),
        "rw_v2": nrm((n_v, VRES_LORA, D), 0.3 * VRES_LORA ** -0.5),
        "rw_g1": nrm((n_a, D, GATE_LORA), D ** -0.5),
        "rw_g2": nrm((n_a, GATE_LORA, D), GATE_LORA ** -0.5),
        "rw_kk": 0.85 + nrm((n_a, D), 0.05),
        "rw_ka": 1.0 + nrm((n_a, D), 0.05),
        "rw_rk": nrm((n_a, N_HEADS, HEAD_SIZE), 0.1),
        "rw_lnx_g": 1.0 + nrm((n_a, D), 0.05),
        "rw_lnx_b": nrm((n_a, D), 0.01),
        "sg_w_in": nrm((n_b, D, SG_FFN), D ** -0.5),
        "sg_b_in": nrm((n_b, SG_FFN), 0.02),
        "sg_ln_g": 1.0 + nrm((n_b, SG_HALF), 0.05),
        "sg_ln_b": nrm((n_b, SG_HALF), 0.01),
        "sg_w_s": nrm((n_b, SG_GROUPS, CHUNK, CHUNK), CHUNK ** -0.5),
        "sg_b_s": 1.0 + nrm((n_b, SG_GROUPS, CHUNK), 0.1),
        "sg_w_out": nrm((n_b, SG_HALF, D), SG_HALF ** -0.5),
        "w_router": nrm((D, E), D ** -0.5),
        "router_bias": nrm((E,), 0.01),
        "ex_w_gate": nrm((DEPTH, E, D, F), D ** -0.5),
        "ex_w_up": nrm((DEPTH, E, D, F), D ** -0.5),
        "ex_w_down": nrm((DEPTH, E, F, D), F ** -0.5),
        "final_g": 1.0 + nrm((D,), 0.05),
    }

def reference(x, c, ctx, c_ctx, w_mod, b_mod, norm1_g, norm2_g, rw_mu, rw_wr, rw_wk, rw_wv, rw_wo,
              rw_w0, rw_w1, rw_w2, rw_a0, rw_a1, rw_a2, rw_v0, rw_v1, rw_v2, rw_g1, rw_g2, rw_kk, rw_ka,
              rw_rk, rw_lnx_g, rw_lnx_b, sg_w_in, sg_b_in, sg_ln_g, sg_ln_b, sg_w_s, sg_b_s, sg_w_out,
              w_router, router_bias, ex_w_gate, ex_w_up, ex_w_down, final_g):
    x_lat, x_ctx = x, ctx
    Lc = ctx.shape[1]
    v_first = None
    for i in range(DEPTH):
        mixer = i % N_MIXERS
        ctx_out = any(j % N_MIXERS == 0 for j in range(i + 1, DEPTH))
        ctx_live = ctx_out or mixer == 0
        sh1, sc1, gt1, sh2, sc2, gt2 = modulation(c, w_mod[i], b_mod[i])
        h_lat = ada_norm(x_lat, norm1_g[i], sh1, sc1)
        h_ctx = None
        if ctx_live:
            csh1, csc1, cgt1, csh2, csc2, cgt2 = modulation(c_ctx, w_mod[i], b_mod[i])
            h_ctx = ada_norm(x_ctx, norm1_g[i], csh1, csc1)

        if mixer == 0:
            a = i // N_MIXERS
            vres = (rw_v0[a - 1], rw_v1[a - 1], rw_v2[a - 1]) if a > 0 else None
            o_ctx, o_lat, v_first = rwkv7_bidir(
                h_ctx, h_lat, v_first, ctx_out, rw_mu[a], rw_wr[a], rw_wk[a], rw_wv[a], rw_wo[a],
                rw_w0[a], rw_w1[a], rw_w2[a], rw_a0[a], rw_a1[a], rw_a2[a], vres,
                rw_g1[a], rw_g2[a], rw_kk[a], rw_ka[a], rw_rk[a], rw_lnx_g[a], rw_lnx_b[a])
        else:
            b = i // N_MIXERS
            h_in = jnp.concatenate([h_ctx, h_lat], axis=1) if ctx_out else h_lat
            o_all = chunk_sgu(h_in, sg_w_in[b], sg_b_in[b], sg_ln_g[b], sg_ln_b[b], sg_w_s[b], sg_b_s[b],
                              sg_w_out[b])
            o_ctx, o_lat = (o_all[:, :Lc], o_all[:, Lc:]) if ctx_out else (None, o_all)

        x_lat = x_lat + gt1 * o_lat
        h_lat = ada_norm(x_lat, norm2_g[i], sh2, sc2)
        if ctx_out:
            x_ctx = x_ctx + cgt1 * o_ctx
            h_ctx = ada_norm(x_ctx, norm2_g[i], csh2, csc2)
            f = moe_ffn(jnp.concatenate([h_ctx, h_lat], axis=1), w_router, router_bias,
                        ex_w_gate[i], ex_w_up[i], ex_w_down[i])
            x_ctx = x_ctx + cgt2 * f[:, :Lc]
            x_lat = x_lat + gt2 * f[:, Lc:]
        else:
            x_lat = x_lat + gt2 * moe_ffn(h_lat, w_router, router_bias, ex_w_gate[i], ex_w_up[i], ex_w_down[i])
    return rms_norm(x_lat, final_g)


_drawn_inputs = setup_inputs


def setup_inputs(seed=0):
    import zlib

    import numpy as np

    out = dict(_drawn_inputs(seed))
    spreads = {}
    factors = {'rw_w1': 6.283, 'rw_w2': 5.637, 'rw_lnx_b': 3.145, 'sg_b_in': 4.595, 'sg_ln_b': 8.0}
    for name, (base, spread) in spreads.items():
        noise = np.random.default_rng([zlib.crc32(name.encode()), seed]).standard_normal(out[name].shape)
        drawn = base * np.exp(spread * noise) if base else spread * noise
        out[name] = __import__('jax').numpy.asarray(drawn.astype(out[name].dtype))
    for name, factor in factors.items():
        out[name] = (out[name] * factor).astype(out[name].dtype)
    return out
```

```python
import concourse.bass as bass
from concourse import mybir
from contextlib import ExitStack
from math import exp

F32 = mybir.dt.float32
ACT = mybir.ActivationFunctionType
ALU = mybir.AluOpType
AX = mybir.AxisListType

P = 128
D = 1024
KT = D // P
T = 256
NT = T // P
HEADS, HS = 16, 64
GRID_W = 64
EXPERTS, FFN = 16, 512
FT = FFN // P
HALF = 2048
VG = HALF // P
UNIT = 4096
RING = 6
DECAY = exp(-0.5)
LEVELS = [2, 4, 8, 16, 32, 64]


def bc(ap, dim, shape):
    return ap.unsqueeze(dim).broadcast_to(shape)


def build(nc, A, out):
    ctx = ExitStack()
    with ctx:
        def sem(name):
            return ctx.enter_context(nc.semaphore(name))

        ARENA = 52864
        arena = ctx.enter_context(nc.sbuf_tensor("arena", [P, ARENA], F32))
        psum = ctx.enter_context(nc.psum_tensor("psum", [P, 8 * 512], F32))

        def bank(i):
            return psum[:, 512 * i:512 * i + 512]

        class Place:

            def __init__(self, at):
                self.at = at

            def __call__(self, *dims):
                n = 1
                for x in dims:
                    n *= x
                ap = arena[:, self.at:self.at + n]
                self.at += n
                assert self.at <= ARENA, self.at
                if len(dims) == 2:
                    ap = ap.rearrange("p (a b) -> p a b", b=dims[1])
                elif len(dims) == 3:
                    ap = ap.rearrange("p (a b c) -> p a b c", b=dims[1], c=dims[2])
                return ap

        keep = Place(0)
        ident = keep(P)
        ones = keep(P)
        xT = keep(KT, T)
        cols = keep(3, P)
        modc = keep(2, 48, 2)
        silc = keep(KT, 2)
        gs = keep(5, KT)
        epsc = keep(4)
        tie = keep(16)
        wr = keep(KT, EXPERTS)
        rbias = keep(EXPERTS)
        route = keep(640)
        KEEP_END = keep.at

        c_cols, ctx_cols = cols[:, 0, 0:8], cols[:, 0, 8:16]
        n1_cols = [cols[:, 0, 16 + 8 * l:24 + 8 * l] for l in range(2)]
        n2_cols = [cols[:, 0, 32 + 8 * l:40 + 8 * l] for l in range(2)]
        w0_cols = [cols[:, 0, 48 + 8 * d:56 + 8 * d] for d in range(2)]
        a0_cols = [cols[:, 0, 64 + 8 * d:72 + 8 * d] for d in range(2)]
        kk_cols, ka_cols, rk_cols = cols[:, 0, 80:88], cols[:, 0, 88:96], cols[:, 0, 96:104]
        fin_cols, bu_cols = cols[:, 0, 104:112], cols[:, 0, 112:128]
        bm_cols = [cols[:, 1, 48 * l:48 * l + 48] for l in range(2)]
        mu_cols = [cols[:, 2, 8 * j:8 * j + 8] for j in range(6)]

        RING_AT = KEEP_END
        ring = [arena[:, RING_AT + UNIT * s:RING_AT + UNIT * (s + 1)] for s in range(RING)]

        rw = Place(KEEP_END)
        kT = rw(KT, 2 * T)
        kkT = rw(KT, 2 * T)
        hones = rw(P)
        merge_mask = rw(2 * 7, P)
        strict = rw(2, P)
        incl = rw(2, P)
        rT = rw(KT, T)
        V = rw(4, D)
        tanw = rw(2 * T)
        loa = rw(2 * T)
        sigg = rw(T)
        lora2 = rw(3, D)
        omka = rw(KT)
        rksel = rw(KT, 2)
        smid, send = rw(KT), rw(KT)
        lmid, lend = rw(KT), rw(KT)
        bonus = rw(NT, HEADS)
        Yacc = rw(NT, D)
        TEMP_AT = rw.at
        wo = [arena[:, KEEP_END + UNIT * s:KEEP_END + UNIT * (s + 1)] for s in range(2)]
        lora1 = arena[:, TEMP_AT - NT * D:TEMP_AT + 1024].rearrange("p (w k c) -> p w k c", w=3, c=P)

        pj = Place(TEMP_AT + 1024)
        hT = pj(KT, 2 * T)
        xx = pj(KT, 2 * T)
        xj = [pj(KT, 2 * T), pj(KT, 2 * T)]
        slots2 = [pj(UNIT), pj(UNIT)]
        xtok = arena[:, pj.at - 4 * UNIT:pj.at - 3 * UNIT].rearrange("p (t d) -> p t d", d=D)
        xcT = xx[:, 0:4, :].rearrange("p a b -> p (a b)").rearrange("p (k t) -> p k t", t=T)
        sq0 = xx[:, 4:8, :].rearrange("p a b -> p (a b)").rearrange("p (k t) -> p k t", t=T)
        prow = arena[:, pj.at - UNIT:pj.at - UNIT + 3 * P].rearrange("p (a b) -> p a b", b=P)
        rs0 = arena[:, pj.at - 3 * UNIT:pj.at - 3 * UNIT + T]
        ck = Place(TEMP_AT)
        AT, BT, KTl, RT = ck(KT, P), ck(KT, P), ck(KT, P), ck(KT, P)
        Btok, Ktok = ck(D), ck(D)
        buf1, buf2 = ck(HEADS, P), ck(HEADS, P)
        X, XT, T1 = ck(HEADS, P), ck(HEADS, P), ck(HEADS, P)
        sig, icl, D0, D1, E2 = ck(KT, P), ck(KT, P), ck(KT, P), ck(KT, P), ck(KT, P)
        W, U, S = ck(D), ck(D), ck(KT, P)
        yo = Place(TEMP_AT)
        lng, lnb = yo(D), yo(D)
        ysq, gT, ygT = yo(NT, D), yo(KT, T), yo(KT, T)
        ym, yv, yr = yo(NT * HEADS), yo(NT * HEADS), yo(NT * HEADS)

        mx = Place(RING_AT + RING * UNIT)
        h2T = mx(KT, T)
        sq = mx(KT, T)
        rs = mx(T)
        gbc = mx(EXPERTS, T)
        he = mx(2, FT, T)
        sg = mx(2, 2 * T)
        sgg = mx(2, 2 * T)
        uT = arena[:, mx.at - 8192:mx.at - 4096].rearrange("p (g t) -> p g t", t=T)
        vtok = arena[:, mx.at - 4096:mx.at].rearrange("p (t c) -> p t c", c=HALF)
        wsT = mx(VG, P)
        brow = mx(3, HALF)
        bsrow = mx(VG * P)
        stat = mx(2, 4, 6)
        mv = mx(2, 2)
        rstd = mx(2)
        tok_out = gbc.rearrange("p a b -> p (a b)").rearrange("p (t d) -> p t d", d=D * 2)[:, :, 0:D]

        cst = sem("constants_made")
        rows_in, x_in, small_in, lora1_in, lora2_in = map(sem, ("rows_in", "x_in", "small_in", "lora1_in", "lora2_in"))
        rows_T, cols_ready, sil_ready = sem("rows_transposed"), sem("cols_ready"), sem("silu_ready")
        x_T, xT_ready = sem("x_transposed"), sem("xT_ready")
        loaded = [sem(f"unit_loaded{s}") for s in range(RING)]
        mod_done, mod_ready = sem("mod_unit_done"), sem("mod_cols_ready")
        n_sq, n_ss, n_rt, n_h = sem("norm_squares"), sem("norm_sum"), sem("norm_root"), sem("norm_ready")
        dst, ast, pst = sem("dve_step"), sem("act_step"), sem("pool_step")
        xj_ready, pj_mm, pj_ev = sem("mix_ready"), sem("proj_done"), sem("proj_evacuated")
        pslot = [sem("proj_loaded0"), sem("proj_loaded1")]
        kk_sq, kk_ss, kk_mx, kk_rt, kk_ready = map(sem, ("kk_squares", "kk_sums", "kk_max", "kk_root", "kk_ready"))
        z_mm, z_sig, lmid_r, d1_r, d0_r, e_r = map(sem, ("z_done", "z_sigmoid", "mid_ready", "log_incl", "log_excl", "exps_ready"))
        til_r, prod_r, bon_mm, bon_ev = map(sem, ("tilde_ready", "bonus_prod", "bonus_done", "bonus_added"))
        bk_T, bk_tok = sem("tok_transposed"), sem("tok_ready")
        pr_mm, pr_ev = sem("pairs_done"), sem("pairs_masked")
        w1_mm, w1_ev = sem("w1_done"), sem("w1_ready")
        y1_mm, y1_ev = sem("y1_done"), sem("y1_added")
        xt2_r, tp_mm, tp_ev = sem("xt2_ready"), sem("x_transpose"), sem("xt_ready")
        t1_mm, t1_ev, x_mm, x_ev = map(sem, ("merge_nx", "merge_nx_masked", "merge_xnx", "merge_x_ready"))
        w_mm, w_ev, u_mm, u_ev, y_mm, y_ev, s_mm, s_ev, s_mid = map(sem, (
            "w_state_done", "w_ready", "u_done", "u_ready", "y_done", "y_added", "state_done", "state_next", "state_mid"))
        wo_in, ln_in = sem("wo_in"), sem("lnx_in")
        g_mm, g_ev, var_r, sd_r, y_r, y_T, yg_r, o_mm, x_r = map(sem, (
            "gate_done", "gate_ready", "var_ready", "sd_ready", "y_normed", "y_transposed", "yg_ready", "mixer_out_done", "x_mixed"))
        lg_mm, sc_r, gt_r, gt_T, gt_ev, gb_mm, gb_ev = map(sem, (
            "logits_done", "scores_ready", "gates_ready", "gates_transposed", "gates_T_ready", "gates_bc", "gates_bc_ready"))
        eg, eu, sg_r, sgg_r, he_r, dn, moe_x = map(sem, (
            "expert_gate", "expert_up", "silu_gate", "gated_silu", "expert_hidden", "expert_down", "x_after_moe"))
        gm_in = sem("gmlp_rows_in")
        u_pj, u_gl, v_pj, v_add, v_gl, v_ln0, v_sd, v_ln, ws_tr, ws_ev, sp_mm, sp_ev, go_mm = map(sem, (
            "u_proj", "u_gelu", "v_proj", "v_biased", "v_gelu", "v_var", "v_sd", "v_normed", "ws_transposed", "ws_ready",
            "spatial_done", "spatial_gated", "gmlp_out"))
        f_T, f_ev, stored = sem("out_transposed"), sem("out_ready"), sem("out_stored")

        CONSTS = [0]

        U_MOD0, U_EX0, U_MOD1 = 0, 12, 60
        U_WIN, U_WS, U_WOUT, U_EX1 = 72, 80, 81, 85
        U_EX = [U_EX0, U_EX1]

        def landed(eng, n):
            eng.wait_ge(loaded[n % RING], 16 * (n // RING + 1))

        STEPS = [(d, c) for d in range(2) for c in ((0, 1, 2, 3) if d == 0 else (1, 0, 3, 2))]

        def lat_before(n):
            return n // 4 * 2 + max(0, n % 4 - 2)

        def entered_before(n):
            return n - (n + 3) // 4

        def handed_before(n):
            return n // 4 * 3 + n % 4

        block = ctx.enter_context(nc.Block())

        @block.sync
        def _(sp):
            def unit(n, src):
                sp.dma_start(ring[n % RING].rearrange("p (k f) -> p k f", f=src.shape[-1]), src)\
                  .then_inc(loaded[n % RING], 16)

            sp.dma_start(xtok[:, 0:2, :], A["ctx"][0].rearrange("(t p) d -> p t d", p=P)).then_inc(x_in, 16)
            sp.dma_start(xtok[:, 2:4, :], A["x"][0].rearrange("(t p) d -> p t d", p=P)).then_inc(x_in, 16)
            for u in range(12):
                if u >= RING:
                    sp.wait_ge(mod_done, u - RING + 1)
                unit(U_MOD0 + u, A["w_mod"][0].rearrange("(k p) (u f) -> u p k f", p=P, f=512)[u])
            for n, (w, h) in enumerate([(w, h) for w in ("rw_wk", "rw_wv", "rw_wr") for h in range(2)]):
                if n == 0:
                    sp.wait_ge(x_T, 16)
                if n >= 2:
                    sp.wait_ge(pj_mm, 4 * (n - 1))
                sp.dma_start(slots2[n % 2].rearrange("p (k f) -> p k f", f=512),
                             A[w][0].rearrange("(k p) (h f) -> h p k f", p=P, f=512)[h]).then_inc(pslot[n % 2], 16)
                if n == 1:
                    sp.wait_ge(mod_done, 12)
                    for i, w in enumerate(("rw_w1", "rw_a1")):
                        for d in range(2):
                            sp.dma_start(lora1[:, i, :, 64 * d:64 * d + 64],
                                         A[w][0, d].rearrange("(k p) c -> p k c", p=P)).then_inc(lora1_in, 16)
                    sp.dma_start(lora1[:, 2, :, :], A["rw_g1"][0].rearrange("(k p) c -> p k c", p=P))\
                      .then_inc(lora1_in, 16)
                    for i, w in enumerate(("rw_w2", "rw_a2")):
                        for d in range(2):
                            sp.dma_start(lora2[64 * d:64 * d + 64, i, :], A[w][0, d]).then_inc(lora2_in, 16)
                    sp.dma_start(lora2[:, 2, :], A["rw_g2"][0]).then_inc(lora2_in, 16)
            sp.wait_ge(til_r, 8)
            for h in range(2):
                sp.dma_start(wo[h].rearrange("p (k f) -> p k f", f=512),
                             A["rw_wo"][0].rearrange("(k p) (h f) -> h p k f", p=P, f=512)[h]).then_inc(wo_in, 16)
            sp.wait_ge(y_ev, 4)
            sp.dma_start(lng, A["rw_lnx_g"][0].partition_broadcast(P)).then_inc(ln_in, 16)
            sp.dma_start(lnb, A["rw_lnx_b"][0].partition_broadcast(P)).then_inc(ln_in, 16)

            def experts(l):
                src = [A["ex_w_gate"][l].rearrange("e (k p) f -> e p k f", p=P),
                       A["ex_w_up"][l].rearrange("e (k p) f -> e p k f", p=P),
                       A["ex_w_down"][l].rearrange("e (k p) f -> e p k f", p=P)]
                for e in range(2):
                    for j in range(3):
                        n = U_EX[l] + 3 * e + j
                        if l == 1:
                            sp.wait_ge(*before[n - RING])
                        unit(n, src[j][e])
                with sp.Fori(1, EXPERTS // 2) as i:
                    for e in range(2):
                        for j in range(3):
                            n = U_EX[l] + 3 * e + j
                            s = n % RING
                            if j < 2:
                                sp.wait_ge((eg, eu)[j], i * 4 + (32 * l + 2 * (e - 2) + 2))
                            else:
                                sp.wait_ge(dn, i * 2 + (16 * l + e - 2 + 1))
                            dst = ring[s].rearrange("p (k f) -> p k f", f=src[j].shape[-1])
                            sp.dma_start(dst, src[j][i * 2 + e]).then_inc(loaded[s], 16)

            before = {}
            for e in (14, 15):
                for j in range(3):
                    before[U_EX0 + 3 * e + j] = ((eg, 32), (eu, 32), (dn, 16))[j] if e == 15 else \
                        ((eg, 30), (eu, 30), (dn, 15))[j]
            for u in range(12):
                before[U_MOD1 + u] = (mod_done, 12 + u + 1)
            for u in range(4):
                before[U_WIN + u] = (u_pj, 4 * (u + 1))
                before[U_WIN + 4 + u] = (v_pj, 2 * (u + 1))
                before[U_WOUT + u] = (go_mm, u + 1)
            before[U_WS] = (ws_tr, 4)

            sp.wait_ge(x_r, 1)
            experts(0)
            for u in range(12):
                sp.wait_ge(*before[U_MOD1 + u - RING])
                unit(U_MOD1 + u, A["w_mod"][1].rearrange("(k p) (u f) -> u p k f", p=P, f=512)[u])
            sp.dma_start(brow[:, 0, :], A["sg_b_in"][0, HALF:2 * HALF].partition_broadcast(P)).then_inc(gm_in, 16)
            sp.dma_start(brow[:, 1, :], A["sg_ln_g"][0].partition_broadcast(P)).then_inc(gm_in, 16)
            sp.dma_start(brow[:, 2, :], A["sg_ln_b"][0].partition_broadcast(P)).then_inc(gm_in, 16)
            sp.dma_start(bsrow[0:1, :], A["sg_b_s"][0].rearrange("(a g) i -> a (g i)", a=1)).then_inc(gm_in, 16)
            for u in range(8):
                sp.wait_ge(*before[U_WIN + u - RING])
                unit(U_WIN + u, A["sg_w_in"][0].rearrange("(k p) (u f) -> u p k f", p=P, f=512)[u])
            sp.wait_ge(*before[U_WS - RING])
            s = U_WS % RING
            sp.dma_start(ring[s][:, 0:VG * P].rearrange("p (g j) -> p g j", j=P),
                         A["sg_w_s"][0].rearrange("g i j -> i g j")).then_inc(loaded[s], 16)
            for u in range(4):
                sp.wait_ge(*before[U_WOUT + u - RING])
                unit(U_WOUT + u, A["sg_w_out"][0].rearrange("(u k p) f -> u p k f", p=P, k=4)[u])
            experts(1)
            sp.wait_ge(f_ev, 2)
            sp.dma_start(out[0].rearrange("(t p) d -> p t d", p=P), tok_out).then_inc(stored, 16)
            sp.wait_ge(stored, 16)

        @block.gpsimd
        def _(pool):
            at = 0
            for name, n in (("c", 8), ("c_ctx", 8), ("norm1_g", 16), ("norm2_g", 16), ("rw_w0", 16), ("rw_a0", 16),
                            ("rw_kk", 8), ("rw_ka", 8), ("rw_rk", 8), ("final_g", 8)):
                src = A[name]
                while len(src.shape) > 1:
                    src = src.rearrange("a b c -> (a b c)") if len(src.shape) == 3 else src.rearrange("a b -> (a b)")
                pool.dma_start(prow[at:at + n, 0, :], src.rearrange("(r p) -> r p", p=P)).then_inc(rows_in, 16)
                at += n
            pool.dma_start(prow[at:at + 16, 0, :], A["sg_b_in"][0, 0:HALF].rearrange("(r p) -> r p", p=P)).then_inc(rows_in, 16)
            pool.dma_start(prow[0:96, 1, :], A["b_mod"].rearrange("l (r p) -> (l r) p", p=P)).then_inc(rows_in, 16)
            pool.dma_start(prow[0:48, 2, :], A["rw_mu"][0].rearrange("j (r p) -> (j r) p", p=P)).then_inc(rows_in, 16)
            pool.dma_start(wr, A["w_router"].rearrange("(k p) e -> p k e", p=P)).then_inc(small_in, 16)
            pool.dma_start(rbias, A["router_bias"].partition_broadcast(P)).then_inc(small_in, 16)

            made = [0]

            def make(ins):
                made[0] += 1
                ins.then_inc(cst, 1)
                pool.wait_ge(cst, made[0])

            make(pool.memset(ident, 0.0))
            make(pool.memset(ones, 1.0))
            for i, v in enumerate((1e-6, 64e-5, 1e-5)):
                make(pool.memset(epsc[:, i:i + 1], v))
            make(pool.memset(tie, 0.0))
            make(pool.affine_select(out=ident, in_=ident, compare_op=ALU.not_equal, fill=1.0, base=0,
                                    pattern=[[-1, P]], channel_multiplier=1))
            for i in range(1, 4):
                make(pool.memset(tie[:, 4 * i:4 * i + i], 1.0))
            CONSTS[0] = made[0]

            pool.wait_ge(mod_done, 12)
            make(pool.memset(hones, 0.0))
            make(pool.memset(merge_mask, 0.0))
            make(pool.memset(strict, 1.0))
            make(pool.memset(incl, 1.0))
            make(pool.memset(rksel, 0.0))
            for h in range(2):
                make(pool.memset(hones[64 * h:64 * h + 64, 64 * h:64 * h + 64], 1.0))
            for d, (step, cm) in enumerate(((1, -1), (-1, 1))):
                make(pool.affine_select(out=strict[:, d, :], in_=strict[:, d, :], compare_op=ALU.is_gt, fill=0.0,
                                        base=0, pattern=[[step, P]], channel_multiplier=cm))
                make(pool.affine_select(out=incl[:, d, :], in_=incl[:, d, :], compare_op=ALU.is_ge, fill=0.0,
                                        base=0, pattern=[[step, P]], channel_multiplier=cm))
            views = []
            for d in range(2):
                for i, m in enumerate([1] + LEVELS):
                    v = merge_mask[:, 7 * d + i, :].rearrange("p (b c) -> p b c", c=2 * m)
                    v = v[:, :, 0:m] if d == 0 else v[:, :, m:2 * m]
                    make(pool.memset(v, 1.0))
                    views.append((d, m, v))
            for d, m, v in views:
                first = m if d == 0 else 0
                make(pool.affine_select(out=v, in_=v, compare_op=ALU.is_ge, fill=0.0, base=-first,
                                        pattern=[[-2 * m, P // (2 * m)], [0, m]], channel_multiplier=1))
            for d, m, v in views:
                first = m if d == 0 else 0
                make(pool.affine_select(out=v, in_=v, compare_op=ALU.is_ge, fill=0.0, base=first + m - 1,
                                        pattern=[[2 * m, P // (2 * m)], [0, m]], channel_multiplier=-1))
            CONSTS.append(made[0])

        @block.scalar
        def _(act):
            act.wait_ge(rows_T, 3)
            act.wait_ge(cst, CONSTS[0])
            for i in range(3):
                n = (P, 96, 48)[i]
                act.copy(cols[:, i, 0:n], bank(0)[:, P * i:P * i + n]).then_inc(cols_ready, 1)
            act.wait_ge(cols_ready, 3)
            act.activation(silc[:, :, 0], c_cols, ACT.Silu).then_inc(sil_ready, 1)
            act.activation(silc[:, :, 1], ctx_cols, ACT.Silu).then_inc(sil_ready, 1)
            for b in range(8):
                act.wait_ge(x_T, 4 * b + 4)
                dst = xcT if b < 4 else xT
                act.copy(dst[:, 2 * (b % 4):2 * (b % 4) + 2, :], bank(b).rearrange("p (a t) -> p a t", t=T)).then_inc(xT_ready, 1)

            def norm(q, src, sqb, rsb):
                act.activation(sqb, src, ACT.Square).then_inc(n_sq, 1)
                act.wait_ge(n_ss, q + 1)
                act.activation(rsb, bank(0)[:, 0:T], ACT.Sqrt, bias=epsc[:, 0:1], scale=1.0 / D).then_inc(n_rt, 1)

            act.wait_ge(xT_ready, 8)
            norm(0, xcT, sq0, rs0)
            act.wait_ge(n_h, 1)
            norm(1, xT, sq0, rs0)

            for q in range(27):
                act.wait_ge(pj_mm, q + 1)
                src = bank(q % 8)
                if q < 8:
                    ins = act.copy(kT[:, q, :], src)
                elif q < 16:
                    hf, t = (q - 8) // 4, (q - 8) % 4
                    ins = act.copy(V[:, t, 512 * hf:512 * hf + 512], src)
                elif q < 24:
                    ins = act.copy(rT[:, q - 16, :], src[:, 0:T])
                elif q == 24:
                    ins = act.activation(tanw, src, ACT.Tanh)
                elif q == 25:
                    ins = act.copy(loa, src)
                else:
                    ins = act.activation(sigg, src[:, 0:T], ACT.Sigmoid)
                ins.then_inc(pj_ev, 1)
            act.wait_ge(kk_mx, 8)
            act.activation(xj[1], xj[1], ACT.Sqrt).then_inc(kk_rt, 1)

            for n, (d, c) in enumerate(STEPS):
                lat, last = c >= 2, n % 4 == 3
                nl = lat_before(n)
                for m in range(8):
                    act.wait_ge(z_mm, 4 * n + m // 4 + 1)
                    if m == 0 and n > 0:
                        act.wait_ge(bk_tok, 4 * handed_before(n))
                        act.wait_ge(til_r, n)
                        if nl:
                            act.wait_ge(bon_mm, nl)
                    act.activation(sig[:, m, :], psum[:, P * m:P * m + P], ACT.Sigmoid, bias=w0_cols[d][:, m:m + 1]).then_inc(z_sig, 1)
                for m in range(8):
                    act.wait_ge(z_mm, 4 * n + 2 + m // 4 + 1)
                    act.activation(icl[:, m, :], psum[:, 1024 + P * m:1024 + P * m + P], ACT.Sigmoid, bias=a0_cols[d][:, m:m + 1]).then_inc(z_sig, 1)
                act.wait_ge(lmid_r, 2 * n + 2)
                act.activation(smid, lmid, ACT.Exp, scale=-DECAY).then_inc(e_r, 1)
                act.activation(send, lend, ACT.Exp, scale=-DECAY).then_inc(e_r, 1)
                act.wait_ge(d0_r, n + 1)
                act.activation(E2, D1, ACT.Exp, scale=DECAY).then_inc(e_r, 1)
                act.activation(D0, D0, ACT.Exp, scale=-DECAY).then_inc(e_r, 1)
                act.wait_ge(e_r, 5 * n + 3)
                act.activation(D1, D1, ACT.Exp, scale=-DECAY).then_inc(e_r, 1)
                if not last:
                    for j, dst in enumerate((Btok, Btok, Ktok, Ktok)):
                        act.wait_ge(bk_T, 4 * handed_before(n) + j + 1)
                        act.copy(dst[:, 512 * (j % 2):512 * (j % 2) + 512], bank(4 + j)).then_inc(bk_tok, 1)
                act.wait_ge(w1_mm, 2 * n + 2)
                act.copy(W, psum[:, 0:1024]).then_inc(w1_ev, 1)
                for i in range(6):
                    for g in range(4):
                        act.wait_ge(tp_mm, 24 * n + 4 * i + g + 1)
                        dst = X if i == 0 else XT
                        act.copy(dst[:, 4 * g:4 * g + 4, :], bank(2 * g).rearrange("p (a b) -> p a b", b=P)).then_inc(tp_ev, 1)
                act.wait_ge(u_mm, 2 * n + 2)
                act.copy(U, psum[:, 1024:2048]).then_inc(u_ev, 1)

            act.wait_ge(g_mm, 4)
            act.copy(gT, psum[:, 2048:4096].rearrange("p (k t) -> p k t", t=T)).then_inc(g_ev, 1)
            act.wait_ge(var_r, 1)
            act.activation(yr, yv, ACT.Sqrt).then_inc(sd_r, 1)

            def router(l):
                act.wait_ge(lg_mm, l + 1)
                act.activation(route[:, 0:32], bank(1)[:, 0:32], ACT.Sigmoid).then_inc(sc_r, 1)
                act.wait_ge(gt_T, l + 1)
                act.copy(route[0:16, 384:640], bank(2)[0:16, 0:T]).then_inc(gt_ev, 1)
                for b in range(8):
                    act.wait_ge(gb_mm, 8 * l + b + 1)
                    act.copy(gbc[:, 2 * b:2 * b + 2, :], bank(b).rearrange("p (a t) -> p a t", t=T)).then_inc(gb_ev, 1)

            def silu(l, q, hf):
                act.wait_ge(eg, q + 1)
                if not (isinstance(q, int) and q < 2):
                    act.wait_ge(sgg_r, q - 1)
                act.activation(sg[:, hf, :], bank(4 + 2 * hf), ACT.Silu).then_inc(sg_r, 1)

            def moe(l):
                for e in range(2):
                    for hf in range(2):
                        silu(l, 32 * l + 2 * e + hf, hf)
                with act.Fori(1, EXPERTS // 2) as i:
                    for e in range(2):
                        for hf in range(2):
                            silu(l, i * 4 + (32 * l + 2 * e + hf), hf)

            act.wait_ge(x_r, 1)
            norm(2, xT, sq, rs)
            router(0)
            moe(0)
            act.wait_ge(moe_x, 8)
            norm(3, xT, sq, rs)
            for m in range(16):
                act.wait_ge(u_pj, m // 2 * 2 + 2)
                act.activation(uT[:, m, :], bank(m // 2)[:, T * (m % 2):T * (m % 2) + T], ACT.Gelu,
                               bias=bu_cols[:, m:m + 1]).then_inc(u_gl, 1)
            for q in range(8):
                u, t = q // 2, q % 2
                act.wait_ge(v_add, q + 1)
                act.activation(vtok[:, t, 512 * u:512 * u + 512], vtok[:, t, 512 * u:512 * u + 512], ACT.Gelu).then_inc(v_gl, 1)
            for b in range(4):
                act.wait_ge(ws_tr, b + 1)
                act.copy(wsT[:, 4 * b:4 * b + 4, :], bank(b).rearrange("p (a j) -> p a j", j=P)).then_inc(ws_ev, 1)
            act.wait_ge(v_ln0, 2)
            act.activation(rstd, mv[:, :, 1], ACT.Sqrt, bias=epsc[:, 2:3]).then_inc(v_sd, 1)
            act.wait_ge(x_r, 2)
            norm(4, xT, sq, rs)
            router(1)
            moe(1)
            act.wait_ge(moe_x, 16)
            norm(5, xT, sq, rs)
            for t in range(2):
                act.wait_ge(f_T, 2 * t + 2)
                act.copy(tok_out[:, t, :], psum[:, 1024 + 1024 * t:2048 + 1024 * t]).then_inc(f_ev, 1)

        @block.vector
        def _(dve):
            steps = [0]

            def link(ins):
                steps[0] += 1
                ins.then_inc(dst, 1)
                dve.wait_ge(dst, steps[0])

            def send_step(ins):
                steps[0] += 1
                ins.then_inc(dst, 1)

            def mods(l):
                dve.wait_ge(mod_done, 12 * (l + 1))
                dve.wait_ge(cols_ready, 3)
                link(dve.tensor_tensor(modc[:, l, :, :], bank(7)[:, 0:96].rearrange("p (a b) -> p a b", b=2),
                                       bc(bm_cols[l], 2, [P, 48, 2]), ALU.add))
                m = modc[:, l, :, :]
                todo = [(0, m[:, 8:16, 1], n1_cols[0]), (1, m[:, 8:16, 0], n1_cols[0]), (2, m[:, 32:40, 0], n2_cols[0])] if l == 0 \
                    else [(3, m[:, 8:16, 0], n1_cols[1]), (4, m[:, 32:40, 0], n2_cols[1])]
                for i, sc, g in todo:
                    ins = dve.scalar_tensor_tensor(out=gs[:, i, :], in0=sc, scalar=1.0, in1=g, op0=ALU.add, op1=ALU.mult)
                    send_step(ins)
                dve.wait_ge(dst, steps[0])

            def norm(q, src, dest, scale, shift, rsb):
                dve.wait_ge(n_rt, q + 1)
                link(dve.reciprocal(rsb, rsb))
                link(dve.tensor_tensor(dest, src, bc(rsb, 1, [P, KT, T]), ALU.mult))
                for k in range(KT):
                    if shift is None:
                        ins = dve.tensor_scalar(dest[:, k, :], dest[:, k, :], scale[:, k:k + 1], None, ALU.mult)
                    else:
                        ins = dve.tensor_scalar(dest[:, k, :], dest[:, k, :], scale[:, k:k + 1], shift[:, k:k + 1], ALU.mult, ALU.add)
                    if k < KT - 1:
                        send_step(ins)
                dve.wait_ge(dst, steps[0])
                ins.then_inc(n_h, 1)

            mods(0)
            norm(0, xcT, hT[:, :, 0:T], gs[:, 0, :], modc[:, 0, 0:8, 1], rs0)
            norm(1, xT, hT[:, :, T:2 * T], gs[:, 1, :], modc[:, 0, 0:8, 0], rs0)
            dve.wait_ge(n_h, 2)

            H, Hh = hT, KT // 2
            for a, b, to, fr, edge in ((0, Hh, slice(1, T), slice(0, T - 1), slice(0, 1)),
                                       (Hh, KT, slice(0, T - 1), slice(1, T), slice(T - 1, T))):
                send_step(dve.tensor_tensor(xx[:, a:b, to], H[:, a:b, fr], H[:, a:b, to], ALU.subtract))
                send_step(dve.tensor_scalar(xx[:, a:b, edge], H[:, a:b, edge], -1.0, None, ALU.mult))
            for qd in range(4):
                for k in range(2 * qd, 2 * qd + 2):
                    hl, xl = H[:, k, T:2 * T], xx[:, k, T:2 * T]
                    if qd < 2:
                        g = lambda v: v.rearrange("p (r c) -> p r c", c=GRID_W)
                        to, fr = (slice(1, GRID_W), slice(0, GRID_W - 1))[::1 if qd == 0 else -1]
                        edge = slice(0, 1) if qd == 0 else slice(GRID_W - 1, GRID_W)
                        send_step(dve.tensor_tensor(g(xl)[:, :, to], g(hl)[:, :, fr], g(hl)[:, :, to], ALU.subtract))
                        send_step(dve.tensor_scalar(g(xl)[:, :, edge], g(hl)[:, :, edge], -1.0, None, ALU.mult))
                    else:
                        to, fr = (slice(GRID_W, T), slice(0, T - GRID_W))[::1 if qd == 2 else -1]
                        edge = slice(0, GRID_W) if qd == 2 else slice(T - GRID_W, T)
                        send_step(dve.tensor_tensor(xl[:, to], hl[:, fr], hl[:, to], ALU.subtract))
                        send_step(dve.tensor_scalar(xl[:, edge], hl[:, edge], -1.0, None, ALU.mult))
            dve.wait_ge(dst, steps[0])
            read_by = (8, 16, 24, 25, 26, 27)
            for i, j in enumerate((2, 3, 0, 1, 4, 5)):
                if i >= 2:
                    dve.wait_ge(pj_mm, read_by[i - 2])
                lo = T if j in (0, 5) else 0
                for k in range(KT):
                    dve.scalar_tensor_tensor(out=xj[i % 2][:, k, lo:2 * T], in0=xx[:, k, lo:2 * T],
                                             scalar=mu_cols[j][:, k:k + 1], in1=H[:, k, lo:2 * T],
                                             op0=ALU.mult, op1=ALU.add).then_inc(xj_ready, 1)

            dve.wait_ge(pj_ev, 27)
            dve.wait_ge(cst, CONSTS[1])
            for k in range(KT):
                send_step(dve.tensor_scalar(kkT[:, k, :], kT[:, k, :], kk_cols[:, k:k + 1], None, ALU.mult))
            dve.wait_ge(dst, steps[0])
            for k in range(KT):
                dve.tensor_tensor(xj[0][:, k, :], kkT[:, k, :], kkT[:, k, :], ALU.mult).then_inc(kk_sq, 1)
            for k in range(KT):
                dve.wait_ge(kk_ss, k + 1)
                dve.tensor_scalar(xj[1][:, k, :], bank(k), 1e-24, None, ALU.max).then_inc(kk_mx, 1)
            dve.wait_ge(kk_rt, 1)
            link(dve.reciprocal(xj[1], xj[1]))
            link(dve.tensor_tensor(kkT, kkT, xj[1], ALU.mult))
            link(dve.tensor_scalar(omka, ka_cols, -1.0, 1.0, ALU.mult, ALU.add))
            for h in range(2):
                send_step(dve.tensor_copy(rksel[64 * h:64 * h + 64, :, h], rk_cols[64 * h:64 * h + 64, :]))
            dve.memset(bonus, 0.0).then_inc(kk_ready, 1)
            dve.wait_ge(kk_ready, 1)

            for n, (d, c) in enumerate(STEPS):
                lat, last, first = c >= 2, n % 4 == 3, n % 4 == 0
                nl, ns = lat_before(n), handed_before(n)
                tok = slice(P * c, P * c + P)
                dve.wait_ge(z_sig, 16 * n + 16)
                rev = slice(None, None, -1) if d else slice(None)
                for m in range(KT):
                    send_step(dve.tensor_tensor_scan(D1[:, m, rev], ones[:, rev], sig[:, m, rev], 0.0, ALU.mult, ALU.add))
                dve.wait_ge(dst, steps[0])
                if n:
                    dve.wait_ge(s_mid, n)
                mid, end = P // 2, (P - 1 if d == 0 else 0)
                dve.tensor_copy(lmid, D1[:, :, mid]).then_inc(lmid_r, 1)
                dve.tensor_tensor(lend, D1[:, :, end], D1[:, :, mid], ALU.subtract).then_inc(lmid_r, 1)
                dve.wait_ge(lmid_r, 2 * n + 2)
                link(dve.tensor_tensor(D1, D1, bc(lmid, 2, [P, KT, P]), ALU.subtract))
                dve.tensor_tensor(D0, D1, sig, ALU.subtract).then_inc(d0_r, 1)
                send_step(dve.tensor_tensor(BT, kkT[:, :, tok], icl, ALU.mult))
                for m in range(KT):
                    send_step(dve.tensor_scalar(KTl[:, m, :], icl[:, m, :], ka_cols[:, m:m + 1], omka[:, m:m + 1], ALU.mult, ALU.add))
                dve.wait_ge(dst, steps[0])
                link(dve.tensor_tensor(KTl, KTl, kT[:, :, tok], ALU.mult))
                if lat:
                    dve.wait_ge(d0_r, n + 1)
                    dve.tensor_tensor(sig, KTl, rT[:, :, P * (c - 2):P * (c - 1)], ALU.mult).then_inc(prod_r, 1)
                dve.wait_ge(e_r, 5 * n + 5)
                send_step(dve.scalar_tensor_tensor(out=AT, in0=kkT[:, :, tok], scalar=-1.0, in1=D0, op0=ALU.mult, op1=ALU.mult))
                send_step(dve.tensor_tensor(BT, BT, E2, ALU.mult))
                if lat:
                    send_step(dve.tensor_tensor(RT, rT[:, :, P * (c - 2):P * (c - 1)], D1, ALU.mult))
                dve.wait_ge(dst, steps[0])
                if lat:
                    dve.wait_ge(prod_r, nl + 1)
                dve.tensor_tensor(KTl, KTl, E2, ALU.mult).then_inc(til_r, 1)
                dve.wait_ge(e_r, 5 * n + 5)
                if first:
                    dve.memset(S, 0.0).then_inc(s_mid, 1)
                else:
                    dve.tensor_tensor(S, S, bc(smid, 2, [P, KT, P]), ALU.mult).then_inc(s_mid, 1)
                if lat:
                    dve.wait_ge(bon_mm, nl + 1)
                    dve.tensor_tensor(bonus[:, c - 2, :], bonus[:, c - 2, :], bank(0)[:, 0:16], ALU.add).then_inc(bon_ev, 1)

                def masked(dest, b, mask, q):
                    dve.wait_ge(pr_mm, q)
                    dve.tensor_tensor(dest, bank(b).rearrange("p (a t) -> p a t", t=P), bc(mask, 1, [P, 4, P]), ALU.mult).then_inc(pr_ev, 1)

                base = 8 * n + 8 * nl
                for g in range(4):
                    masked(buf1[:, 4 * g:4 * g + 4, :], g, strict[:, d, :], base + g + 1)
                if lat:
                    for g in range(4):
                        masked(buf2[:, 4 * g:4 * g + 4, :], 4 + g, incl[:, d, :], base + 4 + g + 1)
                    dve.wait_ge(y1_mm, 2 * nl + 2)
                    if d == 0:
                        dve.tensor_copy(Yacc[:, c - 2, :], psum[:, 1024:2048]).then_inc(y1_ev, 1)
                    else:
                        dve.tensor_tensor(Yacc[:, c - 2, :], Yacc[:, c - 2, :], psum[:, 1024:2048], ALU.add).then_inc(y1_ev, 1)
                base += 8 if lat else 4
                for g in range(4):
                    masked(buf1[:, 4 * g:4 * g + 4, :], 4 + g, strict[:, d, :], base + g + 1)
                if lat:
                    for g in range(4):
                        masked(buf2[:, 4 * g:4 * g + 4, :], g, incl[:, d, :], base + 4 + g + 1)
                base_nt = base
                for g in range(4):
                    hd = slice(4 * g, 4 * g + 4)
                    dve.wait_ge(pr_ev, base_nt + g + 1)
                    link(dve.tensor_tensor(XT[:, hd, :], buf1[:, hd, :], bc(merge_mask[:, 7 * (1 - d), :], 1, [P, 4, P]), ALU.mult))
                    dve.tensor_tensor(XT[:, hd, :], XT[:, hd, :], bc(ident, 1, [P, 4, P]), ALU.add).then_inc(xt2_r, 1)
                for l in range(6):
                    for g in range(4):
                        hd = slice(4 * g, 4 * g + 4)
                        dve.wait_ge(t1_mm, 24 * n + 4 * l + g + 1)
                        dve.tensor_tensor(T1[:, hd, :], bank(2 * g).rearrange("p (a t) -> p a t", t=P),
                                          bc(merge_mask[:, 7 * d + 1 + l, :], 1, [P, 4, P]), ALU.mult).then_inc(t1_ev, 1)
                    for g in range(4):
                        hd = slice(4 * g, 4 * g + 4)
                        dve.wait_ge(x_mm, 24 * n + 4 * l + g + 1)
                        dest = (X if l < 5 else XT)[:, hd, :]
                        if l == 0 or l == 5:
                            dve.wait_ge(tp_ev, 24 * n + (4 * (0 if l == 0 else 5)) + g + 1)
                        dve.tensor_tensor(dest, dest, bank(2 * g + 1).rearrange("p (a t) -> p a t", t=P), ALU.add).then_inc(x_ev, 1)
                if not first:
                    dve.wait_ge(w_mm, 2 * entered_before(n) + 2)
                    dve.wait_ge(w1_ev, n + 1)
                    dve.tensor_tensor(W, W, psum[:, 0:1024], ALU.add).then_inc(w_ev, 1)
                if lat:
                    dve.wait_ge(y_mm, 2 * nl + 2)
                    dve.wait_ge(y1_ev, nl + 1)
                    dve.tensor_tensor(Yacc[:, c - 2, :], Yacc[:, c - 2, :], psum[:, 2048:3072], ALU.add).then_inc(y_ev, 1)
                if not last:
                    dve.wait_ge(s_mm, 2 * ns + 2)
                    dve.wait_ge(s_mid, n + 1)
                    link(dve.tensor_tensor(D1, psum[:, 3072:4096].rearrange("p (k t) -> p k t", t=P),
                                           bc(hones, 1, [P, KT, P]), ALU.mult))
                    link(dve.tensor_tensor(D1, D1, S, ALU.add))
                    dve.tensor_tensor(S, D1, bc(send, 2, [P, KT, P]), ALU.mult).then_inc(s_ev, 1)
                    dve.wait_ge(s_ev, ns + 1)

            dve.wait_ge(y_ev, 4)
            Yh = Yacc.rearrange("p t (h c) -> p (t h) c", c=HS)
            Yq = ysq.rearrange("p t (h c) -> p (t h) c", c=HS)
            NH = NT * HEADS
            dve.wait_ge(u_ev, 8)
            link(dve.tensor_reduce(ym, Yh, AX.X, ALU.add))
            link(dve.tensor_scalar(ym, ym, 1.0 / HS, None, ALU.mult))
            link(dve.tensor_tensor(Yh, Yh, bc(ym, 2, [P, NH, HS]), ALU.subtract))
            link(dve.tensor_tensor(Yq, Yh, Yh, ALU.mult))
            link(dve.tensor_reduce(yv, Yq, AX.X, ALU.add))
            dve.tensor_scalar(yv, yv, 1.0 / HS, 64e-5, ALU.mult, ALU.add).then_inc(var_r, 1)
            dve.wait_ge(sd_r, 1)
            link(dve.reciprocal(yr, yr))
            link(dve.tensor_tensor(Yh, Yh, bc(yr, 2, [P, NH, HS]), ALU.mult))
            dve.wait_ge(ln_in, 32)
            link(dve.tensor_tensor(Yacc, Yacc, bc(lng, 1, [P, NT, D]), ALU.mult))
            link(dve.tensor_tensor(Yacc, Yacc, bc(lnb, 1, [P, NT, D]), ALU.add))
            dve.wait_ge(bon_ev, 4)
            link(dve.tensor_tensor(Yq, V[:, 2:4, :].rearrange("p t (h c) -> p (t h) c", c=HS),
                                   bc(bonus.rearrange("p t h -> p (t h)"), 2, [P, NH, HS]), ALU.mult))
            dve.tensor_tensor(Yacc, Yacc, ysq, ALU.add).then_inc(y_r, 1)
            for b in range(4):
                dve.wait_ge(y_T, b + 1)
                dve.wait_ge(g_ev, 1)
                dve.tensor_tensor(ygT[:, 2 * b:2 * b + 2, :], bank(b).rearrange("p (a t) -> p a t", t=T),
                                  gT[:, 2 * b:2 * b + 2, :], ALU.mult).then_inc(yg_r, 1)

            def residual(src, gate, s, q0, done, fin):
                for m in range(KT):
                    dve.wait_ge(s, q0 + (m // 2 * 2 + 2 if done else 1))
                    ins = dve.scalar_tensor_tensor(out=xT[:, m, :], in0=src(m), scalar=gate[:, m:m + 1], in1=xT[:, m, :],
                                                   op0=ALU.mult, op1=ALU.add)
                    if fin is moe_x:
                        ins.then_inc(moe_x, 1)
                    elif m < KT - 1:
                        send_step(ins)
                    else:
                        dve.wait_ge(dst, steps[0])
                        ins.then_inc(fin, 1)

            halfbank = lambda b0: (lambda m: bank(b0 + m // 2)[:, T * (m % 2):T * (m % 2) + T])
            residual(halfbank(4), modc[:, 0, 16:24, 0], o_mm, 0, True, x_r)

            def router(l):
                dve.wait_ge(small_in, 32)
                dve.wait_ge(sc_r, l + 1)
                dve.wait_ge(cst, CONSTS[0])
                R = route
                sc3 = R[:, 0:32].rearrange("p (t e) -> p t e", e=16)
                b = R[:, 32:64]
                b3 = b.rearrange("p (t e) -> p t e", e=16)
                v = b.rearrange("p (g e) -> p g e", e=4)
                hi, lo = R[:, 64:80].rearrange("p (g e) -> p g e", e=2), R[:, 80:96].rearrange("p (g e) -> p g e", e=2)
                top, sec, gsc = R[:, 96:104], R[:, 104:112], R[:, 112:120]
                link(dve.tensor_tensor(b3, sc3, bc(rbias, 1, [P, 2, 16]), ALU.add))
                send_step(dve.tensor_tensor(hi, v[:, :, 0:2], v[:, :, 2:4], ALU.max))
                link(dve.tensor_tensor(lo, v[:, :, 0:2], v[:, :, 2:4], ALU.min))
                send_step(dve.tensor_tensor(top, hi[:, :, 0], hi[:, :, 1], ALU.max))
                send_step(dve.tensor_tensor(sec, hi[:, :, 0], hi[:, :, 1], ALU.min))
                link(dve.tensor_tensor(gsc, lo[:, :, 0], lo[:, :, 1], ALU.max))
                link(dve.tensor_tensor(sec, sec, gsc, ALU.max))
                link(dve.tensor_tensor(gsc, top, sec, ALU.add))

                def chosen(val, groups, few, dest):
                    n = groups
                    one = R[:, 128:128 + 16 * n].rearrange("p (g i j) -> p g i j", i=4, j=4)
                    two = R[:, 256:256 + 16 * n].rearrange("p (g i j) -> p g i j", i=4, j=4)
                    vj, vi = bc(val, 2, [P, n, 4, 4]), bc(val, 3, [P, n, 4, 4])
                    send_step(dve.tensor_tensor(one, vj, vi, ALU.is_gt))
                    link(dve.tensor_tensor(two, vj, vi, ALU.is_equal))
                    flat = two.rearrange("p g i j -> p g (i j)")
                    link(dve.tensor_tensor(flat, flat, bc(tie, 1, [P, n, 16]), ALU.mult))
                    link(dve.tensor_tensor(one, one, two, ALU.add))
                    link(dve.tensor_reduce(dest, one, AX.X, ALU.add))
                    link(dve.tensor_scalar(dest, dest, few - 0.5, None, ALU.is_lt))

                sel_e = R[:, 64:96].rearrange("p (g e) -> p g e", e=4)
                sel_g = R[:, 96:104].rearrange("p (t g) -> p t g", g=4)
                chosen(gsc.rearrange("p (t g) -> p t g", g=4), 2, 1, sel_g)
                chosen(v, 8, 2, sel_e)
                link(dve.tensor_tensor(sel_e, sel_e, bc(R[:, 96:104], 2, [P, 8, 4]), ALU.mult))
                wts = R[:, 64:96]
                link(dve.tensor_tensor(wts, wts, R[:, 0:32], ALU.mult))
                w3 = wts.rearrange("p (t e) -> p t e", e=16)
                link(dve.tensor_reduce(R[:, 104:106], w3, AX.X, ALU.add))
                link(dve.reciprocal(R[:, 106:108], R[:, 104:106]))
                dve.tensor_tensor(w3, w3, bc(R[:, 106:108], 2, [P, 2, 16]), ALU.mult).then_inc(gt_r, 1)

            def hidden(q, e, hf, par, dnw):
                dve.wait_ge(sg_r, q + 1)
                dve.tensor_tensor(sgg[:, hf, :].rearrange("p (a t) -> p a t", t=T),
                                  sg[:, hf, :].rearrange("p (a t) -> p a t", t=T),
                                  bc(gbc[:, e, :], 1, [P, 2, T]), ALU.mult).then_inc(sgg_r, 1)
                dve.wait_ge(sgg_r, q + 1)
                dve.wait_ge(eu, q + 1)
                if dnw is not None:
                    dve.wait_ge(dn, dnw)
                dve.tensor_tensor(he[:, par, 2 * hf:2 * hf + 2, :], sgg[:, hf, :].rearrange("p (a t) -> p a t", t=T),
                                  bank(5 + 2 * hf).rearrange("p (a t) -> p a t", t=T), ALU.mult).then_inc(he_r, 1)

            def moe(l):
                for e in range(2):
                    for hf in range(2):
                        hidden(32 * l + 2 * e + hf, e, hf, e, 16 * l + e - 1 if l else None)
                with dve.Fori(1, EXPERTS // 2) as i:
                    for e in range(2):
                        for hf in range(2):
                            hidden(i * 4 + (32 * l + 2 * e + hf), i * 2 + e, hf, e, i * 2 + (16 * l + e - 1))
                residual(halfbank(0), modc[:, l, 40:48, 0], dn, 16 * (l + 1) - 1, False, moe_x)

            dve.wait_ge(x_r, 1)
            norm(2, xT, h2T, gs[:, 2, :], modc[:, 0, 24:32, 0], rs)
            router(0)
            moe(0)
            mods(1)
            dve.wait_ge(moe_x, 8)
            norm(3, xT, h2T, gs[:, 3, :], modc[:, 1, 0:8, 0], rs)
            dve.wait_ge(gm_in, 64)
            for q in range(8):
                u, t = q // 2, q % 2
                dve.wait_ge(v_pj, q + 1)
                dve.tensor_tensor(vtok[:, t, 512 * u:512 * u + 512], bank(q), brow[:, 0, 512 * u:512 * u + 512], ALU.add).then_inc(v_add, 1)
            for t in range(2):
                for u in range(4):
                    dve.wait_ge(v_gl, 2 * u + t + 1)
                    send_step(dve.bn_stats(stat[:, t, u, :], vtok[:, t, 512 * u:512 * u + 512]))
                dve.wait_ge(dst, steps[0])
                dve.bn_aggr(mv[:, t, :], stat[:, t, :, :]).then_inc(v_ln0, 1)
            dve.wait_ge(v_sd, 1)
            dve.wait_ge(v_ln0, 2)
            link(dve.reciprocal(rstd, rstd))
            for t in range(2):
                link(dve.tensor_scalar(vtok[:, t, :], vtok[:, t, :], mv[:, t, 0:1], rstd[:, t:t + 1], ALU.subtract, ALU.mult))
                link(dve.tensor_tensor(vtok[:, t, :], vtok[:, t, :], brow[:, 1, :], ALU.mult))
                dve.tensor_tensor(vtok[:, t, :], vtok[:, t, :], brow[:, 2, :], ALU.add).then_inc(v_ln, 1)
            for g in range(VG):
                dve.wait_ge(sp_mm, g // 2 * 2 + 2)
                dve.wait_ge(u_gl, g + 1)
                dve.tensor_tensor(uT[:, g, :], uT[:, g, :], bank(4 + g // 2 % 4)[:, T * (g % 2):T * (g % 2) + T], ALU.mult).then_inc(sp_ev, 1)
            residual(halfbank(0), modc[:, 1, 16:24, 0], go_mm, 3, False, x_r)
            dve.wait_ge(x_r, 2)
            norm(4, xT, h2T, gs[:, 4, :], modc[:, 1, 24:32, 0], rs)
            router(1)
            moe(1)
            dve.wait_ge(moe_x, 16)
            norm(5, xT, h2T, fin_cols, None, rs)

        @block.tensor
        def _(pe):
            def product(dest, lhs, rhs, k):
                for i in range(k):
                    mm = pe.matmul(dest, lhs(i), rhs(i), start=(i == 0), stop=(i == k - 1))
                return mm

            pe.wait_ge(cst, CONSTS[0])
            pe.wait_ge(rows_in, 16 * 13)
            for i in range(3):
                n = (P, 96, 48)[i]
                pe.transpose(bank(0)[:, P * i:P * i + n], prow[0:n, i, :], ident[0:n, 0:n]).then_inc(rows_T, 1)
            pe.wait_ge(cols_ready, 3)
            pe.wait_ge(x_in, 32)
            for b in range(8):
                for a in range(2):
                    for t in range(2):
                        k = 2 * (b % 4) + a
                        pe.transpose(bank(b)[:, T * a + P * t:T * a + P * t + P],
                                     xtok[:, 2 * (b // 4) + t, P * k:P * k + P], ident).then_inc(x_T, 1)

            def modulation(l):
                for u in range(12):
                    landed(pe, (U_MOD0, U_MOD1)[l] + u)
                    w = ring[((U_MOD0, U_MOD1)[l] + u) % RING].rearrange("p (k f) -> p k f", f=512)
                    for m in range(4):
                        j = 4 * u + m
                        mm = product(bank(7)[:, 2 * j:2 * j + 2], lambda k: w[:, k, P * m:P * m + P], lambda k: silc[:, k, :], KT)
                    mm.then_inc(mod_done, 1)

            def norm(q, sqb):
                pe.wait_ge(n_sq, q + 1)
                product(bank(0)[:, 0:T], lambda k: ones, lambda k: sqb[:, k, :], KT).then_inc(n_ss, 1)

            pe.wait_ge(sil_ready, 2)
            pe.wait_ge(xT_ready, 8)
            modulation(0)
            norm(0, sq0)
            norm(1, sq0)
            pe.wait_ge(n_rt, 2)

            def slot(n):
                pe.wait_ge(pslot[n % 2], 16 * (n // 2 + 1))
                return slots2[n % 2].rearrange("p (k f) -> p k f", f=512)

            q = 0
            for m in range(8):
                if m % 4 == 0:
                    w = slot(m // 4)
                if m == 0:
                    pe.wait_ge(xj_ready, 8)
                product(bank(q % 8), lambda k: w[:, k, P * (m % 4):P * (m % 4) + P], lambda k: xj[0][:, k, :], KT).then_inc(pj_mm, 1)
                q += 1
            pe.wait_ge(xj_ready, 16)
            for hf in range(2):
                w = slot(2 + hf)
                for t in range(4):
                    pe.wait_ge(pj_ev, q - 7)
                    product(bank(q % 8), lambda k: xj[1][:, k, P * t:P * t + P], lambda k: w[:, k, :], KT).then_inc(pj_mm, 1)
                    q += 1
            pe.wait_ge(xj_ready, 24)
            for m in range(8):
                if m % 4 == 0:
                    w = slot(4 + m // 4)
                pe.wait_ge(pj_ev, q - 7)
                product(bank(q % 8)[:, 0:T], lambda k: w[:, k, P * (m % 4):P * (m % 4) + P], lambda k: xj[0][:, k, T:2 * T], KT).then_inc(pj_mm, 1)
                q += 1
            pe.wait_ge(lora1_in, 80)
            for i in range(3):
                pe.wait_ge(xj_ready, 32 + 8 * i)
                pe.wait_ge(pj_ev, q - 7)
                src = xj[(1, 0, 1)[i]]
                lo = T if i == 2 else 0
                product(bank(q % 8)[:, 0:2 * T - lo], lambda k: lora1[:, i, k, :], lambda k: src[:, k, lo:2 * T], KT).then_inc(pj_mm, 1)
                q += 1
            pe.wait_ge(pj_ev, q)
            for k in range(KT):
                pe.wait_ge(kk_sq, k + 1)
                pe.matmul(bank(k), hones, xj[0][:, k, :], start=True, stop=True).then_inc(kk_ss, 1)
            pe.wait_ge(kk_ready, 1)
            pe.wait_ge(lora2_in, 80)

            def place(h):
                return 8 * (h // 8) + 4 * (h % 2) + h % 8 // 2

            def rows_of(h):
                return slice(64 * (h % 2), 64 * (h % 2) + 64)

            for n, (d, c) in enumerate(STEPS):
                lat, last, first = c >= 2, n % 4 == 3, n % 4 == 0
                nl, ns = lat_before(n), handed_before(n)
                rows = slice(64 * d, 64 * d + 64)
                if n:
                    pe.wait_ge(u_ev, n)
                    if entered_before(n):
                        pe.wait_ge(w_ev, entered_before(n))
                for i, src in enumerate((tanw, loa)):
                    for m in range(8):
                        mm = pe.matmul(psum[:, 1024 * i + P * m:1024 * i + P * m + P], lora2[rows, i, P * m:P * m + P],
                                       src[rows, P * c:P * c + P], start=True, stop=True)
                        if m % 4 == 3:
                            mm.then_inc(z_mm, 1)
                if lat:
                    pe.wait_ge(prod_r, nl + 1)
                    pe.wait_ge(z_sig, 16 * n + 16)
                    for m in range(8):
                        mm = pe.matmul(bank(0)[:, 2 * m:2 * m + 2], sig[:, m, :], rksel[:, m, :], start=True, stop=True)
                    mm.then_inc(bon_mm, 1)
                pe.wait_ge(til_r, n + 1)
                pe.wait_ge(z_sig, 16 * n + 16)
                if nl:
                    pe.wait_ge(y_ev, nl)
                if ns:
                    pe.wait_ge(s_ev, ns)
                if not last:
                    for j, src in enumerate((BT, BT, KTl, KTl)):
                        for m in range(4):
                            mm = pe.transpose(bank(4 + j)[:, P * m:P * m + P], src[:, 4 * (j % 2) + m, :], ident)
                        mm.then_inc(bk_T, 1)

                def pairs(left, right, b0):
                    for g in range(4):
                        for a in range(4):
                            h = 8 * (g // 2) + 2 * a + g % 2
                            mm = pe.matmul(bank(b0 + g)[:, P * a:P * a + P], left[rows_of(h), h // 2, :],
                                           right[rows_of(h), h // 2, :], start=True, stop=True)
                        mm.then_inc(pr_mm, 1)

                base = 8 * n + 8 * nl
                if lat:
                    pe.wait_ge(bon_ev, nl + 1)
                pairs(KTl, AT, 0)
                if lat:
                    pe.wait_ge(bk_tok, 4 * (ns + (0 if last else 1)))
                    pairs(KTl, RT, 4)
                pe.wait_ge(pr_ev, base + 4)
                for h in range(HEADS):
                    mm = pe.matmul(psum[:, 64 * h:64 * h + 64], buf1[:, place(h), :], V[:, c, 64 * h:64 * h + 64], start=True, stop=True)
                    if h % 8 == 7:
                        mm.then_inc(w1_mm, 1)
                if lat:
                    pe.wait_ge(pr_ev, base + 8)
                    for h in range(HEADS):
                        mm = pe.matmul(psum[:, 1024 + 64 * h:1024 + 64 * h + 64], buf2[:, place(h), :], V[:, c, 64 * h:64 * h + 64], start=True, stop=True)
                        if h % 8 == 7:
                            mm.then_inc(y1_mm, 1)
                base += 8 if lat else 4
                if not last:
                    pe.wait_ge(bk_tok, 4 * (ns + 1))
                pairs(BT, AT, 4)
                pe.wait_ge(w1_ev, n + 1)
                if lat:
                    pe.wait_ge(y1_ev, nl + 1)
                    pairs(BT, RT, 0)
                    pe.wait_ge(pr_ev, base + 8)
                pe.wait_ge(pr_ev, base + 4)

                def turn(src, i, g):
                    for a in range(4):
                        mm = pe.transpose(bank(2 * g)[:, P * a:P * a + P], src[:, 4 * g + a, :], ident)
                    mm.then_inc(tp_mm, 1)

                for g in range(4):
                    pe.wait_ge(xt2_r, 4 * n + g + 1)
                    turn(XT, 0, g)
                for l in range(6):
                    for g in range(4):
                        pe.wait_ge(tp_ev, 24 * n + 4 * l + g + 1)
                        for a in range(4):
                            h = 4 * g + a
                            mm = pe.matmul(bank(2 * g)[:, P * a:P * a + P], buf1[:, h, :], X[:, h, :], start=True, stop=True)
                        mm.then_inc(t1_mm, 1)
                    for g in range(4):
                        pe.wait_ge(t1_ev, 24 * n + 4 * l + g + 1)
                        for a in range(4):
                            h = 4 * g + a
                            if l < 5:
                                mm = pe.matmul(bank(2 * g + 1)[:, P * a:P * a + P], XT[:, h, :], T1[:, h, :], start=True, stop=True)
                            else:
                                mm = pe.matmul(bank(2 * g + 1)[:, P * a:P * a + P], T1[:, h, :], XT[:, h, :], start=True, stop=True)
                        mm.then_inc(x_mm, 1)
                    if l < 5:
                        for g in range(4):
                            pe.wait_ge(x_ev, 24 * n + 4 * l + g + 1)
                            turn(X, l + 1, g)
                pe.wait_ge(x_ev, 24 * n + 24)
                pe.wait_ge(s_mid, n + 1)
                if not first:
                    for m in range(8):
                        mm = pe.matmul(psum[:, P * m:P * m + P], AT[:, m, :], S[:, m, :], start=True, stop=True)
                        if m % 4 == 3:
                            mm.then_inc(w_mm, 1)
                    pe.wait_ge(w_ev, entered_before(n) + 1)
                for h in range(HEADS):
                    mm = pe.matmul(psum[:, 1024 + 64 * h:1024 + 64 * h + 64], XT[:, place(h), :], W[:, 64 * h:64 * h + 64], start=True, stop=True)
                    if h % 8 == 7:
                        mm.then_inc(u_mm, 1)
                pe.wait_ge(u_ev, n + 1)
                if lat:
                    for m in range(8):
                        pe.matmul(psum[:, 2048 + P * m:2048 + P * m + P], RT[:, m, :], S[:, m, :], start=True, stop=False,
                                  skip_group_check=True)
                        for h in (2 * m, 2 * m + 1):
                            mm = pe.matmul(psum[:, 2048 + 64 * h:2048 + 64 * h + 64], buf2[:, place(h), :], U[:, 64 * h:64 * h + 64],
                                           start=False, stop=True, skip_group_check=True)
                        if m % 4 == 3:
                            mm.then_inc(y_mm, 1)
                if not last:
                    for m in range(8):
                        ch = slice(P * m, P * m + P)
                        pe.matmul(psum[:, 3072 + P * m:3072 + P * m + P], Btok[:, ch], U[:, ch], start=True, stop=False)
                        mm = pe.matmul(psum[:, 3072 + P * m:3072 + P * m + P], Ktok[:, ch], V[:, c, ch], start=False, stop=True)
                        if m % 4 == 3:
                            mm.then_inc(s_mm, 1)

            pe.wait_ge(y_ev, 4)
            pe.wait_ge(s_ev, 6)
            for m in range(8):
                mm = pe.matmul(psum[:, 2048 + T * m:2048 + T * m + T], lora2[:, 2, P * m:P * m + P], sigg, start=True, stop=True)
                if m % 2 == 1:
                    mm.then_inc(g_mm, 1)
            pe.wait_ge(y_r, 1)
            pe.wait_ge(u_ev, 8)
            for b in range(4):
                for a in range(2):
                    for t in range(2):
                        k = 2 * b + a
                        mm = pe.transpose(bank(b)[:, T * a + P * t:T * a + P * t + P], Yacc[:, t, P * k:P * k + P], ident)
                mm.then_inc(y_T, 1)
            pe.wait_ge(wo_in, 32)
            pe.wait_ge(yg_r, 4)
            for m in range(8):
                w = wo[m // 4].rearrange("p (k f) -> p k f", f=512)
                product(bank(4 + m // 2)[:, T * (m % 2):T * (m % 2) + T], lambda k: w[:, k, P * (m % 4):P * (m % 4) + P],
                        lambda k: ygT[:, k, :], KT).then_inc(o_mm, 1)

            def router(l, q):
                pe.wait_ge(n_h, q + 1)
                pe.wait_ge(small_in, 32)
                for t in range(2):
                    mm = product(bank(1)[:, 16 * t:16 * t + 16], lambda k: h2T[:, k, P * t:P * t + P], lambda k: wr[:, k, :], KT)
                mm.then_inc(lg_mm, 1)
                pe.wait_ge(gt_r, l + 1)
                for t in range(2):
                    mm = pe.transpose(bank(2)[0:16, P * t:P * t + P], route[:, 64 + 16 * t:80 + 16 * t], ident)
                mm.then_inc(gt_T, 1)
                pe.wait_ge(gt_ev, l + 1)
                for e in range(EXPERTS):
                    mm = pe.matmul(bank(e // 2)[:, T * (e % 2):T * (e % 2) + T], ident[0:16, e:e + 1].broadcast_to([16, P]),
                                   route[0:16, 384:640], start=True, stop=True)
                    if e % 2 == 1:
                        mm.then_inc(gb_mm, 1)

            def hidden(l, e, hf, i, q):
                for j, s in enumerate((eg, eu)):
                    n = U_EX[l] + 3 * e + j
                    if hf == 0:
                        pe.wait_ge(loaded[n % RING], (16 * (n // RING + 1) if i is None else i * 16 + 16 * (n // RING + 1)))
                    if not (l == 0 and i is None and e == 0):
                        pe.wait_ge((sg_r, he_r)[j], q - 1)
                    w = ring[n % RING].rearrange("p (k f) -> p k f", f=FFN)
                    for f in (2 * hf, 2 * hf + 1):
                        mm = product(bank(4 + 2 * hf + j)[:, T * (f % 2):T * (f % 2) + T], lambda k: w[:, k, P * f:P * f + P],
                                     lambda k: h2T[:, k, :], KT)
                    mm.then_inc(s, 1)

            def down(l, e, i, q, opening=False):
                n = U_EX[l] + 3 * e + 2
                pe.wait_ge(loaded[n % RING], (16 * (n // RING + 1) if i is None else i * 16 + 16 * (n // RING + 1)))
                pe.wait_ge(he_r, q)
                w = ring[n % RING].rearrange("p (k f) -> p k f", f=D)
                for m in range(KT):
                    for k in range(FT):
                        mm = pe.matmul(bank(m // 2)[:, T * (m % 2):T * (m % 2) + T], w[:, k, P * m:P * m + P],
                                       he[:, e, k, :], start=(opening and k == 0 and m % 2 == 0), stop=False,
                                       skip_group_check=True)
                mm.then_inc(dn, 1)

            def moe(l):
                pe.wait_ge(gb_ev, 8 * (l + 1))
                hidden(l, 0, 0, None, 32 * l)
                hidden(l, 0, 1, None, 32 * l + 1)
                hidden(l, 1, 0, None, 32 * l + 2)
                down(l, 0, None, 32 * l + 2, opening=True)
                hidden(l, 1, 1, None, 32 * l + 3)
                with pe.Fori(1, EXPERTS // 2) as i:
                    hidden(l, 0, 0, i, i * 4 + 32 * l)
                    down(l, 1, i - 1, i * 4 + 32 * l)
                    hidden(l, 0, 1, i, i * 4 + (32 * l + 1))
                    hidden(l, 1, 0, i, i * 4 + (32 * l + 2))
                    down(l, 0, i, i * 4 + (32 * l + 2))
                    hidden(l, 1, 1, i, i * 4 + (32 * l + 3))
                down(l, 1, EXPERTS // 2 - 1, 32 * (l + 1))

            norm(2, sq)
            router(0, 2)
            moe(0)
            pe.wait_ge(he_r, 32)
            modulation(1)
            norm(3, sq)
            pe.wait_ge(n_h, 4)
            pe.wait_ge(n_rt, 4)
            pe.wait_ge(moe_x, 8)
            for m in range(16):
                n = U_WIN + m // 4
                landed(pe, n)
                w = ring[n % RING].rearrange("p (k f) -> p k f", f=512)
                product(bank(m // 2)[:, T * (m % 2):T * (m % 2) + T], lambda k: w[:, k, P * (m % 4):P * (m % 4) + P],
                        lambda k: h2T[:, k, :], KT).then_inc(u_pj, 1)
            for q in range(8):
                u, t = q // 2, q % 2
                n = U_WIN + 4 + u
                landed(pe, n)
                pe.wait_ge(u_gl, 2 * q + 2)
                w = ring[n % RING].rearrange("p (k f) -> p k f", f=512)
                product(bank(q), lambda k: h2T[:, k, P * t:P * t + P], lambda k: w[:, k, :], KT).then_inc(v_pj, 1)
            landed(pe, U_WS)
            wsr = ring[U_WS % RING][:, 0:VG * P].rearrange("p (g j) -> p g j", j=P)
            for b in range(4):
                pe.wait_ge(v_add, b + 1)
                for a in range(4):
                    mm = pe.transpose(bank(b)[:, P * a:P * a + P], wsr[:, 4 * b + a, :], ident)
                mm.then_inc(ws_tr, 1)
            pe.wait_ge(ws_ev, 4)
            pe.wait_ge(v_ln, 2)
            pe.wait_ge(v_add, 8)
            for g in range(VG):
                if g >= 8:
                    pe.wait_ge(sp_ev, g // 2 * 2 - 6)
                for t in range(2):
                    dest = bank(4 + g // 2 % 4)[:, T * (g % 2) + P * t:T * (g % 2) + P * t + P]
                    pe.matmul(dest, vtok[:, t, P * g:P * g + P], wsT[:, g, :], start=True, stop=False)
                    mm = pe.matmul(dest, ones[0:1, :], bsrow[0:1, P * g:P * g + P], start=False, stop=True)
                mm.then_inc(sp_mm, 1)
            for u in range(4):
                n = U_WOUT + u
                landed(pe, n)
                pe.wait_ge(sp_ev, 4 * u + 4)
                w = ring[n % RING].rearrange("p (k f) -> p k f", f=D)
                for m in range(KT):
                    for k in range(4):
                        mm = pe.matmul(bank(m // 2)[:, T * (m % 2):T * (m % 2) + T], w[:, k, P * m:P * m + P],
                                       uT[:, 4 * u + k, :], start=(u == 0 and k == 0 and m % 2 == 0), stop=False,
                                       skip_group_check=True)
                mm.then_inc(go_mm, 1)
            pe.wait_ge(x_r, 2)
            norm(4, sq)
            router(1, 4)
            moe(1)
            pe.wait_ge(moe_x, 16)
            norm(5, sq)
            pe.wait_ge(n_h, 6)
            for t in range(2):
                for j in range(2):
                    for a in range(4):
                        k = 4 * j + a
                        mm = pe.transpose(psum[:, 1024 + 1024 * t + P * k:1024 + 1024 * t + P * k + P],
                                          h2T[:, k, P * t:P * t + P], ident)
                    mm.then_inc(f_T, 1)


_INS = ["x", "c", "ctx", "c_ctx", "w_mod", "b_mod", "norm1_g", "norm2_g", "rw_mu", "rw_wr", "rw_wk", "rw_wv", "rw_wo",
        "rw_w0", "rw_w1", "rw_w2", "rw_a0", "rw_a1", "rw_a2", "rw_g1", "rw_g2", "rw_kk", "rw_ka", "rw_rk", "rw_lnx_g",
        "rw_lnx_b", "sg_w_in", "sg_b_in", "sg_ln_g", "sg_ln_b", "sg_w_s", "sg_b_s", "sg_w_out", "w_router",
        "router_bias", "ex_w_gate", "ex_w_up", "ex_w_down", "final_g"]


def kernel(**inputs):
    import numpy as np
    import concourse.bacc as bacc
    from concourse.bass_utils import run_bass_kernel_spmd as run

    nc = bacc.Bacc("TRN2", target_bir_lowering=False, num_devices=1)
    arrays, aps = {}, {}
    for name in _INS:
        a = np.ascontiguousarray(inputs[name])
        arrays[f"in_{name}"] = a
        aps[name] = nc.dram_tensor(f"in_{name}", a.shape, mybir.dt.from_np(a.dtype), kind="ExternalInput").ap()
    out = nc.dram_tensor("out_0", (1, T, D), F32, kind="ExternalOutput").ap()
    build(nc, aps, out)
    return run(nc, [arrays], core_ids=[0]).results[0]["out_0"]
```

```python
import concourse.bass as bass
from concourse import mybir
from contextlib import ExitStack
from math import exp

F32 = mybir.dt.float32
ACT = mybir.ActivationFunctionType
ALU = mybir.AluOpType
AX = mybir.AxisListType

P = 128
D = 1024
KT = D // P
T = 256
NT = T // P
HEADS, HS = 16, 64
GRID_W = 64
EXPERTS, FFN = 16, 512
FT = FFN // P
HALF = 2048
VG = HALF // P
SLOTS = 64
PAIRS = EXPERTS // 2
MORE = 4
UNIT = 4096
RING = 6
DECAY = exp(-0.5)
LEVELS = [2, 4, 8, 16, 32, 64]


def bc(ap, dim, shape):
    return ap.unsqueeze(dim).broadcast_to(shape)


def build(nc, A, out):
    ctx = ExitStack()
    with ctx:
        def sem(name):
            return ctx.enter_context(nc.semaphore(name))

        ARENA = 53184
        arena = ctx.enter_context(nc.sbuf_tensor("arena", [P, ARENA], F32))
        psum = ctx.enter_context(nc.psum_tensor("psum", [P, 8 * 512], F32))

        def bank(i):
            return psum[:, 512 * i:512 * i + 512]

        class Place:

            def __init__(self, at):
                self.at = at

            def __call__(self, *dims):
                n = 1
                for x in dims:
                    n *= x
                ap = arena[:, self.at:self.at + n]
                self.at += n
                assert self.at <= ARENA, self.at
                if len(dims) == 2:
                    ap = ap.rearrange("p (a b) -> p a b", b=dims[1])
                elif len(dims) == 3:
                    ap = ap.rearrange("p (a b c) -> p a b c", b=dims[1], c=dims[2])
                return ap

        keep = Place(0)
        ident = keep(P)
        ones = keep(P)
        xT = keep(KT, T)
        cols = keep(3, P)
        modc = keep(2, 48, 2)
        silc = keep(KT, 2)
        gs = keep(5, KT)
        epsc = keep(4)
        tie = keep(16)
        before = keep(P)
        iota = keep(P)
        wr = keep(KT, EXPERTS)
        rbias = keep(EXPERTS)
        route = keep(512)
        plan = keep(2, 9).bitcast(mybir.dt.int32)
        KEEP_END = keep.at

        c_cols, ctx_cols = cols[:, 0, 0:8], cols[:, 0, 8:16]
        n1_cols = [cols[:, 0, 16 + 8 * l:24 + 8 * l] for l in range(2)]
        n2_cols = [cols[:, 0, 32 + 8 * l:40 + 8 * l] for l in range(2)]
        w0_cols = [cols[:, 0, 48 + 8 * d:56 + 8 * d] for d in range(2)]
        a0_cols = [cols[:, 0, 64 + 8 * d:72 + 8 * d] for d in range(2)]
        kk_cols, ka_cols, rk_cols = cols[:, 0, 80:88], cols[:, 0, 88:96], cols[:, 0, 96:104]
        fin_cols, bu_cols = cols[:, 0, 104:112], cols[:, 0, 112:128]
        bm_cols = [cols[:, 1, 48 * l:48 * l + 48] for l in range(2)]
        mu_cols = [cols[:, 2, 8 * j:8 * j + 8] for j in range(6)]

        RING_AT = KEEP_END
        ring = [arena[:, RING_AT + UNIT * s:RING_AT + UNIT * (s + 1)] for s in range(RING)]

        rw = Place(KEEP_END)
        kT = rw(KT, 2 * T)
        kkT = rw(KT, 2 * T)
        hones = rw(P)
        merge_mask = rw(2 * 7, P)
        strict = rw(2, P)
        incl = rw(2, P)
        rT = rw(KT, T)
        V = rw(4, D)
        tanw = rw(2 * T)
        loa = rw(2 * T)
        sigg = rw(T)
        lora2 = rw(3, D)
        omka = rw(KT)
        rksel = rw(KT, 2)
        smid, send = rw(KT), rw(KT)
        lmid, lend = rw(KT), rw(KT)
        bonus = rw(NT, HEADS)
        Yacc = rw(NT, D)
        TEMP_AT = rw.at
        wo = [arena[:, KEEP_END + UNIT * s:KEEP_END + UNIT * (s + 1)] for s in range(2)]
        lora1 = arena[:, TEMP_AT - NT * D:TEMP_AT + 1024].rearrange("p (w k c) -> p w k c", w=3, c=P)

        pj = Place(TEMP_AT + 1024)
        hT = pj(KT, 2 * T)
        xx = pj(KT, 2 * T)
        xj = [pj(KT, 2 * T), pj(KT, 2 * T)]
        slots2 = [pj(UNIT), pj(UNIT)]
        xtok = arena[:, pj.at - 4 * UNIT:pj.at - 3 * UNIT].rearrange("p (t d) -> p t d", d=D)
        xcT = xx[:, 0:4, :].rearrange("p a b -> p (a b)").rearrange("p (k t) -> p k t", t=T)
        sq0 = xx[:, 4:8, :].rearrange("p a b -> p (a b)").rearrange("p (k t) -> p k t", t=T)
        prow = arena[:, pj.at - UNIT:pj.at - UNIT + 3 * P].rearrange("p (a b) -> p a b", b=P)
        rs0 = arena[:, pj.at - 3 * UNIT:pj.at - 3 * UNIT + T]
        ck = Place(TEMP_AT)
        AT, BT, KTl, RT = ck(KT, P), ck(KT, P), ck(KT, P), ck(KT, P)
        Btok, Ktok = ck(D), ck(D)
        buf1, buf2 = ck(HEADS, P), ck(HEADS, P)
        X, XT, T1 = ck(HEADS, P), ck(HEADS, P), ck(HEADS, P)
        sig, icl, D0, D1, E2 = ck(KT, P), ck(KT, P), ck(KT, P), ck(KT, P), ck(KT, P)
        W, U, S = ck(D), ck(D), ck(KT, P)
        yo = Place(TEMP_AT)
        lng, lnb = yo(D), yo(D)
        ysq, gT, ygT = yo(NT, D), yo(KT, T), yo(KT, T)
        ym, yv, yr = yo(NT * HEADS), yo(NT * HEADS), yo(NT * HEADS)

        mx = Place(RING_AT + RING * UNIT)
        h2T = mx(KT, T)
        sq = mx(KT, T)
        rs = mx(T)
        gm = Place(mx.at)
        h2tok = mx(NT, D)
        pick = mx(NT, EXPERTS * SLOTS)
        gpick = sq.rearrange("p a b -> p (a b)").rearrange("p (t c) -> p t c", t=NT)
        giveT = mx(PAIRS, T)
        xs = mx(KT, P)
        sg = mx(FFN)
        he = mx(FFN)
        heT = mx(FT, P)
        ye = mx(D)
        uT = gm(VG, T)
        vtok = gm(NT, HALF)
        wsT = mx(VG, P)
        brow = mx(3, HALF)
        bsrow = mx(VG * P)
        stat = mx(2, 4, 6)
        mv = mx(2, 2)
        rstd = mx(2)
        tok_out = h2tok

        cst = sem("constants_made")
        rows_in, x_in, small_in, lora1_in, lora2_in = map(sem, ("rows_in", "x_in", "small_in", "lora1_in", "lora2_in"))
        rows_T, cols_ready, sil_ready = sem("rows_transposed"), sem("cols_ready"), sem("silu_ready")
        x_T, xT_ready = sem("x_transposed"), sem("xT_ready")
        loaded = [sem(f"unit_loaded{s}") for s in range(RING)]
        mod_done = sem("mod_unit_done")
        n_sq, n_ss, n_rt, n_h = sem("norm_squares"), sem("norm_sum"), sem("norm_root"), sem("norm_ready")
        dst = sem("dve_step")
        xj_ready, pj_mm, pj_ev = sem("mix_ready"), sem("proj_done"), sem("proj_evacuated")
        pslot = [sem("proj_loaded0"), sem("proj_loaded1")]
        kk_sq, kk_ss, kk_mx, kk_rt, kk_ready = map(sem, ("kk_squares", "kk_sums", "kk_max", "kk_root", "kk_ready"))
        z_mm, z_sig, lmid_r, d0_r, e_r = map(sem, ("z_done", "z_sigmoid", "mid_ready", "log_excl", "exps_ready"))
        til_r, prod_r, bon_mm, bon_ev = map(sem, ("tilde_ready", "bonus_prod", "bonus_done", "bonus_added"))
        bk_T, bk_tok = sem("tok_transposed"), sem("tok_ready")
        pr_mm, pr_ev = sem("pairs_done"), sem("pairs_masked")
        w1_mm, w1_ev = sem("w1_done"), sem("w1_ready")
        y1_mm, y1_ev = sem("y1_done"), sem("y1_added")
        xt2_r, tp_mm, tp_ev = sem("xt2_ready"), sem("x_transpose"), sem("xt_ready")
        t1_mm, t1_ev, x_mm, x_ev = map(sem, ("merge_nx", "merge_nx_masked", "merge_xnx", "merge_x_ready"))
        w_mm, w_ev, u_mm, u_ev, y_mm, y_ev, s_mm, s_ev, s_mid = map(sem, (
            "w_state_done", "w_ready", "u_done", "u_ready", "y_done", "y_added", "state_done", "state_next", "state_mid"))
        wo_in, ln_in = sem("wo_in"), sem("lnx_in")
        g_mm, g_ev, var_r, sd_r, y_r, y_T, yg_r, o_mm, x_r = map(sem, (
            "gate_done", "gate_ready", "var_ready", "sd_ready", "y_normed", "y_transposed", "yg_ready", "mixer_out_done", "x_mixed"))
        lg_mm, sc_r, m_r, rank_mm, ht_mm, ht_r, plan_r, moe_x = map(sem, (
            "logits_done", "scores_ready", "choice_ready", "ranks_done", "h_tok_transposed", "h_tok_ready",
            "plan_ready", "x_after_moe"))

        class Pass:

            def __init__(self, name):
                (self.picked, self.turned, self.given, self.gathered, self.staged, self.gate, self.up, self.silu,
                 self.hidden, self.hidden_turned, self.hidden_ready, self.down, self.out, self.scattered) = (
                    sem(f"{name}_{x}") for x in (
                        "picked", "pick_turned", "gates_turned", "gathered", "staged", "gate_done", "up_done", "silu_done",
                        "hidden_done", "hidden_turned", "hidden_ready", "down_done", "out_ready", "scattered"))

        moe_s = [Pass(f"moe{l}") for l in range(2)]
        more_in = [sem(f"moe{l}_more_weights") for l in range(2)]
        gm_in = sem("gmlp_rows_in")
        u_pj, u_gl, v_pj, v_add, v_gl, v_ln0, v_sd, v_ln, ws_tr, ws_ev, sp_mm, sp_ev, go_mm = map(sem, (
            "u_proj", "u_gelu", "v_proj", "v_biased", "v_gelu", "v_var", "v_sd", "v_normed", "ws_transposed", "ws_ready",
            "spatial_done", "spatial_gated", "gmlp_out"))
        f_T, f_ev, stored = sem("out_transposed"), sem("out_ready"), sem("out_stored")

        CONSTS = [0]

        U_MOD0, U_EX0, U_MOD1 = 0, 12, 60
        U_WIN, U_WS, U_WOUT, U_EX1 = 72, 80, 81, 85
        U_EX = [U_EX0, U_EX1]

        def landed(eng, n):
            eng.wait_ge(loaded[n % RING], 16 * (n // RING + 1))

        STEPS = [(d, c) for d in range(2) for c in ((0, 1, 2, 3) if d == 0 else (1, 0, 3, 2))]

        def lat_before(n):
            return n // 4 * 2 + max(0, n % 4 - 2)

        def entered_before(n):
            return n - (n + 3) // 4

        def handed_before(n):
            return n // 4 * 3 + n % 4

        def further(eng, l):
            eng.wait_ge(plan_r, 2 * (l + 1))
            return eng.value_load(plan[0:1, l, 0:1], min_val=0, max_val=MORE)

        block = ctx.enter_context(nc.Block())

        @block.sync
        def _(sp):
            def unit(n, src):
                sp.dma_start(ring[n % RING].rearrange("p (k f) -> p k f", f=src.shape[-1]), src)\
                  .then_inc(loaded[n % RING], 16)

            sp.dma_start(xtok[:, 0:2, :], A["ctx"][0].rearrange("(t p) d -> p t d", p=P)).then_inc(x_in, 16)
            sp.dma_start(xtok[:, 2:4, :], A["x"][0].rearrange("(t p) d -> p t d", p=P)).then_inc(x_in, 16)
            for u in range(12):
                if u >= RING:
                    sp.wait_ge(mod_done, u - RING + 1)
                unit(U_MOD0 + u, A["w_mod"][0].rearrange("(k p) (u f) -> u p k f", p=P, f=512)[u])
            for n, (w, h) in enumerate([(w, h) for w in ("rw_wk", "rw_wv", "rw_wr") for h in range(2)]):
                if n == 0:
                    sp.wait_ge(x_T, 16)
                if n >= 2:
                    sp.wait_ge(pj_mm, 4 * (n - 1))
                sp.dma_start(slots2[n % 2].rearrange("p (k f) -> p k f", f=512),
                             A[w][0].rearrange("(k p) (h f) -> h p k f", p=P, f=512)[h]).then_inc(pslot[n % 2], 16)
                if n == 1:
                    sp.wait_ge(mod_done, 12)
                    for i, w in enumerate(("rw_w1", "rw_a1")):
                        for d in range(2):
                            sp.dma_start(lora1[:, i, :, 64 * d:64 * d + 64],
                                         A[w][0, d].rearrange("(k p) c -> p k c", p=P)).then_inc(lora1_in, 16)
                    sp.dma_start(lora1[:, 2, :, :], A["rw_g1"][0].rearrange("(k p) c -> p k c", p=P))\
                      .then_inc(lora1_in, 16)
                    for i, w in enumerate(("rw_w2", "rw_a2")):
                        for d in range(2):
                            sp.dma_start(lora2[64 * d:64 * d + 64, i, :], A[w][0, d]).then_inc(lora2_in, 16)
                    sp.dma_start(lora2[:, 2, :], A["rw_g2"][0]).then_inc(lora2_in, 16)
            sp.wait_ge(til_r, 8)
            for h in range(2):
                sp.dma_start(wo[h].rearrange("p (k f) -> p k f", f=512),
                             A["rw_wo"][0].rearrange("(k p) (h f) -> h p k f", p=P, f=512)[h]).then_inc(wo_in, 16)
            sp.wait_ge(y_ev, 4)
            sp.dma_start(lng, A["rw_lnx_g"][0].partition_broadcast(P)).then_inc(ln_in, 16)
            sp.dma_start(lnb, A["rw_lnx_b"][0].partition_broadcast(P)).then_inc(ln_in, 16)

            def experts(l):
                src = [A["ex_w_gate"][l].rearrange("(i e) (k p) f -> i e p k f", p=P, e=2),
                       A["ex_w_up"][l].rearrange("(i e) (k p) f -> i e p k f", p=P, e=2),
                       A["ex_w_down"][l].rearrange("(i e) (k p) f -> i e p k f", p=P, e=2)]
                used = (moe_s[l].gate, moe_s[l].up, moe_s[l].down)

                def fetch(j, e, i, done):
                    s = ring[(U_EX[l] + 2 * j + e) % RING]
                    sp.dma_start(s.rearrange("p (k f) -> p k f", f=src[j].shape[-1]), src[j][i, e]).then_inc(done, 16)

                for j in range(3):
                    for e in range(2):
                        n = U_EX[l] + 2 * j + e
                        if l == 1:
                            sp.wait_ge(*freed[n - RING])
                        fetch(j, e, 0, loaded[n % RING])
                with sp.Fori(1, PAIRS) as i:
                    for j in range(3):
                        sp.wait_ge(used[j], i)
                        for e in range(2):
                            fetch(j, e, i, loaded[(U_EX[l] + 2 * j + e) % RING])
                by_expert = [x.rearrange("i e p k f -> (i e) p k f") for x in src]
                n_more = further(sp, l)
                with sp.Fori(0, MORE) as i:
                    with sp.If(n_more > i):
                        ids = [sp.value_load(plan[0:1, l, bass.ds(i * 2 + (1 + e), 1)], min_val=0, max_val=EXPERTS - 1)
                               for e in range(2)]
                        for j in range(3):
                            sp.wait_ge(used[j], i + PAIRS)
                            for e in range(2):
                                s = ring[(U_EX[l] + 2 * j + e) % RING]
                                sp.dma_start(s.rearrange("p (k f) -> p k f", f=src[j].shape[-1]), by_expert[j][ids[e]])\
                                  .then_inc(more_in[l], 16)
                return n_more

            freed = {}
            for j in range(3):
                for e in range(2):
                    freed[U_EX0 + 6 * (PAIRS - 1) + 2 * j + e] = (moe_s[0].gate, moe_s[0].up, moe_s[0].down)[j]
            for u in range(12):
                freed[U_MOD1 + u] = (mod_done, 12 + u + 1)
            for u in range(4):
                freed[U_WIN + u] = (u_pj, 4 * (u + 1))
                freed[U_WIN + 4 + u] = (v_pj, 2 * (u + 1))
                freed[U_WOUT + u] = (go_mm, u + 1)
            freed[U_WS] = (ws_tr, 4)

            sp.wait_ge(x_r, 1)
            n_more = experts(0)
            for u in range(12):
                if u < RING:
                    sp.wait_ge(freed[U_MOD1 + u - RING], n_more + PAIRS)
                else:
                    sp.wait_ge(*freed[U_MOD1 + u - RING])
                unit(U_MOD1 + u, A["w_mod"][1].rearrange("(k p) (u f) -> u p k f", p=P, f=512)[u])
            sp.dma_start(brow[:, 0, :], A["sg_b_in"][0, HALF:2 * HALF].partition_broadcast(P)).then_inc(gm_in, 16)
            sp.dma_start(brow[:, 1, :], A["sg_ln_g"][0].partition_broadcast(P)).then_inc(gm_in, 16)
            sp.dma_start(brow[:, 2, :], A["sg_ln_b"][0].partition_broadcast(P)).then_inc(gm_in, 16)
            sp.dma_start(bsrow[0:1, :], A["sg_b_s"][0].rearrange("(a g) i -> a (g i)", a=1)).then_inc(gm_in, 16)
            for u in range(8):
                sp.wait_ge(*freed[U_WIN + u - RING])
                unit(U_WIN + u, A["sg_w_in"][0].rearrange("(k p) (u f) -> u p k f", p=P, f=512)[u])
            sp.wait_ge(*freed[U_WS - RING])
            s = U_WS % RING
            sp.dma_start(ring[s][:, 0:VG * P].rearrange("p (g j) -> p g j", j=P),
                         A["sg_w_s"][0].rearrange("g i j -> i g j")).then_inc(loaded[s], 16)
            for u in range(4):
                sp.wait_ge(*freed[U_WOUT + u - RING])
                unit(U_WOUT + u, A["sg_w_out"][0].rearrange("(u k p) f -> u p k f", p=P, k=4)[u])
            experts(1)
            sp.wait_ge(f_ev, 2)
            sp.dma_start(out[0].rearrange("(t p) d -> p t d", p=P), tok_out).then_inc(stored, 16)
            sp.wait_ge(stored, 16)

        @block.gpsimd
        def _(pool):
            at = 0
            for name, n in (("c", 8), ("c_ctx", 8), ("norm1_g", 16), ("norm2_g", 16), ("rw_w0", 16), ("rw_a0", 16),
                            ("rw_kk", 8), ("rw_ka", 8), ("rw_rk", 8), ("final_g", 8)):
                src = A[name]
                while len(src.shape) > 1:
                    src = src.rearrange("a b c -> (a b c)") if len(src.shape) == 3 else src.rearrange("a b -> (a b)")
                pool.dma_start(prow[at:at + n, 0, :], src.rearrange("(r p) -> r p", p=P)).then_inc(rows_in, 16)
                at += n
            pool.dma_start(prow[at:at + 16, 0, :], A["sg_b_in"][0, 0:HALF].rearrange("(r p) -> r p", p=P)).then_inc(rows_in, 16)
            pool.dma_start(prow[0:96, 1, :], A["b_mod"].rearrange("l (r p) -> (l r) p", p=P)).then_inc(rows_in, 16)
            pool.dma_start(prow[0:48, 2, :], A["rw_mu"][0].rearrange("j (r p) -> (j r) p", p=P)).then_inc(rows_in, 16)
            pool.dma_start(wr, A["w_router"].rearrange("(k p) e -> p k e", p=P)).then_inc(small_in, 16)
            pool.dma_start(rbias, A["router_bias"].partition_broadcast(P)).then_inc(small_in, 16)

            made = [0]

            def make(ins):
                made[0] += 1
                ins.then_inc(cst, 1)
                pool.wait_ge(cst, made[0])

            make(pool.memset(ident, 0.0))
            make(pool.memset(ones, 1.0))
            for i, v in enumerate((1e-6, 64e-5, 1e-5)):
                make(pool.memset(epsc[:, i:i + 1], v))
            make(pool.memset(tie, 0.0))
            make(pool.memset(before, 1.0))
            make(pool.iota(iota, pattern=[[1, P]], base=0, channel_multiplier=0, allow_small_or_imprecise_dtypes=True))
            make(pool.affine_select(out=before, in_=before, compare_op=ALU.is_gt, fill=0.0, base=0,
                                    pattern=[[1, P]], channel_multiplier=-1))
            make(pool.affine_select(out=ident, in_=ident, compare_op=ALU.not_equal, fill=1.0, base=0,
                                    pattern=[[-1, P]], channel_multiplier=1))
            for i in range(1, 4):
                make(pool.memset(tie[:, 4 * i:4 * i + i], 1.0))
            CONSTS[0] = made[0]

            pool.wait_ge(mod_done, 12)
            make(pool.memset(hones, 0.0))
            make(pool.memset(merge_mask, 0.0))
            make(pool.memset(strict, 1.0))
            make(pool.memset(incl, 1.0))
            make(pool.memset(rksel, 0.0))
            for h in range(2):
                make(pool.memset(hones[64 * h:64 * h + 64, 64 * h:64 * h + 64], 1.0))
            for d, (step, cm) in enumerate(((1, -1), (-1, 1))):
                make(pool.affine_select(out=strict[:, d, :], in_=strict[:, d, :], compare_op=ALU.is_gt, fill=0.0,
                                        base=0, pattern=[[step, P]], channel_multiplier=cm))
                make(pool.affine_select(out=incl[:, d, :], in_=incl[:, d, :], compare_op=ALU.is_ge, fill=0.0,
                                        base=0, pattern=[[step, P]], channel_multiplier=cm))
            views = []
            for d in range(2):
                for i, m in enumerate([1] + LEVELS):
                    v = merge_mask[:, 7 * d + i, :].rearrange("p (b c) -> p b c", c=2 * m)
                    v = v[:, :, 0:m] if d == 0 else v[:, :, m:2 * m]
                    make(pool.memset(v, 1.0))
                    views.append((d, m, v))
            for d, m, v in views:
                first = m if d == 0 else 0
                make(pool.affine_select(out=v, in_=v, compare_op=ALU.is_ge, fill=0.0, base=-first,
                                        pattern=[[-2 * m, P // (2 * m)], [0, m]], channel_multiplier=1))
            for d, m, v in views:
                first = m if d == 0 else 0
                make(pool.affine_select(out=v, in_=v, compare_op=ALU.is_ge, fill=0.0, base=first + m - 1,
                                        pattern=[[2 * m, P // (2 * m)], [0, m]], channel_multiplier=-1))
            CONSTS.append(made[0])

        @block.scalar
        def _(act):
            act.wait_ge(rows_T, 3)
            act.wait_ge(cst, CONSTS[0])
            for i in range(3):
                n = (P, 96, 48)[i]
                act.copy(cols[:, i, 0:n], bank(0)[:, P * i:P * i + n]).then_inc(cols_ready, 1)
            act.wait_ge(cols_ready, 3)
            act.activation(silc[:, :, 0], c_cols, ACT.Silu).then_inc(sil_ready, 1)
            act.activation(silc[:, :, 1], ctx_cols, ACT.Silu).then_inc(sil_ready, 1)
            for b in range(8):
                act.wait_ge(x_T, 4 * b + 4)
                dst = xcT if b < 4 else xT
                act.copy(dst[:, 2 * (b % 4):2 * (b % 4) + 2, :], bank(b).rearrange("p (a t) -> p a t", t=T)).then_inc(xT_ready, 1)

            def norm(q, src, sqb, rsb):
                act.activation(sqb, src, ACT.Square).then_inc(n_sq, 1)
                act.wait_ge(n_ss, q + 1)
                act.activation(rsb, bank(0)[:, 0:T], ACT.Sqrt, bias=epsc[:, 0:1], scale=1.0 / D).then_inc(n_rt, 1)

            act.wait_ge(xT_ready, 8)
            norm(0, xcT, sq0, rs0)
            act.wait_ge(n_h, 1)
            norm(1, xT, sq0, rs0)

            for q in range(27):
                act.wait_ge(pj_mm, q + 1)
                src = bank(q % 8)
                if q < 8:
                    ins = act.copy(kT[:, q, :], src)
                elif q < 16:
                    hf, t = (q - 8) // 4, (q - 8) % 4
                    ins = act.copy(V[:, t, 512 * hf:512 * hf + 512], src)
                elif q < 24:
                    ins = act.copy(rT[:, q - 16, :], src[:, 0:T])
                elif q == 24:
                    ins = act.activation(tanw, src, ACT.Tanh)
                elif q == 25:
                    ins = act.copy(loa, src)
                else:
                    ins = act.activation(sigg, src[:, 0:T], ACT.Sigmoid)
                ins.then_inc(pj_ev, 1)
            act.wait_ge(kk_mx, 8)
            act.activation(xj[1], xj[1], ACT.Sqrt).then_inc(kk_rt, 1)

            for n, (d, c) in enumerate(STEPS):
                lat, last = c >= 2, n % 4 == 3
                nl = lat_before(n)
                for m in range(8):
                    act.wait_ge(z_mm, 4 * n + m // 4 + 1)
                    if m == 0 and n > 0:
                        act.wait_ge(bk_tok, 4 * handed_before(n))
                        act.wait_ge(til_r, n)
                        if nl:
                            act.wait_ge(bon_mm, nl)
                    act.activation(sig[:, m, :], psum[:, P * m:P * m + P], ACT.Sigmoid, bias=w0_cols[d][:, m:m + 1]).then_inc(z_sig, 1)
                for m in range(8):
                    act.wait_ge(z_mm, 4 * n + 2 + m // 4 + 1)
                    act.activation(icl[:, m, :], psum[:, 1024 + P * m:1024 + P * m + P], ACT.Sigmoid, bias=a0_cols[d][:, m:m + 1]).then_inc(z_sig, 1)
                act.wait_ge(lmid_r, 2 * n + 2)
                act.activation(smid, lmid, ACT.Exp, scale=-DECAY).then_inc(e_r, 1)
                act.activation(send, lend, ACT.Exp, scale=-DECAY).then_inc(e_r, 1)
                act.wait_ge(d0_r, n + 1)
                act.activation(E2, D1, ACT.Exp, scale=DECAY).then_inc(e_r, 1)
                act.activation(D0, D0, ACT.Exp, scale=-DECAY).then_inc(e_r, 1)
                act.wait_ge(e_r, 5 * n + 3)
                act.activation(D1, D1, ACT.Exp, scale=-DECAY).then_inc(e_r, 1)
                if not last:
                    for j, dst in enumerate((Btok, Btok, Ktok, Ktok)):
                        act.wait_ge(bk_T, 4 * handed_before(n) + j + 1)
                        act.copy(dst[:, 512 * (j % 2):512 * (j % 2) + 512], bank(4 + j)).then_inc(bk_tok, 1)
                act.wait_ge(w1_mm, 2 * n + 2)
                act.copy(W, psum[:, 0:1024]).then_inc(w1_ev, 1)
                for i in range(6):
                    for g in range(4):
                        act.wait_ge(tp_mm, 24 * n + 4 * i + g + 1)
                        dst = X if i == 0 else XT
                        act.copy(dst[:, 4 * g:4 * g + 4, :], bank(2 * g).rearrange("p (a b) -> p a b", b=P)).then_inc(tp_ev, 1)
                act.wait_ge(u_mm, 2 * n + 2)
                act.copy(U, psum[:, 1024:2048]).then_inc(u_ev, 1)

            act.wait_ge(g_mm, 4)
            act.copy(gT, psum[:, 2048:4096].rearrange("p (k t) -> p k t", t=T)).then_inc(g_ev, 1)
            act.wait_ge(var_r, 1)
            act.activation(yr, yv, ACT.Sqrt).then_inc(sd_r, 1)

            def router(l):
                act.wait_ge(lg_mm, l + 1)
                act.activation(route[:, 0:32], bank(1)[:, 0:32], ACT.Sigmoid).then_inc(sc_r, 1)
                for b in range(4):
                    act.wait_ge(ht_mm, 4 * l + b + 1)
                    act.copy(h2tok[:, b // 2, 512 * (b % 2):512 * (b % 2) + 512], bank(4 + b)).then_inc(ht_r, 1)

            def pair(Q, q):
                act.wait_ge(Q.gathered, q + 1)
                act.copy(xs, psum[:, 2048:3072].rearrange("p (k t) -> p k t", t=P)).then_inc(Q.staged, 1)
                act.wait_ge(Q.gate, q + 1)
                act.activation(sg, bank(4), ACT.Silu).then_inc(Q.silu, 1)
                act.wait_ge(Q.hidden_turned, q + 1)
                act.copy(heT, bank(6).rearrange("p (k t) -> p k t", t=P)).then_inc(Q.hidden_ready, 1)

            def moe(l):
                Q = moe_s[l]
                for b in range(4):
                    act.wait_ge(Q.turned, b + 1)
                    act.copy(giveT[:, 2 * b:2 * b + 2, :], bank(4 + b).rearrange("p (a t) -> p a t", t=T)).then_inc(Q.given, 1)
                with act.Fori(0, PAIRS) as i:
                    pair(Q, i)
                n_more = further(act, l)
                with act.Fori(0, MORE) as i:
                    with act.If(n_more > i):
                        act.wait_ge(Q.turned, i + 5)
                        act.copy(giveT[:, 0, :], bank(4)[:, 0:T]).then_inc(Q.given, 1)
                        pair(Q, i + PAIRS)

            act.wait_ge(x_r, 1)
            norm(2, xT, sq, rs)
            router(0)
            moe(0)
            act.wait_ge(moe_x, 8)
            norm(3, xT, sq, rs)
            for m in range(16):
                act.wait_ge(u_pj, m // 2 * 2 + 2)
                act.activation(uT[:, m, :], bank(m // 2)[:, T * (m % 2):T * (m % 2) + T], ACT.Gelu,
                               bias=bu_cols[:, m:m + 1]).then_inc(u_gl, 1)
            for q in range(8):
                u, t = q // 2, q % 2
                act.wait_ge(v_add, q + 1)
                act.activation(vtok[:, t, 512 * u:512 * u + 512], vtok[:, t, 512 * u:512 * u + 512], ACT.Gelu).then_inc(v_gl, 1)
            for b in range(4):
                act.wait_ge(ws_tr, b + 1)
                act.copy(wsT[:, 4 * b:4 * b + 4, :], bank(b).rearrange("p (a j) -> p a j", j=P)).then_inc(ws_ev, 1)
            act.wait_ge(v_ln0, 2)
            act.activation(rstd, mv[:, :, 1], ACT.Sqrt, bias=epsc[:, 2:3]).then_inc(v_sd, 1)
            act.wait_ge(x_r, 2)
            norm(4, xT, sq, rs)
            router(1)
            moe(1)
            act.wait_ge(moe_x, 16)
            norm(5, xT, sq, rs)
            for t in range(2):
                act.wait_ge(f_T, 2 * t + 2)
                act.copy(tok_out[:, t, :], psum[:, 1024 + 1024 * t:2048 + 1024 * t]).then_inc(f_ev, 1)

        @block.vector
        def _(dve):
            steps = [0]

            def link(ins):
                steps[0] += 1
                ins.then_inc(dst, 1)
                dve.wait_ge(dst, steps[0])

            def send_step(ins):
                steps[0] += 1
                ins.then_inc(dst, 1)

            def mods(l):
                dve.wait_ge(mod_done, 12 * (l + 1))
                dve.wait_ge(cols_ready, 3)
                link(dve.tensor_tensor(modc[:, l, :, :], bank(7)[:, 0:96].rearrange("p (a b) -> p a b", b=2),
                                       bc(bm_cols[l], 2, [P, 48, 2]), ALU.add))
                m = modc[:, l, :, :]
                todo = [(0, m[:, 8:16, 1], n1_cols[0]), (1, m[:, 8:16, 0], n1_cols[0]), (2, m[:, 32:40, 0], n2_cols[0])] if l == 0 \
                    else [(3, m[:, 8:16, 0], n1_cols[1]), (4, m[:, 32:40, 0], n2_cols[1])]
                for i, sc, g in todo:
                    ins = dve.scalar_tensor_tensor(out=gs[:, i, :], in0=sc, scalar=1.0, in1=g, op0=ALU.add, op1=ALU.mult)
                    send_step(ins)
                dve.wait_ge(dst, steps[0])

            def norm(q, src, dest, scale, shift, rsb):
                dve.wait_ge(n_rt, q + 1)
                link(dve.reciprocal(rsb, rsb))
                link(dve.tensor_tensor(dest, src, bc(rsb, 1, [P, KT, T]), ALU.mult))
                for k in range(KT):
                    if shift is None:
                        ins = dve.tensor_scalar(dest[:, k, :], dest[:, k, :], scale[:, k:k + 1], None, ALU.mult)
                    else:
                        ins = dve.tensor_scalar(dest[:, k, :], dest[:, k, :], scale[:, k:k + 1], shift[:, k:k + 1], ALU.mult, ALU.add)
                    if k < KT - 1:
                        send_step(ins)
                dve.wait_ge(dst, steps[0])
                ins.then_inc(n_h, 1)

            mods(0)
            norm(0, xcT, hT[:, :, 0:T], gs[:, 0, :], modc[:, 0, 0:8, 1], rs0)
            norm(1, xT, hT[:, :, T:2 * T], gs[:, 1, :], modc[:, 0, 0:8, 0], rs0)
            dve.wait_ge(n_h, 2)

            H, Hh = hT, KT // 2
            for a, b, to, fr, edge in ((0, Hh, slice(1, T), slice(0, T - 1), slice(0, 1)),
                                       (Hh, KT, slice(0, T - 1), slice(1, T), slice(T - 1, T))):
                send_step(dve.tensor_tensor(xx[:, a:b, to], H[:, a:b, fr], H[:, a:b, to], ALU.subtract))
                send_step(dve.tensor_scalar(xx[:, a:b, edge], H[:, a:b, edge], -1.0, None, ALU.mult))
            for qd in range(4):
                for k in range(2 * qd, 2 * qd + 2):
                    hl, xl = H[:, k, T:2 * T], xx[:, k, T:2 * T]
                    if qd < 2:
                        g = lambda v: v.rearrange("p (r c) -> p r c", c=GRID_W)
                        to, fr = (slice(1, GRID_W), slice(0, GRID_W - 1))[::1 if qd == 0 else -1]
                        edge = slice(0, 1) if qd == 0 else slice(GRID_W - 1, GRID_W)
                        send_step(dve.tensor_tensor(g(xl)[:, :, to], g(hl)[:, :, fr], g(hl)[:, :, to], ALU.subtract))
                        send_step(dve.tensor_scalar(g(xl)[:, :, edge], g(hl)[:, :, edge], -1.0, None, ALU.mult))
                    else:
                        to, fr = (slice(GRID_W, T), slice(0, T - GRID_W))[::1 if qd == 2 else -1]
                        edge = slice(0, GRID_W) if qd == 2 else slice(T - GRID_W, T)
                        send_step(dve.tensor_tensor(xl[:, to], hl[:, fr], hl[:, to], ALU.subtract))
                        send_step(dve.tensor_scalar(xl[:, edge], hl[:, edge], -1.0, None, ALU.mult))
            dve.wait_ge(dst, steps[0])
            read_by = (8, 16, 24, 25, 26, 27)
            for i, j in enumerate((2, 3, 0, 1, 4, 5)):
                if i >= 2:
                    dve.wait_ge(pj_mm, read_by[i - 2])
                lo = T if j in (0, 5) else 0
                for k in range(KT):
                    dve.scalar_tensor_tensor(out=xj[i % 2][:, k, lo:2 * T], in0=xx[:, k, lo:2 * T],
                                             scalar=mu_cols[j][:, k:k + 1], in1=H[:, k, lo:2 * T],
                                             op0=ALU.mult, op1=ALU.add).then_inc(xj_ready, 1)

            dve.wait_ge(pj_ev, 27)
            dve.wait_ge(cst, CONSTS[1])
            for k in range(KT):
                send_step(dve.tensor_scalar(kkT[:, k, :], kT[:, k, :], kk_cols[:, k:k + 1], None, ALU.mult))
            dve.wait_ge(dst, steps[0])
            for k in range(KT):
                dve.tensor_tensor(xj[0][:, k, :], kkT[:, k, :], kkT[:, k, :], ALU.mult).then_inc(kk_sq, 1)
            for k in range(KT):
                dve.wait_ge(kk_ss, k + 1)
                dve.tensor_scalar(xj[1][:, k, :], bank(k), 1e-24, None, ALU.max).then_inc(kk_mx, 1)
            dve.wait_ge(kk_rt, 1)
            link(dve.reciprocal(xj[1], xj[1]))
            link(dve.tensor_tensor(kkT, kkT, xj[1], ALU.mult))
            link(dve.tensor_scalar(omka, ka_cols, -1.0, 1.0, ALU.mult, ALU.add))
            for h in range(2):
                send_step(dve.tensor_copy(rksel[64 * h:64 * h + 64, :, h], rk_cols[64 * h:64 * h + 64, :]))
            dve.memset(bonus, 0.0).then_inc(kk_ready, 1)
            dve.wait_ge(kk_ready, 1)

            for n, (d, c) in enumerate(STEPS):
                lat, last, first = c >= 2, n % 4 == 3, n % 4 == 0
                nl, ns = lat_before(n), handed_before(n)
                tok = slice(P * c, P * c + P)
                dve.wait_ge(z_sig, 16 * n + 16)
                rev = slice(None, None, -1) if d else slice(None)
                for m in range(KT):
                    send_step(dve.tensor_tensor_scan(D1[:, m, rev], ones[:, rev], sig[:, m, rev], 0.0, ALU.mult, ALU.add))
                dve.wait_ge(dst, steps[0])
                if n:
                    dve.wait_ge(s_mid, n)
                mid, end = P // 2, (P - 1 if d == 0 else 0)
                dve.tensor_copy(lmid, D1[:, :, mid]).then_inc(lmid_r, 1)
                dve.tensor_tensor(lend, D1[:, :, end], D1[:, :, mid], ALU.subtract).then_inc(lmid_r, 1)
                dve.wait_ge(lmid_r, 2 * n + 2)
                link(dve.tensor_tensor(D1, D1, bc(lmid, 2, [P, KT, P]), ALU.subtract))
                dve.tensor_tensor(D0, D1, sig, ALU.subtract).then_inc(d0_r, 1)
                send_step(dve.tensor_tensor(BT, kkT[:, :, tok], icl, ALU.mult))
                for m in range(KT):
                    send_step(dve.tensor_scalar(KTl[:, m, :], icl[:, m, :], ka_cols[:, m:m + 1], omka[:, m:m + 1], ALU.mult, ALU.add))
                dve.wait_ge(dst, steps[0])
                link(dve.tensor_tensor(KTl, KTl, kT[:, :, tok], ALU.mult))
                if lat:
                    dve.wait_ge(d0_r, n + 1)
                    dve.tensor_tensor(sig, KTl, rT[:, :, P * (c - 2):P * (c - 1)], ALU.mult).then_inc(prod_r, 1)
                dve.wait_ge(e_r, 5 * n + 5)
                send_step(dve.scalar_tensor_tensor(out=AT, in0=kkT[:, :, tok], scalar=-1.0, in1=D0, op0=ALU.mult, op1=ALU.mult))
                send_step(dve.tensor_tensor(BT, BT, E2, ALU.mult))
                if lat:
                    send_step(dve.tensor_tensor(RT, rT[:, :, P * (c - 2):P * (c - 1)], D1, ALU.mult))
                dve.wait_ge(dst, steps[0])
                if lat:
                    dve.wait_ge(prod_r, nl + 1)
                dve.tensor_tensor(KTl, KTl, E2, ALU.mult).then_inc(til_r, 1)
                dve.wait_ge(e_r, 5 * n + 5)
                if first:
                    dve.memset(S, 0.0).then_inc(s_mid, 1)
                else:
                    dve.tensor_tensor(S, S, bc(smid, 2, [P, KT, P]), ALU.mult).then_inc(s_mid, 1)
                if lat:
                    dve.wait_ge(bon_mm, nl + 1)
                    dve.tensor_tensor(bonus[:, c - 2, :], bonus[:, c - 2, :], bank(0)[:, 0:16], ALU.add).then_inc(bon_ev, 1)

                def masked(dest, b, mask, q):
                    dve.wait_ge(pr_mm, q)
                    dve.tensor_tensor(dest, bank(b).rearrange("p (a t) -> p a t", t=P), bc(mask, 1, [P, 4, P]), ALU.mult).then_inc(pr_ev, 1)

                base = 8 * n + 8 * nl
                for g in range(4):
                    masked(buf1[:, 4 * g:4 * g + 4, :], g, strict[:, d, :], base + g + 1)
                if lat:
                    for g in range(4):
                        masked(buf2[:, 4 * g:4 * g + 4, :], 4 + g, incl[:, d, :], base + 4 + g + 1)
                    dve.wait_ge(y1_mm, 2 * nl + 2)
                    if d == 0:
                        dve.tensor_copy(Yacc[:, c - 2, :], psum[:, 1024:2048]).then_inc(y1_ev, 1)
                    else:
                        dve.tensor_tensor(Yacc[:, c - 2, :], Yacc[:, c - 2, :], psum[:, 1024:2048], ALU.add).then_inc(y1_ev, 1)
                base += 8 if lat else 4
                for g in range(4):
                    masked(buf1[:, 4 * g:4 * g + 4, :], 4 + g, strict[:, d, :], base + g + 1)
                if lat:
                    for g in range(4):
                        masked(buf2[:, 4 * g:4 * g + 4, :], g, incl[:, d, :], base + 4 + g + 1)
                base_nt = base
                for g in range(4):
                    hd = slice(4 * g, 4 * g + 4)
                    dve.wait_ge(pr_ev, base_nt + g + 1)
                    link(dve.tensor_tensor(XT[:, hd, :], buf1[:, hd, :], bc(merge_mask[:, 7 * (1 - d), :], 1, [P, 4, P]), ALU.mult))
                    dve.tensor_tensor(XT[:, hd, :], XT[:, hd, :], bc(ident, 1, [P, 4, P]), ALU.add).then_inc(xt2_r, 1)
                for l in range(6):
                    for g in range(4):
                        hd = slice(4 * g, 4 * g + 4)
                        dve.wait_ge(t1_mm, 24 * n + 4 * l + g + 1)
                        dve.tensor_tensor(T1[:, hd, :], bank(2 * g).rearrange("p (a t) -> p a t", t=P),
                                          bc(merge_mask[:, 7 * d + 1 + l, :], 1, [P, 4, P]), ALU.mult).then_inc(t1_ev, 1)
                    for g in range(4):
                        hd = slice(4 * g, 4 * g + 4)
                        dve.wait_ge(x_mm, 24 * n + 4 * l + g + 1)
                        dest = (X if l < 5 else XT)[:, hd, :]
                        if l == 0 or l == 5:
                            dve.wait_ge(tp_ev, 24 * n + (4 * (0 if l == 0 else 5)) + g + 1)
                        dve.tensor_tensor(dest, dest, bank(2 * g + 1).rearrange("p (a t) -> p a t", t=P), ALU.add).then_inc(x_ev, 1)
                if not first:
                    dve.wait_ge(w_mm, 2 * entered_before(n) + 2)
                    dve.wait_ge(w1_ev, n + 1)
                    dve.tensor_tensor(W, W, psum[:, 0:1024], ALU.add).then_inc(w_ev, 1)
                if lat:
                    dve.wait_ge(y_mm, 2 * nl + 2)
                    dve.wait_ge(y1_ev, nl + 1)
                    dve.tensor_tensor(Yacc[:, c - 2, :], Yacc[:, c - 2, :], psum[:, 2048:3072], ALU.add).then_inc(y_ev, 1)
                if not last:
                    dve.wait_ge(s_mm, 2 * ns + 2)
                    dve.wait_ge(s_mid, n + 1)
                    link(dve.tensor_tensor(D1, psum[:, 3072:4096].rearrange("p (k t) -> p k t", t=P),
                                           bc(hones, 1, [P, KT, P]), ALU.mult))
                    link(dve.tensor_tensor(D1, D1, S, ALU.add))
                    dve.tensor_tensor(S, D1, bc(send, 2, [P, KT, P]), ALU.mult).then_inc(s_ev, 1)
                    dve.wait_ge(s_ev, ns + 1)

            dve.wait_ge(y_ev, 4)
            Yh = Yacc.rearrange("p t (h c) -> p (t h) c", c=HS)
            Yq = ysq.rearrange("p t (h c) -> p (t h) c", c=HS)
            NH = NT * HEADS
            dve.wait_ge(u_ev, 8)
            link(dve.tensor_reduce(ym, Yh, AX.X, ALU.add))
            link(dve.tensor_scalar(ym, ym, 1.0 / HS, None, ALU.mult))
            link(dve.tensor_tensor(Yh, Yh, bc(ym, 2, [P, NH, HS]), ALU.subtract))
            link(dve.tensor_tensor(Yq, Yh, Yh, ALU.mult))
            link(dve.tensor_reduce(yv, Yq, AX.X, ALU.add))
            dve.tensor_scalar(yv, yv, 1.0 / HS, 64e-5, ALU.mult, ALU.add).then_inc(var_r, 1)
            dve.wait_ge(sd_r, 1)
            link(dve.reciprocal(yr, yr))
            link(dve.tensor_tensor(Yh, Yh, bc(yr, 2, [P, NH, HS]), ALU.mult))
            dve.wait_ge(ln_in, 32)
            link(dve.tensor_tensor(Yacc, Yacc, bc(lng, 1, [P, NT, D]), ALU.mult))
            link(dve.tensor_tensor(Yacc, Yacc, bc(lnb, 1, [P, NT, D]), ALU.add))
            dve.wait_ge(bon_ev, 4)
            link(dve.tensor_tensor(Yq, V[:, 2:4, :].rearrange("p t (h c) -> p (t h) c", c=HS),
                                   bc(bonus.rearrange("p t h -> p (t h)"), 2, [P, NH, HS]), ALU.mult))
            dve.tensor_tensor(Yacc, Yacc, ysq, ALU.add).then_inc(y_r, 1)
            for b in range(4):
                dve.wait_ge(y_T, b + 1)
                dve.wait_ge(g_ev, 1)
                dve.tensor_tensor(ygT[:, 2 * b:2 * b + 2, :], bank(b).rearrange("p (a t) -> p a t", t=T),
                                  gT[:, 2 * b:2 * b + 2, :], ALU.mult).then_inc(yg_r, 1)

            def residual(src, gate, s, q0, done, fin):
                for m in range(KT):
                    dve.wait_ge(s, q0 + (m // 2 * 2 + 2 if done else 1))
                    ins = dve.scalar_tensor_tensor(out=xT[:, m, :], in0=src(m), scalar=gate[:, m:m + 1], in1=xT[:, m, :],
                                                   op0=ALU.mult, op1=ALU.add)
                    if m < KT - 1:
                        send_step(ins)
                    else:
                        dve.wait_ge(dst, steps[0])
                        ins.then_inc(fin, 1)

            halfbank = lambda b0: (lambda m: bank(b0 + m // 2)[:, T * (m % 2):T * (m % 2) + T])
            residual(halfbank(4), modc[:, 0, 16:24, 0], o_mm, 0, True, x_r)

            def router(l):
                dve.wait_ge(small_in, 32)
                dve.wait_ge(sc_r, l + 1)
                dve.wait_ge(cst, CONSTS[0])
                R = route
                M, wts = R[:, 384:416], R[:, 416:448]
                sc3 = R[:, 0:32].rearrange("p (t e) -> p t e", e=16)
                b = R[:, 32:64]
                b3 = b.rearrange("p (t e) -> p t e", e=16)
                v = b.rearrange("p (g e) -> p g e", e=4)
                hi, lo = R[:, 64:80].rearrange("p (g e) -> p g e", e=2), R[:, 80:96].rearrange("p (g e) -> p g e", e=2)
                top, sec, gsc = R[:, 96:104], R[:, 104:112], R[:, 112:120]
                link(dve.tensor_tensor(b3, sc3, bc(rbias, 1, [P, 2, 16]), ALU.add))
                send_step(dve.tensor_tensor(hi, v[:, :, 0:2], v[:, :, 2:4], ALU.max))
                link(dve.tensor_tensor(lo, v[:, :, 0:2], v[:, :, 2:4], ALU.min))
                send_step(dve.tensor_tensor(top, hi[:, :, 0], hi[:, :, 1], ALU.max))
                send_step(dve.tensor_tensor(sec, hi[:, :, 0], hi[:, :, 1], ALU.min))
                link(dve.tensor_tensor(gsc, lo[:, :, 0], lo[:, :, 1], ALU.max))
                link(dve.tensor_tensor(sec, sec, gsc, ALU.max))
                link(dve.tensor_tensor(gsc, top, sec, ALU.add))

                def chosen(val, groups, few, dest):
                    n = groups
                    one = R[:, 128:128 + 16 * n].rearrange("p (g i j) -> p g i j", i=4, j=4)
                    two = R[:, 256:256 + 16 * n].rearrange("p (g i j) -> p g i j", i=4, j=4)
                    vj, vi = bc(val, 2, [P, n, 4, 4]), bc(val, 3, [P, n, 4, 4])
                    send_step(dve.tensor_tensor(one, vj, vi, ALU.is_gt))
                    link(dve.tensor_tensor(two, vj, vi, ALU.is_equal))
                    flat = two.rearrange("p g i j -> p g (i j)")
                    link(dve.tensor_tensor(flat, flat, bc(tie, 1, [P, n, 16]), ALU.mult))
                    link(dve.tensor_tensor(one, one, two, ALU.add))
                    link(dve.tensor_reduce(dest, one, AX.X, ALU.add))
                    link(dve.tensor_scalar(dest, dest, few - 0.5, None, ALU.is_lt))

                sel_e = M.rearrange("p (g e) -> p g e", e=4)
                sel_g = R[:, 96:104].rearrange("p (t g) -> p t g", g=4)
                chosen(gsc.rearrange("p (t g) -> p t g", g=4), 2, 1, sel_g)
                chosen(v, 8, 2, sel_e)
                dve.tensor_tensor(sel_e, sel_e, bc(R[:, 96:104], 2, [P, 8, 4]), ALU.mult).then_inc(m_r, 1)
                dve.wait_ge(m_r, l + 1)
                w3, rk = wts.rearrange("p (t e) -> p t e", e=16), R[:, 448:480]
                link(dve.tensor_tensor(wts, M, R[:, 0:32], ALU.mult))
                link(dve.tensor_reduce(R[:, 104:106], w3, AX.X, ALU.add))
                link(dve.reciprocal(R[:, 106:108], R[:, 104:106]))
                link(dve.tensor_tensor(w3, w3, bc(R[:, 106:108], 2, [P, 2, 16]), ALU.mult))
                dve.wait_ge(rank_mm, l + 1)
                Rk, cnt, extra, cum = R[:, 128:160], R[:, 160:176], R[:, 176:192], R[:, 192:208]
                link(dve.tensor_copy(R[:, 128:176], bank(3)[:, 0:48]))
                link(dve.scalar_tensor_tensor(out=rk, in0=Rk, scalar=1.0, in1=M, op0=ALU.add, op1=ALU.mult))
                link(dve.tensor_scalar(rk, rk, -1.0, None, ALU.add))
                link(dve.tensor_scalar(extra, cnt, float(SLOTS), None, ALU.is_gt))
                for n in range(2 * SLOTS, T, SLOTS):
                    link(dve.scalar_tensor_tensor(out=extra, in0=cnt, scalar=float(n), in1=extra, op0=ALU.is_gt, op1=ALU.add))
                link(dve.tensor_tensor_scan(cum, ones[:, 0:16], extra, 0.0, ALU.mult, ALU.add))
                four, lots = R[:, 208:212], R[:, 212:220]
                link(dve.tensor_tensor(four, cum[:, 15:16].broadcast_to([P, MORE]), iota[:, 0:2 * MORE:2], ALU.is_gt))
                link(dve.tensor_reduce(R[:, 220:221], four, AX.X, ALU.add))
                by_lot = R[:, 256:384].rearrange("p (v e) -> p v e", e=EXPERTS)
                link(dve.tensor_tensor(by_lot, bc(cum, 1, [P, 2 * MORE, EXPERTS]), bc(iota[:, 0:2 * MORE], 2, [P, 2 * MORE, EXPERTS]), ALU.is_le))
                link(dve.tensor_reduce(lots, by_lot, AX.X, ALU.add))
                link(dve.tensor_scalar(lots, lots, float(EXPERTS - 1), None, ALU.min))
                dve.tensor_copy(plan[:, l, 0:1], R[:, 220:221]).then_inc(plan_r, 1)
                dve.tensor_copy(plan[:, l, 1:9], lots).then_inc(plan_r, 1)
                start, past = R[:, 160:176], R[:, 224:256]
                far = Rk.rearrange("p (t e) -> p t e", e=16)
                link(dve.tensor_tensor(start, cum, extra, ALU.subtract))
                link(dve.tensor_scalar(start, start, float(SLOTS), 1.0 - SLOTS, ALU.mult, ALU.add))
                link(dve.tensor_scalar(past, Rk, SLOTS - 0.5, None, ALU.is_gt))
                link(dve.tensor_tensor(past, past, M, ALU.mult))
                link(dve.tensor_tensor(far, far, bc(start, 1, [P, 2, 16]), ALU.add))
                link(dve.tensor_tensor(Rk, Rk, past, ALU.mult))
                placeA, placeB, gateA, gateB = R[:, 480:482], R[:, 482:484], R[:, 484:486], R[:, 486:488]
                link(dve.tensor_reduce(placeA, far, AX.X, ALU.max))
                link(dve.tensor_reduce(placeB, far, AX.X, ALU.add))
                link(dve.tensor_tensor(placeB, placeB, placeA, ALU.subtract))
                for pl, gt in ((placeA, gateA), (placeB, gateB)):
                    p3 = past.rearrange("p (t e) -> p t e", e=16)
                    link(dve.tensor_tensor(p3, far, bc(pl, 2, [P, 2, 16]), ALU.is_equal))
                    link(dve.tensor_tensor(past, past, wts, ALU.mult))
                    link(dve.tensor_reduce(gt, p3, AX.X, ALU.add))
                link(dve.tensor_scalar(R[:, 480:484], R[:, 480:484], -1.0, None, ALU.add))

            def choose(Q):
                rk, wts = route[:, 448:480], route[:, 416:448]
                for t in range(NT):
                    e_s = lambda v: v[:, t, :].rearrange("p (e s) -> p e s", s=SLOTS)
                    dve.tensor_tensor(e_s(pick), bc(rk[:, 16 * t:16 * t + 16], 2, [P, EXPERTS, SLOTS]),
                                      bc(iota[:, 0:SLOTS], 1, [P, EXPERTS, SLOTS]), ALU.is_equal).then_inc(Q.picked, 1)
                    dve.wait_ge(Q.picked, 2 * t + 1)
                    dve.tensor_tensor(e_s(gpick), e_s(pick), bc(wts[:, 16 * t:16 * t + 16], 2, [P, EXPERTS, SLOTS]),
                                      ALU.mult).then_inc(Q.picked, 1)

            def choose_further(Q, i):
                place, gate = [route[:, 480 + 2 * x:482 + 2 * x] for x in range(2)], [route[:, 484 + 2 * x:486 + 2 * x] for x in range(2)]
                done = 4

                def then(ins):
                    nonlocal done
                    done += 1
                    ins.then_inc(Q.picked, 1)
                    dve.wait_ge(Q.picked, i * 11 + done)

                for t in range(NT):
                    A_, B_ = place[0][:, t:t + 1], place[1][:, t:t + 1]
                    p1, g1, g2 = pick[:, t, 0:P], gpick[:, t, 0:P], gpick[:, t, P:2 * P]
                    then(dve.tensor_scalar(p1, iota, A_, None, ALU.is_equal))
                    then(dve.scalar_tensor_tensor(out=p1, in0=iota, scalar=B_, in1=p1, op0=ALU.is_equal, op1=ALU.add))
                    then(dve.tensor_scalar(g1, iota, A_, gate[0][:, t:t + 1], ALU.is_equal, ALU.mult))
                    then(dve.tensor_scalar(g2, iota, B_, gate[1][:, t:t + 1], ALU.is_equal, ALU.mult))
                    then(dve.tensor_tensor(g1, g1, g2, ALU.add))
                then(dve.tensor_scalar(route[:, 480:484], route[:, 480:484], -float(P), None, ALU.add))

            def pair(Q, q):
                dve.wait_ge(Q.silu, q + 1)
                dve.wait_ge(Q.up, q + 1)
                dve.tensor_tensor(he, sg, bank(5), ALU.mult).then_inc(Q.hidden, 1)
                dve.wait_ge(Q.down, q + 1)
                dve.tensor_copy(ye, psum[:, 3072:4096]).then_inc(Q.out, 1)

            def moe(l):
                Q = moe_s[l]
                choose(Q)
                with dve.Fori(0, PAIRS) as i:
                    pair(Q, i)
                n_more = further(dve, l)
                with dve.Fori(0, MORE) as i:
                    with dve.If(n_more > i):
                        choose_further(Q, i)
                        pair(Q, i + PAIRS)
                for m in range(KT):
                    dve.wait_ge(Q.scattered, n_more + PAIRS)
                    dve.scalar_tensor_tensor(out=xT[:, m, :], in0=halfbank(0)(m), scalar=modc[:, l, 40 + m:41 + m, 0], in1=xT[:, m, :],
                                             op0=ALU.mult, op1=ALU.add).then_inc(moe_x, 1)

            dve.wait_ge(x_r, 1)
            norm(2, xT, h2T, gs[:, 2, :], modc[:, 0, 24:32, 0], rs)
            router(0)
            moe(0)
            mods(1)
            dve.wait_ge(moe_x, 8)
            norm(3, xT, h2T, gs[:, 3, :], modc[:, 1, 0:8, 0], rs)
            dve.wait_ge(gm_in, 64)
            for q in range(8):
                u, t = q // 2, q % 2
                dve.wait_ge(v_pj, q + 1)
                dve.tensor_tensor(vtok[:, t, 512 * u:512 * u + 512], bank(q), brow[:, 0, 512 * u:512 * u + 512], ALU.add).then_inc(v_add, 1)
            for t in range(2):
                for u in range(4):
                    dve.wait_ge(v_gl, 2 * u + t + 1)
                    send_step(dve.bn_stats(stat[:, t, u, :], vtok[:, t, 512 * u:512 * u + 512]))
                dve.wait_ge(dst, steps[0])
                dve.bn_aggr(mv[:, t, :], stat[:, t, :, :]).then_inc(v_ln0, 1)
            dve.wait_ge(v_sd, 1)
            dve.wait_ge(v_ln0, 2)
            link(dve.reciprocal(rstd, rstd))
            for t in range(2):
                link(dve.tensor_scalar(vtok[:, t, :], vtok[:, t, :], mv[:, t, 0:1], rstd[:, t:t + 1], ALU.subtract, ALU.mult))
                link(dve.tensor_tensor(vtok[:, t, :], vtok[:, t, :], brow[:, 1, :], ALU.mult))
                dve.tensor_tensor(vtok[:, t, :], vtok[:, t, :], brow[:, 2, :], ALU.add).then_inc(v_ln, 1)
            for g in range(VG):
                dve.wait_ge(sp_mm, g // 2 * 2 + 2)
                dve.wait_ge(u_gl, g + 1)
                dve.tensor_tensor(uT[:, g, :], uT[:, g, :], bank(4 + g // 2 % 4)[:, T * (g % 2):T * (g % 2) + T], ALU.mult).then_inc(sp_ev, 1)
            residual(halfbank(0), modc[:, 1, 16:24, 0], go_mm, 3, False, x_r)
            dve.wait_ge(x_r, 2)
            norm(4, xT, h2T, gs[:, 4, :], modc[:, 1, 24:32, 0], rs)
            router(1)
            moe(1)
            dve.wait_ge(moe_x, 16)
            norm(5, xT, h2T, fin_cols, None, rs)

        @block.tensor
        def _(pe):
            def product(dest, lhs, rhs, k):
                for i in range(k):
                    mm = pe.matmul(dest, lhs(i), rhs(i), start=(i == 0), stop=(i == k - 1))
                return mm

            pe.wait_ge(cst, CONSTS[0])
            pe.wait_ge(rows_in, 16 * 13)
            for i in range(3):
                n = (P, 96, 48)[i]
                pe.transpose(bank(0)[:, P * i:P * i + n], prow[0:n, i, :], ident[0:n, 0:n]).then_inc(rows_T, 1)
            pe.wait_ge(cols_ready, 3)
            pe.wait_ge(x_in, 32)
            for b in range(8):
                for a in range(2):
                    for t in range(2):
                        k = 2 * (b % 4) + a
                        pe.transpose(bank(b)[:, T * a + P * t:T * a + P * t + P],
                                     xtok[:, 2 * (b // 4) + t, P * k:P * k + P], ident).then_inc(x_T, 1)

            def modulation(l):
                for u in range(12):
                    landed(pe, (U_MOD0, U_MOD1)[l] + u)
                    w = ring[((U_MOD0, U_MOD1)[l] + u) % RING].rearrange("p (k f) -> p k f", f=512)
                    for m in range(4):
                        j = 4 * u + m
                        mm = product(bank(7)[:, 2 * j:2 * j + 2], lambda k: w[:, k, P * m:P * m + P], lambda k: silc[:, k, :], KT)
                    mm.then_inc(mod_done, 1)

            def norm(q, sqb):
                pe.wait_ge(n_sq, q + 1)
                product(bank(0)[:, 0:T], lambda k: ones, lambda k: sqb[:, k, :], KT).then_inc(n_ss, 1)

            pe.wait_ge(sil_ready, 2)
            pe.wait_ge(xT_ready, 8)
            modulation(0)
            norm(0, sq0)
            norm(1, sq0)
            pe.wait_ge(n_rt, 2)

            def slot(n):
                pe.wait_ge(pslot[n % 2], 16 * (n // 2 + 1))
                return slots2[n % 2].rearrange("p (k f) -> p k f", f=512)

            q = 0
            for m in range(8):
                if m % 4 == 0:
                    w = slot(m // 4)
                if m == 0:
                    pe.wait_ge(xj_ready, 8)
                product(bank(q % 8), lambda k: w[:, k, P * (m % 4):P * (m % 4) + P], lambda k: xj[0][:, k, :], KT).then_inc(pj_mm, 1)
                q += 1
            pe.wait_ge(xj_ready, 16)
            for hf in range(2):
                w = slot(2 + hf)
                for t in range(4):
                    pe.wait_ge(pj_ev, q - 7)
                    product(bank(q % 8), lambda k: xj[1][:, k, P * t:P * t + P], lambda k: w[:, k, :], KT).then_inc(pj_mm, 1)
                    q += 1
            pe.wait_ge(xj_ready, 24)
            for m in range(8):
                if m % 4 == 0:
                    w = slot(4 + m // 4)
                pe.wait_ge(pj_ev, q - 7)
                product(bank(q % 8)[:, 0:T], lambda k: w[:, k, P * (m % 4):P * (m % 4) + P], lambda k: xj[0][:, k, T:2 * T], KT).then_inc(pj_mm, 1)
                q += 1
            pe.wait_ge(lora1_in, 80)
            for i in range(3):
                pe.wait_ge(xj_ready, 32 + 8 * i)
                pe.wait_ge(pj_ev, q - 7)
                src = xj[(1, 0, 1)[i]]
                lo = T if i == 2 else 0
                product(bank(q % 8)[:, 0:2 * T - lo], lambda k: lora1[:, i, k, :], lambda k: src[:, k, lo:2 * T], KT).then_inc(pj_mm, 1)
                q += 1
            pe.wait_ge(pj_ev, q)
            for k in range(KT):
                pe.wait_ge(kk_sq, k + 1)
                pe.matmul(bank(k), hones, xj[0][:, k, :], start=True, stop=True).then_inc(kk_ss, 1)
            pe.wait_ge(kk_ready, 1)
            pe.wait_ge(lora2_in, 80)

            def place(h):
                return 8 * (h // 8) + 4 * (h % 2) + h % 8 // 2

            def rows_of(h):
                return slice(64 * (h % 2), 64 * (h % 2) + 64)

            for n, (d, c) in enumerate(STEPS):
                lat, last, first = c >= 2, n % 4 == 3, n % 4 == 0
                nl, ns = lat_before(n), handed_before(n)
                rows = slice(64 * d, 64 * d + 64)
                if n:
                    pe.wait_ge(u_ev, n)
                    if entered_before(n):
                        pe.wait_ge(w_ev, entered_before(n))
                for i, src in enumerate((tanw, loa)):
                    for m in range(8):
                        mm = pe.matmul(psum[:, 1024 * i + P * m:1024 * i + P * m + P], lora2[rows, i, P * m:P * m + P],
                                       src[rows, P * c:P * c + P], start=True, stop=True)
                        if m % 4 == 3:
                            mm.then_inc(z_mm, 1)
                if lat:
                    pe.wait_ge(prod_r, nl + 1)
                    pe.wait_ge(z_sig, 16 * n + 16)
                    for m in range(8):
                        mm = pe.matmul(bank(0)[:, 2 * m:2 * m + 2], sig[:, m, :], rksel[:, m, :], start=True, stop=True)
                    mm.then_inc(bon_mm, 1)
                pe.wait_ge(til_r, n + 1)
                pe.wait_ge(z_sig, 16 * n + 16)
                if nl:
                    pe.wait_ge(y_ev, nl)
                if ns:
                    pe.wait_ge(s_ev, ns)
                if not last:
                    for j, src in enumerate((BT, BT, KTl, KTl)):
                        for m in range(4):
                            mm = pe.transpose(bank(4 + j)[:, P * m:P * m + P], src[:, 4 * (j % 2) + m, :], ident)
                        mm.then_inc(bk_T, 1)

                def pairs(left, right, b0):
                    for g in range(4):
                        for a in range(4):
                            h = 8 * (g // 2) + 2 * a + g % 2
                            mm = pe.matmul(bank(b0 + g)[:, P * a:P * a + P], left[rows_of(h), h // 2, :],
                                           right[rows_of(h), h // 2, :], start=True, stop=True)
                        mm.then_inc(pr_mm, 1)

                base = 8 * n + 8 * nl
                if lat:
                    pe.wait_ge(bon_ev, nl + 1)
                pairs(KTl, AT, 0)
                if lat:
                    pe.wait_ge(bk_tok, 4 * (ns + (0 if last else 1)))
                    pairs(KTl, RT, 4)
                pe.wait_ge(pr_ev, base + 4)
                for h in range(HEADS):
                    mm = pe.matmul(psum[:, 64 * h:64 * h + 64], buf1[:, place(h), :], V[:, c, 64 * h:64 * h + 64], start=True, stop=True)
                    if h % 8 == 7:
                        mm.then_inc(w1_mm, 1)
                if lat:
                    pe.wait_ge(pr_ev, base + 8)
                    for h in range(HEADS):
                        mm = pe.matmul(psum[:, 1024 + 64 * h:1024 + 64 * h + 64], buf2[:, place(h), :], V[:, c, 64 * h:64 * h + 64], start=True, stop=True)
                        if h % 8 == 7:
                            mm.then_inc(y1_mm, 1)
                base += 8 if lat else 4
                if not last:
                    pe.wait_ge(bk_tok, 4 * (ns + 1))
                pairs(BT, AT, 4)
                pe.wait_ge(w1_ev, n + 1)
                if lat:
                    pe.wait_ge(y1_ev, nl + 1)
                    pairs(BT, RT, 0)
                    pe.wait_ge(pr_ev, base + 8)
                pe.wait_ge(pr_ev, base + 4)

                def turn(src, i, g):
                    for a in range(4):
                        mm = pe.transpose(bank(2 * g)[:, P * a:P * a + P], src[:, 4 * g + a, :], ident)
                    mm.then_inc(tp_mm, 1)

                for g in range(4):
                    pe.wait_ge(xt2_r, 4 * n + g + 1)
                    turn(XT, 0, g)
                for l in range(6):
                    for g in range(4):
                        pe.wait_ge(tp_ev, 24 * n + 4 * l + g + 1)
                        for a in range(4):
                            h = 4 * g + a
                            mm = pe.matmul(bank(2 * g)[:, P * a:P * a + P], buf1[:, h, :], X[:, h, :], start=True, stop=True)
                        mm.then_inc(t1_mm, 1)
                    for g in range(4):
                        pe.wait_ge(t1_ev, 24 * n + 4 * l + g + 1)
                        for a in range(4):
                            h = 4 * g + a
                            if l < 5:
                                mm = pe.matmul(bank(2 * g + 1)[:, P * a:P * a + P], XT[:, h, :], T1[:, h, :], start=True, stop=True)
                            else:
                                mm = pe.matmul(bank(2 * g + 1)[:, P * a:P * a + P], T1[:, h, :], XT[:, h, :], start=True, stop=True)
                        mm.then_inc(x_mm, 1)
                    if l < 5:
                        for g in range(4):
                            pe.wait_ge(x_ev, 24 * n + 4 * l + g + 1)
                            turn(X, l + 1, g)
                pe.wait_ge(x_ev, 24 * n + 24)
                pe.wait_ge(s_mid, n + 1)
                if not first:
                    for m in range(8):
                        mm = pe.matmul(psum[:, P * m:P * m + P], AT[:, m, :], S[:, m, :], start=True, stop=True)
                        if m % 4 == 3:
                            mm.then_inc(w_mm, 1)
                    pe.wait_ge(w_ev, entered_before(n) + 1)
                for h in range(HEADS):
                    mm = pe.matmul(psum[:, 1024 + 64 * h:1024 + 64 * h + 64], XT[:, place(h), :], W[:, 64 * h:64 * h + 64], start=True, stop=True)
                    if h % 8 == 7:
                        mm.then_inc(u_mm, 1)
                pe.wait_ge(u_ev, n + 1)
                if lat:
                    for m in range(8):
                        pe.matmul(psum[:, 2048 + P * m:2048 + P * m + P], RT[:, m, :], S[:, m, :], start=True, stop=False,
                                  skip_group_check=True)
                        for h in (2 * m, 2 * m + 1):
                            mm = pe.matmul(psum[:, 2048 + 64 * h:2048 + 64 * h + 64], buf2[:, place(h), :], U[:, 64 * h:64 * h + 64],
                                           start=False, stop=True, skip_group_check=True)
                        if m % 4 == 3:
                            mm.then_inc(y_mm, 1)
                if not last:
                    for m in range(8):
                        ch = slice(P * m, P * m + P)
                        pe.matmul(psum[:, 3072 + P * m:3072 + P * m + P], Btok[:, ch], U[:, ch], start=True, stop=False)
                        mm = pe.matmul(psum[:, 3072 + P * m:3072 + P * m + P], Ktok[:, ch], V[:, c, ch], start=False, stop=True)
                        if m % 4 == 3:
                            mm.then_inc(s_mm, 1)

            pe.wait_ge(y_ev, 4)
            pe.wait_ge(s_ev, 6)
            for m in range(8):
                mm = pe.matmul(psum[:, 2048 + T * m:2048 + T * m + T], lora2[:, 2, P * m:P * m + P], sigg, start=True, stop=True)
                if m % 2 == 1:
                    mm.then_inc(g_mm, 1)
            pe.wait_ge(y_r, 1)
            pe.wait_ge(u_ev, 8)
            for b in range(4):
                for a in range(2):
                    for t in range(2):
                        k = 2 * b + a
                        mm = pe.transpose(bank(b)[:, T * a + P * t:T * a + P * t + P], Yacc[:, t, P * k:P * k + P], ident)
                mm.then_inc(y_T, 1)
            pe.wait_ge(wo_in, 32)
            pe.wait_ge(yg_r, 4)
            for m in range(8):
                w = wo[m // 4].rearrange("p (k f) -> p k f", f=512)
                product(bank(4 + m // 2)[:, T * (m % 2):T * (m % 2) + T], lambda k: w[:, k, P * (m % 4):P * (m % 4) + P],
                        lambda k: ygT[:, k, :], KT).then_inc(o_mm, 1)

            def router(l, q):
                pe.wait_ge(n_h, q + 1)
                pe.wait_ge(small_in, 32)
                for t in range(2):
                    mm = product(bank(1)[:, 16 * t:16 * t + 16], lambda k: h2T[:, k, P * t:P * t + P], lambda k: wr[:, k, :], KT)
                mm.then_inc(lg_mm, 1)
                for b in range(4):
                    for a in range(4):
                        mm = pe.transpose(bank(4 + b)[:, P * a:P * a + P],
                                          h2T[:, 4 * (b % 2) + a, P * (b // 2):P * (b // 2) + P], ident)
                    mm.then_inc(ht_mm, 1)
                pe.wait_ge(m_r, l + 1)
                M = [route[:, 384 + 16 * t:400 + 16 * t] for t in range(2)]
                R = bank(3)
                pe.matmul(R[:, 0:16], before, M[0], start=True, stop=True)
                for dest, first in ((R[:, 16:32], before), (R[:, 32:48], ones)):
                    pe.matmul(dest, first, M[1], start=True, stop=False)
                    mm = pe.matmul(dest, ones, M[0], start=False, stop=True)
                mm.then_inc(rank_mm, 1)

            def turn_gates(Q):
                pe.wait_ge(Q.picked, 4)
                for b in range(4):
                    for a in range(2):
                        for t in range(NT):
                            i = 2 * b + a
                            mm = pe.transpose(bank(4 + b)[:, T * a + P * t:T * a + P * t + P],
                                              gpick[:, t, P * i:P * i + P], ident)
                    mm.then_inc(Q.turned, 1)

            def gather(Q, i, given):
                pe.wait_ge(Q.given, given)
                for k in range(KT):
                    for t in range(NT):
                        mm = pe.matmul(psum[:, 2048 + P * k:2048 + P * k + P], h2tok[:, t, P * k:P * k + P],
                                       pick[:, t, 0:P] if i is None else pick[:, t, bass.ds(i * P, P)], start=(t == 0), stop=(t == NT - 1))
                mm.then_inc(Q.gathered, 1)

            def scatter(Q, q, i, opening=False):
                pe.wait_ge(Q.out, q + 1)
                for m in range(KT):
                    mm = pe.matmul(bank(m // 2)[:, T * (m % 2):T * (m % 2) + T], ye[:, P * m:P * m + P], giveT[:, i, :],
                                   start=(opening and m % 2 == 0), stop=False, skip_group_check=True)
                mm.then_inc(Q.scattered, 1)

            def expert_pair(l, Q, q, weights):
                w = [ring[(U_EX[l] + n) % RING] for n in range(6)]
                pe.wait_ge(Q.staged, q + 1)
                for j, done in enumerate((Q.gate, Q.up)):
                    weights(j)
                    for k in range(KT):
                        for e in range(2):
                            mm = pe.matmul(bank(4 + j)[SLOTS * e:SLOTS * e + SLOTS, :], xs[:, k, SLOTS * e:SLOTS * e + SLOTS],
                                           w[2 * j + e][:, FFN * k:FFN * k + FFN], start=(k == 0), stop=(k == KT - 1))
                    mm.then_inc(done, 1)
                pe.wait_ge(Q.hidden, q + 1)
                for k in range(FT):
                    mm = pe.transpose(bank(6)[:, P * k:P * k + P], he[:, P * k:P * k + P], ident)
                mm.then_inc(Q.hidden_turned, 1)
                weights(2)
                pe.wait_ge(Q.hidden_ready, q + 1)
                for hf in range(2):
                    for k in range(FT):
                        for e in range(2):
                            mm = pe.matmul(bank(6 + hf)[SLOTS * e:SLOTS * e + SLOTS, :], heT[:, k, SLOTS * e:SLOTS * e + SLOTS],
                                           w[4 + e][:, D * k + 512 * hf:D * k + 512 * hf + 512],
                                           start=(k == 0), stop=(k == FT - 1))
                mm.then_inc(Q.down, 1)

            def moe(l):
                def weights(i):
                    def wait(j):
                        for e in range(2):
                            n = U_EX[l] + 2 * j + e
                            at = 16 * (n // RING + 1)
                            pe.wait_ge(loaded[n % RING], at if i is None else i * 16 + at)
                    return wait

                Q = moe_s[l]
                pe.wait_ge(ht_r, 4 * (l + 1))
                turn_gates(Q)
                gather(Q, 0, 4)
                expert_pair(l, Q, 0, weights(None))
                gather(Q, 1, 4)
                scatter(Q, 0, 0, opening=True)
                expert_pair(l, Q, 1, weights(1))
                with pe.Fori(2, PAIRS) as i:
                    gather(Q, i, 4)
                    scatter(Q, i - 1, i - 1)
                    expert_pair(l, Q, i, weights(i))
                scatter(Q, PAIRS - 1, PAIRS - 1)
                n_more = further(pe, l)
                with pe.Fori(0, MORE) as i:
                    with pe.If(n_more > i):
                        pe.wait_ge(Q.picked, i * 11 + 15)
                        for t in range(NT):
                            mm = pe.transpose(bank(4)[:, P * t:P * t + P], gpick[:, t, 0:P], ident)
                        mm.then_inc(Q.turned, 1)
                        gather(Q, None, i + 5)
                        expert_pair(l, Q, i + PAIRS, lambda j: pe.wait_ge(more_in[l], i * 96 + 96))
                        scatter(Q, i + PAIRS, 0)

            norm(2, sq)
            router(0, 2)
            moe(0)
            modulation(1)
            norm(3, sq)
            pe.wait_ge(n_h, 4)
            pe.wait_ge(n_rt, 4)
            pe.wait_ge(moe_x, 8)
            for m in range(16):
                n = U_WIN + m // 4
                landed(pe, n)
                w = ring[n % RING].rearrange("p (k f) -> p k f", f=512)
                product(bank(m // 2)[:, T * (m % 2):T * (m % 2) + T], lambda k: w[:, k, P * (m % 4):P * (m % 4) + P],
                        lambda k: h2T[:, k, :], KT).then_inc(u_pj, 1)
            for q in range(8):
                u, t = q // 2, q % 2
                n = U_WIN + 4 + u
                landed(pe, n)
                pe.wait_ge(u_gl, 2 * q + 2)
                w = ring[n % RING].rearrange("p (k f) -> p k f", f=512)
                product(bank(q), lambda k: h2T[:, k, P * t:P * t + P], lambda k: w[:, k, :], KT).then_inc(v_pj, 1)
            landed(pe, U_WS)
            wsr = ring[U_WS % RING][:, 0:VG * P].rearrange("p (g j) -> p g j", j=P)
            for b in range(4):
                pe.wait_ge(v_add, b + 1)
                for a in range(4):
                    mm = pe.transpose(bank(b)[:, P * a:P * a + P], wsr[:, 4 * b + a, :], ident)
                mm.then_inc(ws_tr, 1)
            pe.wait_ge(ws_ev, 4)
            pe.wait_ge(v_ln, 2)
            pe.wait_ge(v_add, 8)
            for g in range(VG):
                if g >= 8:
                    pe.wait_ge(sp_ev, g // 2 * 2 - 6)
                for t in range(2):
                    dest = bank(4 + g // 2 % 4)[:, T * (g % 2) + P * t:T * (g % 2) + P * t + P]
                    pe.matmul(dest, vtok[:, t, P * g:P * g + P], wsT[:, g, :], start=True, stop=False)
                    mm = pe.matmul(dest, ones[0:1, :], bsrow[0:1, P * g:P * g + P], start=False, stop=True)
                mm.then_inc(sp_mm, 1)
            for u in range(4):
                n = U_WOUT + u
                landed(pe, n)
                pe.wait_ge(sp_ev, 4 * u + 4)
                w = ring[n % RING].rearrange("p (k f) -> p k f", f=D)
                for m in range(KT):
                    for k in range(4):
                        mm = pe.matmul(bank(m // 2)[:, T * (m % 2):T * (m % 2) + T], w[:, k, P * m:P * m + P],
                                       uT[:, 4 * u + k, :], start=(u == 0 and k == 0 and m % 2 == 0), stop=False,
                                       skip_group_check=True)
                mm.then_inc(go_mm, 1)
            pe.wait_ge(x_r, 2)
            norm(4, sq)
            router(1, 4)
            moe(1)
            pe.wait_ge(moe_x, 16)
            norm(5, sq)
            pe.wait_ge(n_h, 6)
            for t in range(2):
                for j in range(2):
                    for a in range(4):
                        k = 4 * j + a
                        mm = pe.transpose(psum[:, 1024 + 1024 * t + P * k:1024 + 1024 * t + P * k + P],
                                          h2T[:, k, P * t:P * t + P], ident)
                    mm.then_inc(f_T, 1)


_INS = ["x", "c", "ctx", "c_ctx", "w_mod", "b_mod", "norm1_g", "norm2_g", "rw_mu", "rw_wr", "rw_wk", "rw_wv", "rw_wo",
        "rw_w0", "rw_w1", "rw_w2", "rw_a0", "rw_a1", "rw_a2", "rw_g1", "rw_g2", "rw_kk", "rw_ka", "rw_rk", "rw_lnx_g",
        "rw_lnx_b", "sg_w_in", "sg_b_in", "sg_ln_g", "sg_ln_b", "sg_w_s", "sg_b_s", "sg_w_out", "w_router",
        "router_bias", "ex_w_gate", "ex_w_up", "ex_w_down", "final_g"]


def kernel(**inputs):
    import numpy as np
    import concourse.bacc as bacc
    from concourse.bass_utils import run_bass_kernel_spmd as run

    nc = bacc.Bacc("TRN2", target_bir_lowering=False, num_devices=1)
    arrays, aps = {}, {}
    for name in _INS:
        a = np.ascontiguousarray(inputs[name])
        arrays[f"in_{name}"] = a
        aps[name] = nc.dram_tensor(f"in_{name}", a.shape, mybir.dt.from_np(a.dtype), kind="ExternalInput").ap()
    out = nc.dram_tensor("out_0", (1, T, D), F32, kind="ExternalOutput").ap()
    build(nc, aps, out)
    return run(nc, [arrays], core_ids=[0]).results[0]["out_0"]
```

```python
import concourse.bass as bass
from concourse import mybir
from contextlib import ExitStack
from math import exp

F32 = mybir.dt.float32
ACT = mybir.ActivationFunctionType
ALU = mybir.AluOpType
AX = mybir.AxisListType

P = 128
D = 1024
KT = D // P
T = 256
NT = T // P
HEADS, HS = 16, 64
GRID_W = 64
EXPERTS, FFN = 16, 512
FT = FFN // P
HALF = 2048
VG = HALF // P
SLOTS = 64
PAIRS = EXPERTS // 2
MORE = 4
UNIT = 4096
RING = 6
DECAY = exp(-0.5)
LEVELS = [2, 4, 8, 16, 32, 64]


def bc(ap, dim, shape):
    return ap.unsqueeze(dim).broadcast_to(shape)


def build(nc, A, out):
    ctx = ExitStack()
    with ctx:
        def sem(name):
            return ctx.enter_context(nc.semaphore(name))

        ARENA = 53200
        arena = ctx.enter_context(nc.sbuf_tensor("arena", [P, ARENA], F32))
        psum = ctx.enter_context(nc.psum_tensor("psum", [P, 8 * 512], F32))

        def bank(i):
            return psum[:, 512 * i:512 * i + 512]

        class Place:

            def __init__(self, at):
                self.at = at

            def __call__(self, *dims):
                n = 1
                for x in dims:
                    n *= x
                ap = arena[:, self.at:self.at + n]
                self.at += n
                assert self.at <= ARENA, self.at
                if len(dims) == 2:
                    ap = ap.rearrange("p (a b) -> p a b", b=dims[1])
                elif len(dims) == 3:
                    ap = ap.rearrange("p (a b c) -> p a b c", b=dims[1], c=dims[2])
                return ap

        keep = Place(0)
        ident = keep(P)
        ones = keep(P)
        xT = keep(KT, T)
        cols, mus = keep(2, P), keep(48)
        modc = keep(2, 48, 2)
        silc = keep(KT, 32)
        modsel = keep(2)
        gs = keep(5, KT)
        epsc = keep(4)
        tie = keep(16)
        before = keep(P)
        iota = keep(P)
        wr = keep(KT, EXPERTS)
        rbias = keep(EXPERTS)
        route = keep(512)
        plan = keep(2, 9).bitcast(mybir.dt.int32)
        KEEP_END = keep.at

        c_cols, ctx_cols = cols[:, 0, 0:8], cols[:, 0, 8:16]
        n1_cols = [cols[:, 0, 16 + 8 * l:24 + 8 * l] for l in range(2)]
        n2_cols = [cols[:, 0, 32 + 8 * l:40 + 8 * l] for l in range(2)]
        w0_cols = [cols[:, 0, 48 + 8 * d:56 + 8 * d] for d in range(2)]
        a0_cols = [cols[:, 0, 64 + 8 * d:72 + 8 * d] for d in range(2)]
        kk_cols, ka_cols, rk_cols = cols[:, 0, 80:88], cols[:, 0, 88:96], cols[:, 0, 96:104]
        fin_cols, bu_cols = cols[:, 0, 104:112], cols[:, 0, 112:128]
        bm_cols = [cols[:, 1, 48 * l:48 * l + 48] for l in range(2)]
        mu_cols = [mus[:, 8 * j:8 * j + 8] for j in range(6)]

        RING_AT = KEEP_END
        ring = [arena[:, RING_AT + UNIT * s:RING_AT + UNIT * (s + 1)] for s in range(RING)]

        rw = Place(KEEP_END)
        kT = rw(KT, 2 * T)
        kkT = rw(KT, 2 * T)
        hones = rw(P)
        merge_mask = rw(2 * 7, P)
        strict = rw(2, P)
        incl = rw(2, P)
        rT = rw(KT, T)
        V = rw(4, D)
        tanw = rw(2 * T)
        loa = rw(2 * T)
        sigg = rw(T)
        lora2 = rw(3, D)
        omka = rw(KT)
        rksel = rw(KT, 2)
        smid, send = rw(KT), [rw(KT), rw(KT)]
        lmid, lend = rw(KT), rw(KT)
        bonus = rw(NT, HEADS)
        Yacc = rw(NT, D)
        rw.at = max(rw.at, RING_AT + RING * UNIT - 1024)
        TEMP_AT = rw.at
        wo = [arena[:, KEEP_END + UNIT * s:KEEP_END + UNIT * (s + 1)] for s in range(2)]
        kk_tmp = [tanw, loa]
        lora1 = arena[:, TEMP_AT - NT * D:TEMP_AT + 1024].rearrange("p (w k c) -> p w k c", w=3, c=P)

        pj = Place(TEMP_AT + 1024)
        xj = [pj(KT, 2 * T)]
        hT = pj(KT, 2 * T)
        xx = pj(KT, 2 * T)
        xj.append(pj(KT, 2 * T))
        slots2 = [pj(UNIT), pj(UNIT)]
        xtok = arena[:, pj.at - 3 * UNIT:pj.at - 2 * UNIT].rearrange("p (t d) -> p t d", d=D)
        xcT = xx[:, 0:4, :].rearrange("p a b -> p (a b)").rearrange("p (k t) -> p k t", t=T)
        sq0 = xx[:, 4:8, :].rearrange("p a b -> p (a b)").rearrange("p (k t) -> p k t", t=T)
        crow = arena[0:16, pj.at - UNIT + 384:pj.at - UNIT + 512]
        prow = arena[:, pj.at - UNIT:pj.at - UNIT + 3 * P].rearrange("p (a b) -> p a b", b=P)
        modrow0 = arena[:, pj.at - UNIT + 512:pj.at - UNIT + 512 + 1024].rearrange("p (a b) -> p a b", b=512)
        rs0 = [arena[:, pj.at - UNIT + 1536 + T * i:pj.at - UNIT + 1536 + T * i + T] for i in range(2)]
        ck = Place(TEMP_AT)
        AT, BT, KTl, RT = ck(KT, P), ck(KT, P), ck(KT, P), ck(KT, P)
        Btok, Ktok = ck(D), ck(D)
        buf1, buf2 = ck(HEADS, P), ck(HEADS, P)
        X, XT, T1 = ck(HEADS, P), ck(HEADS, P), ck(HEADS, P)
        sig, icl, D0, D1, E2 = ck(KT, P), ck(KT, P), ck(KT, P), ck(KT, P), ck(KT, P)
        W, U, S = ck(D), ck(D), ck(KT, P)
        yo = Place(TEMP_AT)
        lng, lnb = yo(D), yo(D)
        ysq = yo(NT, D)
        ym, yv, yr = yo(NT * HEADS), yo(NT * HEADS), yo(NT * HEADS)
        gT, ygT = yo(KT, T), yo(KT, T)
        yb = [E2.rearrange("p k t -> p (k t)"), D0.rearrange("p k t -> p (k t)")]

        mx = Place(RING_AT + RING * UNIT)
        h2T = mx(KT, T)
        sq = mx(KT, T)
        rs = mx(T)
        gm = Place(mx.at)
        h2tok = mx(NT, D)
        pick = mx(NT, EXPERTS * SLOTS)
        gpick = sq.rearrange("p a b -> p (a b)").rearrange("p (t c) -> p t c", t=NT)
        giveT = mx(PAIRS, T)
        xs = mx(KT, P)
        sg = mx(FFN)
        he = mx(FFN)
        heT = mx(FT, P)
        ye = mx(D)
        ahead = [arena[:, mx.at + UNIT * e:mx.at + UNIT * (e + 1)] for e in range(2)]
        uT = gm(VG, T)
        vtok = gm(NT, HALF)
        wsT = mx(VG, P)
        brow = mx(3, HALF)
        bsrow = mx(VG * P)
        stat = mx(2, 4, 6)
        mv = mx(2, 2)
        rstd = mx(2)
        modrow1 = ye.rearrange("p (a b) -> p a b", b=512)
        tok_out = h2tok

        cst = sem("constants_made")
        rows_in, x_in, small_in, lora1_in, lora2_in = map(sem, ("rows_in", "x_in", "small_in", "lora1_in", "lora2_in"))
        rows_T, cols_ready, sil_ready = sem("rows_transposed"), sem("cols_ready"), sem("silu_ready")
        x_T, xT_ready = sem("x_transposed"), sem("xT_ready")
        loaded = [sem(f"unit_loaded{s}") for s in range(RING)]
        mod_done, mod_row, mod_cols = sem("mod_unit_done"), sem("mod_row_ready"), sem("mod_cols_done")
        c_in, c_T, silc0 = sem("c_in"), sem("c_transposed"), sem("silu_zeros")
        n_sq, n_ss, n_rt, n_m, n_h = map(sem, ("norm_squares", "norm_sum", "norm_root", "norm_scaled", "norm_ready"))
        n_div = sem("norm_divided")
        mods_r, x_tile = sem("mods_ready"), sem("x_tile_updated")
        dst = sem("dve_step")
        xj_ready, pj_mm, pj_ev = sem("mix_ready"), sem("proj_done"), sem("proj_evacuated")
        pslot = [sem("proj_loaded0"), sem("proj_loaded1")]
        kk_raw, kk_sq, kk_ss, kk_mx, kk_rt, kk_ready = map(sem, ("kk_raw", "kk_squares", "kk_sums", "kk_max", "kk_root", "kk_ready"))
        z_mm, z_sig, lmid_r, d0_r, e_r = map(sem, ("z_done", "z_sigmoid", "mid_ready", "log_excl", "exps_ready"))
        til_r, prod_r, bon_mm, bon_ev = map(sem, ("tilde_ready", "bonus_prod", "bonus_done", "bonus_added"))
        bk_T, bk_tok = sem("tok_transposed"), sem("tok_ready")
        pr_mm, pr_ev = sem("pairs_done"), sem("pairs_masked")
        w1_mm, w1_ev = sem("w1_done"), sem("w1_ready")
        y1_mm, y1_ev = sem("y1_done"), sem("y1_added")
        xt2_r, tp_mm, tp_ev = sem("xt2_ready"), sem("x_transpose"), sem("xt_ready")
        t1_mm, t1_ev, x_mm, x_ev = map(sem, ("merge_nx", "merge_nx_masked", "merge_xnx", "merge_x_ready"))
        u_mm, u_ev, y_mm, y_ev, s_mm, s_ev, s_mid = map(sem, (
            "u_done", "u_ready", "y_done", "y_added", "state_done", "state_next", "state_mid"))
        wo_in, ln_in = sem("wo_in"), sem("lnx_in")
        g_mm, g_ev, var_r, sd_r, y_r, y_T, yg_r, o_mm = map(sem, (
            "gate_done", "gate_ready", "var_ready", "sd_ready", "y_normed", "y_transposed", "yg_ready", "mixer_out_done"))
        lg_mm, sc_r, m_r, rank_mm, ht_mm, ht_r, plan_r = map(sem, (
            "logits_done", "scores_ready", "choice_ready", "ranks_done", "h_tok_transposed", "h_tok_ready",
            "plan_ready"))

        class Pass:

            def __init__(self, name):
                (self.picked, self.turned, self.given, self.gathered, self.staged, self.gate, self.up, self.silu,
                 self.hidden, self.hidden_turned, self.hidden_ready, self.down, self.out, self.scattered) = (
                    sem(f"{name}_{x}") for x in (
                        "picked", "pick_turned", "gates_turned", "gathered", "staged", "gate_done", "up_done", "silu_done",
                        "hidden_done", "hidden_turned", "hidden_ready", "down_done", "out_ready", "scattered"))

        moe_s = [Pass(f"moe{l}") for l in range(2)]
        ahead_in = sem("second_gate_weights")
        more_in = [sem(f"moe{l}_more_weights") for l in range(2)]
        gm_in = sem("gmlp_rows_in")
        u_pj, u_gl, v_pj, v_add, v_gl, v_ln0, v_sd, v_ln, ws_tr, ws_ev, sp_mm, sp_ev, go_mm = map(sem, (
            "u_proj", "u_gelu", "v_proj", "v_biased", "v_gelu", "v_var", "v_sd", "v_normed", "ws_transposed", "ws_ready",
            "spatial_done", "spatial_gated", "gmlp_out"))
        f_T, f_ev, stored = sem("out_transposed"), sem("out_ready"), sem("out_stored")

        CONSTS = [0]

        EARLY = 4
        FIRST_MODS = 9
        U_MOD0, U_EX0, U_MOD1 = 0, 12, 60
        U_WIN, U_WS, U_MOD1B, U_WOUT, U_EX1 = 64, 72, 73, 81, 85
        U_EX = [U_EX0, U_EX1]

        def mod_at(l, u):
            return U_MOD0 + u if l == 0 else U_MOD1 + u if u < EARLY else U_MOD1B + u - EARLY

        def landings(n):
            elsewhere = sum(1 for at in U_EX if n >= at + RING and (n - at) % RING < 2)
            return 16 * (n // RING + 1 - elsewhere)

        def landed(eng, n):
            eng.wait_ge(loaded[n % RING], landings(n))

        STEPS = [(d, c) for d in range(2) for c in ((0, 1, 2, 3) if d == 0 else (1, 0, 3, 2))]

        def lat_before(n):
            return n // 4 * 2 + max(0, n % 4 - 2)

        def handed_before(n):
            return n // 4 * 3 + n % 4

        def halves(d):
            return [slice(64 * h, 64 * h + 64) for h in ((0, 1), (1, 0))[d]]

        def further(eng, l):
            eng.wait_ge(plan_r, 2 * (l + 1))
            return eng.value_load(plan[0:1, l, 0:1], min_val=0, max_val=MORE)

        block = ctx.enter_context(nc.Block())

        @block.sync
        def _(sp):
            def unit(n, src):
                sp.dma_start(ring[n % RING].rearrange("p (k f) -> p k f", f=src.shape[-1]), src)\
                  .then_inc(loaded[n % RING], 16)

            for i, name in enumerate(("c", "c_ctx")):
                src = A[name].rearrange("a b -> (a b)") if len(A[name].shape) == 2 else A[name]
                sp.dma_start(crow[8 * i:8 * i + 8, :], src.rearrange("(r p) -> r p", p=P)).then_inc(c_in, 16)
            def first_mods(us):
                for u in us:
                    if u >= RING:
                        sp.wait_ge(mod_done, u - RING + 1)
                    unit(U_MOD0 + u, A["w_mod"][0].rearrange("(k p) (u f) -> u p k f", p=P, f=512)[u])

            first_mods(range(EARLY))
            sp.wait_ge(rows_in, 16 * 13)
            for i, name in enumerate(("ctx", "x")):
                sp.dma_start(xtok[:, 2 * i:2 * i + 2, :], A[name][0].rearrange("(t p) d -> p t d", p=P)).then_inc(x_in, 16)
            first_mods(range(EARLY, FIRST_MODS))
            for n, (w, h) in enumerate([(w, h) for w in ("rw_wk", "rw_wv", "rw_wr") for h in range(2)]):
                if n == 1:
                    first_mods(range(FIRST_MODS, 12))
                    sp.wait_ge(mod_cols, 12)
                    sp.wait_ge(n_div, 2)
                if n >= 2:
                    sp.wait_ge(pj_mm, 4 * (n - 1))
                sp.dma_start(slots2[n % 2].rearrange("p (k f) -> p k f", f=512),
                             A[w][0].rearrange("(k p) (h f) -> h p k f", p=P, f=512)[h]).then_inc(pslot[n % 2], 16)
                if n == 1:
                    sp.wait_ge(mod_done, 12)
                    for i, w in enumerate(("rw_w1", "rw_a1")):
                        for d in range(2):
                            sp.dma_start(lora1[:, i, :, 64 * d:64 * d + 64],
                                         A[w][0, d].rearrange("(k p) c -> p k c", p=P)).then_inc(lora1_in, 16)
                    sp.dma_start(lora1[:, 2, :, :], A["rw_g1"][0].rearrange("(k p) c -> p k c", p=P))\
                      .then_inc(lora1_in, 16)
                    for i, w in enumerate(("rw_w2", "rw_a2")):
                        for d in range(2):
                            sp.dma_start(lora2[64 * d:64 * d + 64, i, :], A[w][0, d]).then_inc(lora2_in, 16)
                    sp.dma_start(lora2[:, 2, :], A["rw_g2"][0]).then_inc(lora2_in, 16)
            sp.wait_ge(til_r, 8)
            for h in range(2):
                sp.dma_start(wo[h].rearrange("p (k f) -> p k f", f=512),
                             A["rw_wo"][0].rearrange("(k p) (h f) -> h p k f", p=P, f=512)[h]).then_inc(wo_in, 16)
            sp.wait_ge(xt2_r, 32)
            sp.dma_start(lng, A["rw_lnx_g"][0].partition_broadcast(P)).then_inc(ln_in, 16)
            sp.dma_start(lnb, A["rw_lnx_b"][0].partition_broadcast(P)).then_inc(ln_in, 16)

            def experts(l):
                src = [A["ex_w_gate"][l].rearrange("(i e) (k p) f -> i e p k f", p=P, e=2),
                       A["ex_w_up"][l].rearrange("(i e) (k p) f -> i e p k f", p=P, e=2),
                       A["ex_w_down"][l].rearrange("(i e) (k p) f -> i e p k f", p=P, e=2)]
                used = (moe_s[l].gate, moe_s[l].up, moe_s[l].down)

                def fetch(j, e, i, done, to=None):
                    s = ring[(U_EX[l] + 2 * j + e) % RING] if to is None else to
                    sp.dma_start(s.rearrange("p (k f) -> p k f", f=src[j].shape[-1]), src[j][i, e]).then_inc(done, 16)

                if l == 0:
                    sp.wait_ge(y_T, 4)
                    sp.wait_ge(g_mm, 4)
                def second_gate():
                    if l == 1:
                        sp.wait_ge(v_ln, 2)
                        sp.wait_ge(sp_mm, VG)
                    for e in range(2):
                        fetch(0, e, 1, ahead_in, ahead[e])

                for j in ((1, 2, 0), (0, 1, 2))[l]:
                    if l == 0 and j == 0:
                        second_gate()
                        sp.wait_ge(o_mm, 8)
                    for e in range(2):
                        n = U_EX[l] + 2 * j + e
                        if l == 1:
                            sp.wait_ge(*freed[n - RING])
                        fetch(j, e, 0, loaded[n % RING])
                    if l == 1 and j == 0:
                        second_gate()

                def stage(j, i):
                    sp.wait_ge(used[j], 1 if j == 0 and i is THIRD else i)
                    for e in range(2):
                        fetch(j, e, i, loaded[(U_EX[l] + 2 * j + e) % RING])

                SECOND, THIRD = 1, 2
                stage(0, THIRD)
                for i in (SECOND, THIRD):
                    stage(1, i)
                    stage(2, i)
                with sp.Fori(3, PAIRS) as i:
                    stage(0, i)
                    stage(1, i)
                    stage(2, i)
                by_expert = [x.rearrange("i e p k f -> (i e) p k f") for x in src]
                n_more = further(sp, l)
                with sp.Fori(0, MORE) as i:
                    with sp.If(n_more > i):
                        ids = [sp.value_load(plan[0:1, l, bass.ds(i * 2 + (1 + e), 1)], min_val=0, max_val=EXPERTS - 1)
                               for e in range(2)]
                        for j in range(3):
                            sp.wait_ge(used[j], i + PAIRS)
                            for e in range(2):
                                s = ring[(U_EX[l] + 2 * j + e) % RING]
                                sp.dma_start(s.rearrange("p (k f) -> p k f", f=src[j].shape[-1]), by_expert[j][ids[e]])\
                                  .then_inc(more_in[l], 16)
                return n_more

            freed = {}
            for j in range(3):
                for e in range(2):
                    freed[U_EX0 + 6 * (PAIRS - 1) + 2 * j + e] = (moe_s[0].gate, moe_s[0].up, moe_s[0].down)[j]
            for u in range(12):
                freed[mod_at(1, u)] = (mod_done, 12 + u + 1)
            for u in range(4):
                freed[U_WIN + u] = (u_pj, 4 * (u + 1))
                freed[U_WIN + 4 + u] = (v_pj, 2 * (u + 1))
                freed[U_WOUT + u] = (go_mm, u + 1)
            freed[U_WS] = (ws_tr, 4)

            n_more = experts(0)

            def space(n):
                if n - RING < U_MOD1:
                    sp.wait_ge(freed[n - RING], n_more + PAIRS)
                else:
                    sp.wait_ge(*freed[n - RING])

            def mod_weights(u):
                space(mod_at(1, u))
                unit(mod_at(1, u), A["w_mod"][1].rearrange("(k p) (u f) -> u p k f", p=P, f=512)[u])

            for u in range(EARLY):
                mod_weights(u)
            sp.dma_start(brow[:, 0, :], A["sg_b_in"][0, HALF:2 * HALF].partition_broadcast(P)).then_inc(gm_in, 16)
            sp.dma_start(brow[:, 1, :], A["sg_ln_g"][0].partition_broadcast(P)).then_inc(gm_in, 16)
            sp.dma_start(brow[:, 2, :], A["sg_ln_b"][0].partition_broadcast(P)).then_inc(gm_in, 16)
            sp.dma_start(bsrow[0:1, :], A["sg_b_s"][0].rearrange("(a g) i -> a (g i)", a=1)).then_inc(gm_in, 16)
            for u in range(8):
                space(U_WIN + u)
                unit(U_WIN + u, A["sg_w_in"][0].rearrange("(k p) (u f) -> u p k f", p=P, f=512)[u])
            space(U_WS)
            s = U_WS % RING
            sp.dma_start(ring[s][:, 0:VG * P].rearrange("p (g j) -> p g j", j=P),
                         A["sg_w_s"][0].rearrange("g i j -> i g j")).then_inc(loaded[s], 16)
            for u in range(EARLY, 12):
                mod_weights(u)
            for u in range(4):
                space(U_WOUT + u)
                unit(U_WOUT + u, A["sg_w_out"][0].rearrange("(u k p) f -> u p k f", p=P, k=4)[u])
            experts(1)
            sp.wait_ge(f_ev, 4)
            sp.dma_start(out[0].rearrange("(t p) d -> p t d", p=P), tok_out).then_inc(stored, 16)
            sp.wait_ge(stored, 16)

        @block.gpsimd
        def _(pool):
            pool.dma_start(wr, A["w_router"].rearrange("(k p) e -> p k e", p=P)).then_inc(small_in, 16)
            pool.dma_start(rbias, A["router_bias"].partition_broadcast(P)).then_inc(small_in, 16)

            made = [0]

            def make(ins):
                made[0] += 1
                ins.then_inc(cst, 1)
                pool.wait_ge(cst, made[0])

            make(pool.memset(ident, 0.0))
            make(pool.memset(ones, 1.0))
            for i, v in enumerate((1e-6, 64e-5, 1e-5)):
                make(pool.memset(epsc[:, i:i + 1], v))
            make(pool.memset(tie, 0.0))
            make(pool.memset(before, 1.0))
            make(pool.iota(iota, pattern=[[1, P]], base=0, channel_multiplier=0, allow_small_or_imprecise_dtypes=True))
            make(pool.affine_select(out=before, in_=before, compare_op=ALU.is_gt, fill=0.0, base=0,
                                    pattern=[[1, P]], channel_multiplier=-1))
            make(pool.affine_select(out=ident, in_=ident, compare_op=ALU.not_equal, fill=1.0, base=0,
                                    pattern=[[-1, P]], channel_multiplier=1))
            for i in range(1, 4):
                make(pool.memset(tie[:, 4 * i:4 * i + i], 1.0))
            CONSTS[0] = made[0]

            pool.wait_ge(mod_done, 12)
            make(pool.memset(hones, 0.0))
            make(pool.memset(merge_mask, 0.0))
            make(pool.memset(strict, 1.0))
            make(pool.memset(incl, 1.0))
            make(pool.memset(rksel, 0.0))
            for h in range(2):
                make(pool.memset(hones[64 * h:64 * h + 64, 64 * h:64 * h + 64], 1.0))
            for d, (step, cm) in enumerate(((1, -1), (-1, 1))):
                make(pool.affine_select(out=strict[:, d, :], in_=strict[:, d, :], compare_op=ALU.is_gt, fill=0.0,
                                        base=0, pattern=[[step, P]], channel_multiplier=cm))
                make(pool.affine_select(out=incl[:, d, :], in_=incl[:, d, :], compare_op=ALU.is_ge, fill=0.0,
                                        base=0, pattern=[[step, P]], channel_multiplier=cm))
            views = []
            for d in range(2):
                for i, m in enumerate([1] + LEVELS):
                    v = merge_mask[:, 7 * d + i, :].rearrange("p (b c) -> p b c", c=2 * m)
                    v = v[:, :, 0:m] if d == 0 else v[:, :, m:2 * m]
                    make(pool.memset(v, 1.0))
                    views.append((d, m, v))
            for d, m, v in views:
                first = m if d == 0 else 0
                make(pool.affine_select(out=v, in_=v, compare_op=ALU.is_ge, fill=0.0, base=-first,
                                        pattern=[[-2 * m, P // (2 * m)], [0, m]], channel_multiplier=1))
            for d, m, v in views:
                first = m if d == 0 else 0
                make(pool.affine_select(out=v, in_=v, compare_op=ALU.is_ge, fill=0.0, base=first + m - 1,
                                        pattern=[[2 * m, P // (2 * m)], [0, m]], channel_multiplier=-1))
            CONSTS.append(made[0])

        @block.scalar
        def _(act):
            at = 0
            for name, n in (("c", 8), ("c_ctx", 8), ("norm1_g", 16), ("norm2_g", 16), ("rw_w0", 16), ("rw_a0", 16),
                            ("rw_kk", 8), ("rw_ka", 8), ("rw_rk", 8), ("final_g", 8)):
                src = A[name]
                while len(src.shape) > 1:
                    src = src.rearrange("a b c -> (a b c)") if len(src.shape) == 3 else src.rearrange("a b -> (a b)")
                act.dma_start(prow[at:at + n, 0, :], src.rearrange("(r p) -> r p", p=P)).then_inc(rows_in, 16)
                at += n
            act.dma_start(prow[at:at + 16, 0, :], A["sg_b_in"][0, 0:HALF].rearrange("(r p) -> r p", p=P)).then_inc(rows_in, 16)
            act.dma_start(prow[0:96, 1, :], A["b_mod"].rearrange("l (r p) -> (l r) p", p=P)).then_inc(rows_in, 16)
            act.dma_start(prow[0:48, 2, :], A["rw_mu"][0].rearrange("j (r p) -> (j r) p", p=P)).then_inc(rows_in, 16)
            act.wait_ge(cst, CONSTS[0])
            act.wait_ge(c_T, 1)
            act.wait_ge(silc0, 1)
            act.activation(silc[:, :, 0], bank(4)[:, 0:8], ACT.Silu).then_inc(sil_ready, 1)
            act.activation(silc[:, :, 1], bank(4)[:, 8:16], ACT.Silu).then_inc(sil_ready, 1)

            def mod_rows(l, us):
                rows = (modrow0, modrow1)[l]
                for u in us:
                    act.wait_ge(mod_done, 12 * l + u + 1)
                    if u >= 2:
                        act.wait_ge(mod_cols, 12 * l + u - 1)
                    act.copy(rows[:, u % 2, :], bank(5 + u % 2)).then_inc(mod_row, 1)

            mod_rows(0, range(EARLY))
            act.wait_ge(rows_T, 3)
            for i in range(3):
                n = (P, 96, 48)[i]
                act.copy(cols[:, i, 0:n] if i < 2 else mus, bank(0)[:, P * i:P * i + n]).then_inc(cols_ready, 1)
            for b in range(8):
                act.wait_ge(x_T, 4 * b + 4)
                dst = xcT if b < 4 else xT
                act.copy(dst[:, 2 * (b % 4):2 * (b % 4) + 2, :], bank(b % 4).rearrange("p (a t) -> p a t", t=T)).then_inc(xT_ready, 1)

            def squares(q, src, sqb):
                for k in range(KT):
                    if q >= 2:
                        act.wait_ge(x_tile, 8 * (q - 2) + k + 1)
                    act.activation(sqb[:, k, :], src[:, k, :], ACT.Square).then_inc(n_sq, 1)

            def root(q, rsb):
                act.wait_ge(n_ss, q + 1)
                act.activation(rsb, bank(0)[:, 0:T], ACT.Sqrt, bias=epsc[:, 0:1], scale=1.0 / D).then_inc(n_rt, 1)

            def norm(q):
                squares(q, xT, sq)
                root(q, rs)

            def shifted(q, shift):
                for k in range(KT):
                    act.wait_ge(n_m, 8 * (q - 2) + k + 1)
                    act.activation(h2T[:, k, :], h2T[:, k, :], ACT.Identity, bias=shift[:, k:k + 1]).then_inc(n_h, 1)

            mod_rows(0, range(4, 5))
            act.wait_ge(xT_ready, 8)
            squares(0, xcT, sq0)
            root(0, rs0[0])
            mod_rows(0, range(5, 6))
            squares(1, xT, sq0)
            root(1, rs0[1])
            mod_rows(0, range(6, 7))
            act.wait_ge(mods_r, 2)
            act.wait_ge(n_div, 1)
            for k in range(KT):
                act.activation(hT[:, k, 0:T], hT[:, k, 0:T], ACT.Identity, bias=modc[:, 0, k:k + 1, 1],
                               scale=gs[:, 0, k:k + 1]).then_inc(n_h, 1)
            mod_rows(0, range(7, FIRST_MODS))

            def kk_root(m):
                act.wait_ge(kk_mx, m + 1)
                act.activation(kk_tmp[m % 2], kk_tmp[m % 2], ACT.Sqrt).then_inc(kk_rt, 1)

            for q in range(27):
                act.wait_ge(pj_mm, q + 1)
                src = bank(q % 7)
                if q == 24:
                    act.wait_ge(kk_ready, 1)
                if q < 8:
                    ins = act.copy(kT[:, q, :], src)
                elif q < 16:
                    hf, t = (q - 8) // 4, (q - 8) % 4
                    ins = act.copy(V[:, t, 512 * hf:512 * hf + 512], src)
                elif q < 24:
                    ins = act.copy(rT[:, q - 16, :], src[:, 0:T])
                elif q == 24:
                    ins = act.activation(tanw, src, ACT.Tanh)
                elif q == 25:
                    ins = act.copy(loa, src)
                else:
                    ins = act.activation(sigg, src[:, 0:T], ACT.Sigmoid)
                ins.then_inc(pj_ev, 1)
                if 1 <= q < 4:
                    mod_rows(0, range(q + 8, q + 9))
                if 9 <= q < 17:
                    kk_root(q - 9)

            def rates(n, m):
                d = STEPS[n][0]
                act.wait_ge(z_mm, 4 * n + m // 4 + 1)
                act.activation(icl[:, m, :], bank(5 + 2 * (m // 4))[:, P * (m % 4):P * (m % 4) + P], ACT.Sigmoid,
                               bias=a0_cols[d][:, m:m + 1]).then_inc(z_sig, 1)

            def decays(n, m):
                d = STEPS[n][0]
                act.wait_ge(z_mm, 4 * n + 2 + m // 4 + 1)
                if lat_before(n):
                    act.wait_ge(bon_mm, lat_before(n))
                act.activation(sig[:, m, :], bank(1 + 2 * (m // 4))[:, P * (m % 4):P * (m % 4) + P], ACT.Sigmoid,
                               bias=w0_cols[d][:, m:m + 1]).then_inc(z_sig, 1)

            def scales(n):
                act.wait_ge(lmid_r, 2 * n + 2)
                if n:
                    act.wait_ge(s_mid, n)
                act.activation(smid, lmid, ACT.Exp, scale=-DECAY).then_inc(e_r, 1)
                act.activation(send[n % 2], lend, ACT.Exp, scale=-DECAY).then_inc(e_r, 1)
                act.wait_ge(d0_r, n + 1)
                act.activation(E2, D1, ACT.Exp, scale=DECAY).then_inc(e_r, 1)
                act.activation(D0, D0, ACT.Exp, scale=-DECAY).then_inc(e_r, 1)
                act.wait_ge(e_r, 5 * n + 3)
                act.activation(D1, D1, ACT.Exp, scale=-DECAY).then_inc(e_r, 1)

            def y_root(t, count):
                act.wait_ge(var_r, count)
                act.activation(yr[:, HEADS * t:HEADS * t + HEADS], yv[:, HEADS * t:HEADS * t + HEADS], ACT.Sqrt).then_inc(sd_r, 1)

            for m in range(8):
                rates(0, m)
            for m in range(8):
                decays(0, m)
            scales(0)
            for n, (d, c) in enumerate(STEPS):
                more, last = n + 1 < len(STEPS), n % 4 == 3
                if not last:
                    for j, dst in enumerate((Btok, Btok, Ktok, Ktok)):
                        act.wait_ge(bk_T, 4 * handed_before(n) + j + 1)
                        act.copy(dst[:, 512 * (j % 2):512 * (j % 2) + 512], bank(4 + j)).then_inc(bk_tok, 1)
                act.wait_ge(w1_mm, 2 * n + 2)
                act.copy(W, psum[:, 0:1024]).then_inc(w1_ev, 1)
                if more:
                    for m in range(8):
                        rates(n + 1, m)
                for i in range(6):
                    for g in range(4):
                        act.wait_ge(tp_mm, 24 * n + 4 * i + g + 1)
                        dst = X if i == 0 else XT
                        act.copy(dst[:, 4 * g:4 * g + 4, :], bank(2 * g).rearrange("p (a b) -> p a b", b=P)).then_inc(tp_ev, 1)
                        if i == 0 and more:
                            decays(n + 1, 2 * g)
                            decays(n + 1, 2 * g + 1)
                    if i == 4:
                        if more:
                            scales(n + 1)
                        else:
                            y_root(1, 1)
                for hf in range(2):
                    act.wait_ge(u_mm, 2 * n + hf + 1)
                    act.copy(U[:, 512 * hf:512 * hf + 512], bank(2 + hf)).then_inc(u_ev, 1)

            act.wait_ge(g_mm, 4)
            act.copy(gT, psum[:, 2048:4096].rearrange("p (k t) -> p k t", t=T)).then_inc(g_ev, 1)
            y_root(0, 2)

            def router(l):
                act.wait_ge(lg_mm, l + 1)
                act.activation(route[:, 0:32], bank(1)[:, 0:32], ACT.Sigmoid).then_inc(sc_r, 1)
                for b in range(4):
                    act.wait_ge(ht_mm, 4 * l + b + 1)
                    act.copy(h2tok[:, b // 2, 512 * (b % 2):512 * (b % 2) + 512], bank(4 + b)).then_inc(ht_r, 1)

            def pair(Q, q):
                act.wait_ge(Q.gathered, q + 1)
                act.copy(xs, psum[:, 2048:3072].rearrange("p (k t) -> p k t", t=P)).then_inc(Q.staged, 1)
                act.wait_ge(Q.gate, q + 1)
                act.activation(sg, bank(4), ACT.Silu).then_inc(Q.silu, 1)
                act.wait_ge(Q.hidden_turned, q + 1)
                act.copy(heT, bank(6).rearrange("p (k t) -> p k t", t=P)).then_inc(Q.hidden_ready, 1)

            def moe(l):
                Q = moe_s[l]
                for b in range(4):
                    act.wait_ge(Q.turned, b + 1)
                    act.copy(giveT[:, 2 * b:2 * b + 2, :], bank(4 + b).rearrange("p (a t) -> p a t", t=T)).then_inc(Q.given, 1)
                with act.Fori(0, PAIRS) as i:
                    pair(Q, i)
                n_more = further(act, l)
                with act.Fori(0, MORE) as i:
                    with act.If(n_more > i):
                        act.wait_ge(Q.turned, i + 5)
                        act.copy(giveT[:, 0, :], bank(4)[:, 0:T]).then_inc(Q.given, 1)
                        pair(Q, i + PAIRS)

            norm(2)
            shifted(2, modc[:, 0, 24:32, 0])
            router(0)
            moe(0)
            mod_rows(1, range(EARLY))
            norm(3)
            act.wait_ge(mods_r, 4)
            shifted(3, modc[:, 1, 0:8, 0])
            for m in range(16):
                act.wait_ge(u_pj, m // 2 * 2 + 2)
                act.activation(uT[:, m, :], bank(m // 2)[:, T * (m % 2):T * (m % 2) + T], ACT.Gelu,
                               bias=bu_cols[:, m:m + 1]).then_inc(u_gl, 1)
            for q in range(8):
                u, t = q // 2, q % 2
                act.wait_ge(v_add, q + 1)
                act.activation(vtok[:, t, 512 * u:512 * u + 512], vtok[:, t, 512 * u:512 * u + 512], ACT.Gelu).then_inc(v_gl, 1)
            for b in range(4):
                act.wait_ge(ws_tr, b + 1)
                act.copy(wsT[:, 4 * b:4 * b + 4, :], bank(b).rearrange("p (a j) -> p a j", j=P)).then_inc(ws_ev, 1)
            act.wait_ge(v_ln0, 2)
            act.activation(rstd, mv[:, :, 1], ACT.Sqrt, bias=epsc[:, 2:3]).then_inc(v_sd, 1)
            mod_rows(1, range(EARLY, 12))
            norm(4)
            shifted(4, modc[:, 1, 24:32, 0])
            router(1)
            moe(1)
            norm(5)
            for j in range(2):
                act.wait_ge(f_T, j + 1)
                act.copy(tok_out[:, 0, 512 * j:512 * j + 512], psum[:, 1024 + 512 * j:1536 + 512 * j]).then_inc(f_ev, 1)

        @block.vector
        def _(dve):
            steps = [0]

            def link(ins):
                steps[0] += 1
                ins.then_inc(dst, 1)
                dve.wait_ge(dst, steps[0])

            def send_step(ins):
                steps[0] += 1
                ins.then_inc(dst, 1)

            def mods(l, tiles, norms, done):
                dve.wait_ge(mod_cols, 12 * l + tiles[1] // 4)
                dve.wait_ge(cols_ready, 3)
                at = slice(*tiles)
                link(dve.tensor_tensor(modc[:, l, at, :], bank(7)[:, 2 * tiles[0]:2 * tiles[1]].rearrange("p (a b) -> p a b", b=2),
                                       bc(bm_cols[l][:, at], 2, [P, tiles[1] - tiles[0], 2]), ALU.add))
                for i, scale, which, g in norms:
                    dve.scalar_tensor_tensor(out=gs[:, i, :], in0=modc[:, l, scale:scale + 8, which], scalar=1.0, in1=g,
                                             op0=ALU.add, op1=ALU.mult).then_inc(mods_r, 1)
                dve.wait_ge(mods_r, done)

            def normed(q, src, dest, rsb):
                dve.wait_ge(n_rt, q + 1)
                link(dve.reciprocal(rsb, rsb))
                dve.tensor_tensor(dest, src, bc(rsb, 1, [P, KT, T]), ALU.mult).then_inc(n_div, 1)

            def norm(q, scale):
                dve.wait_ge(n_rt, q + 1)
                link(dve.reciprocal(rs, rs))
                dve.wait_ge(x_tile, 8 * (q - 1))
                for k in range(KT):
                    dve.scalar_tensor_tensor(out=h2T[:, k, :], in0=xT[:, k, :], scalar=scale[:, k:k + 1], in1=rs,
                                             op0=ALU.mult, op1=ALU.mult).then_inc(n_m if q < 5 else n_h, 1)

            dve.memset(silc, 0.0).then_inc(silc0, 1)
            dve.wait_ge(cst, CONSTS[0])
            link(dve.tensor_reduce(modsel, ident.rearrange("p (j w) -> p w j", w=32)[:, 0:2, :], AX.X, ALU.add))
            mods(0, (0, 16), ((0, 8, 1, n1_cols[0]), (1, 8, 0, n1_cols[0])), 2)
            normed(0, xcT, hT[:, :, 0:T], rs0[0])
            normed(1, xT, hT[:, :, T:2 * T], rs0[1])
            dve.wait_ge(n_div, 2)
            for k in range(KT):
                dve.tensor_scalar(hT[:, k, T:2 * T], hT[:, k, T:2 * T], gs[:, 1, k:k + 1], modc[:, 0, k:k + 1, 0],
                                  ALU.mult, ALU.add).then_inc(n_h, 1)
            dve.wait_ge(n_h, 16)

            H, Hh = hT, KT // 2
            for a, b, to, fr, edge in ((0, Hh, slice(1, T), slice(0, T - 1), slice(0, 1)),
                                       (Hh, KT, slice(0, T - 1), slice(1, T), slice(T - 1, T))):
                send_step(dve.tensor_tensor(xx[:, a:b, to], H[:, a:b, fr], H[:, a:b, to], ALU.subtract))
                send_step(dve.tensor_scalar(xx[:, a:b, edge], H[:, a:b, edge], -1.0, None, ALU.mult))
            for qd in range(4):
                for k in range(2 * qd, 2 * qd + 2):
                    hl, xl = H[:, k, T:2 * T], xx[:, k, T:2 * T]
                    if qd < 2:
                        g = lambda v: v.rearrange("p (r c) -> p r c", c=GRID_W)
                        to, fr = (slice(1, GRID_W), slice(0, GRID_W - 1))[::1 if qd == 0 else -1]
                        edge = slice(0, 1) if qd == 0 else slice(GRID_W - 1, GRID_W)
                        send_step(dve.tensor_tensor(g(xl)[:, :, to], g(hl)[:, :, fr], g(hl)[:, :, to], ALU.subtract))
                        send_step(dve.tensor_scalar(g(xl)[:, :, edge], g(hl)[:, :, edge], -1.0, None, ALU.mult))
                    else:
                        to, fr = (slice(GRID_W, T), slice(0, T - GRID_W))[::1 if qd == 2 else -1]
                        edge = slice(0, GRID_W) if qd == 2 else slice(T - GRID_W, T)
                        send_step(dve.tensor_tensor(xl[:, to], hl[:, fr], hl[:, to], ALU.subtract))
                        send_step(dve.tensor_scalar(xl[:, edge], hl[:, edge], -1.0, None, ALU.mult))
            dve.wait_ge(dst, steps[0])

            def kk_norms():
                dve.wait_ge(pj_ev, 8)
                dve.wait_ge(cst, CONSTS[1])
                for m in range(KT):
                    dve.tensor_scalar(kkT[:, m, :], kT[:, m, :], kk_cols[:, m:m + 1], None, ALU.mult).then_inc(kk_raw, 1)
                dve.wait_ge(kk_raw, 8)

                def squares(m):
                    dve.tensor_tensor(kk_tmp[m % 2], kkT[:, m, :], kkT[:, m, :], ALU.mult).then_inc(kk_sq, 1)

                squares(0)
                squares(1)
                for m in range(KT):
                    tmp = kk_tmp[m % 2]
                    dve.wait_ge(kk_ss, m + 1)
                    dve.tensor_scalar(tmp, bank(7), 1e-24, None, ALU.max).then_inc(kk_mx, 1)
                    dve.wait_ge(kk_rt, m + 1)
                    link(dve.reciprocal(tmp, tmp))
                    link(dve.tensor_tensor(kkT[:, m, :], kkT[:, m, :], tmp, ALU.mult))
                    if m + 2 < KT:
                        squares(m + 2)
                link(dve.tensor_scalar(omka, ka_cols, -1.0, 1.0, ALU.mult, ALU.add))
                for h in range(2):
                    link(dve.tensor_copy(rksel[64 * h:64 * h + 64, :, h], rk_cols[64 * h:64 * h + 64, :]))
                dve.memset(bonus, 0.0).then_inc(kk_ready, 1)
                dve.wait_ge(kk_ready, 1)

            read_by = (8, 16, 24, 25, 26, 27)
            for i, j in enumerate((2, 3, 0, 1, 4, 5)):
                if i == 2:
                    mods(0, (16, 48), ((2, 32, 0, n2_cols[0]),), 3)
                if i == 3:
                    kk_norms()
                if i >= 2:
                    dve.wait_ge(pj_mm, read_by[i - 2])
                lo = T if j in (0, 5) else 0
                for k in range(KT):
                    dve.scalar_tensor_tensor(out=xj[i % 2][:, k, lo:2 * T], in0=xx[:, k, lo:2 * T],
                                             scalar=mu_cols[j][:, k:k + 1], in1=H[:, k, lo:2 * T],
                                             op0=ALU.mult, op1=ALU.add).then_inc(xj_ready, 1)

            def y_norm(t, part):
                hd = slice(HEADS * t, HEADS * t + HEADS)
                by_head = lambda v: v.rearrange("p (h c) -> p h c", c=HS)
                Y, Yh, Yq = Yacc[:, t, :], by_head(Yacc[:, t, :]), by_head(ysq[:, t, :])
                dve.wait_ge(dst, steps[0])
                if part == 0:
                    dve.wait_ge(y_ev, 4 - t)
                    link(dve.tensor_reduce(ym[:, hd], Yh, AX.X, ALU.add))
                    link(dve.tensor_scalar(ym[:, hd], ym[:, hd], 1.0 / HS, None, ALU.mult))
                    send_step(dve.tensor_tensor(Yh, Yh, bc(ym[:, hd], 2, [P, HEADS, HS]), ALU.subtract))
                elif part == 1:
                    link(dve.tensor_tensor(Yq, Yh, Yh, ALU.mult))
                    send_step(dve.tensor_reduce(yv[:, hd], Yq, AX.X, ALU.add))
                elif part == 2:
                    dve.tensor_scalar(yv[:, hd], yv[:, hd], 1.0 / HS, 64e-5, ALU.mult, ALU.add).then_inc(var_r, 1)
                elif part == 3:
                    dve.wait_ge(sd_r, 2 - t)
                    link(dve.reciprocal(yr[:, hd], yr[:, hd]))
                    send_step(dve.tensor_tensor(Yh, Yh, bc(yr[:, hd], 2, [P, HEADS, HS]), ALU.mult))
                else:
                    link(dve.tensor_tensor(Y, Y, lng, ALU.mult))
                    dve.tensor_tensor(Y, Y, yb[t], ALU.add).then_inc(y_r, 1)

            def y_bonus(t):
                dve.wait_ge(til_r, 8)
                dve.wait_ge(bon_ev, 4 - t)
                dve.wait_ge(ln_in, 32)
                link(dve.tensor_tensor(yb[t].rearrange("p (h c) -> p h c", c=HS), V[:, 2 + t, :].rearrange("p (h c) -> p h c", c=HS),
                                       bc(bonus[:, t, :], 2, [P, HEADS, HS]), ALU.mult))
                send_step(dve.tensor_tensor(yb[t], yb[t], lnb, ALU.add))

            def prepare(n, part):
                d, c = STEPS[n]
                lat, nl, tok = c >= 2, lat_before(n), slice(P * c, P * c + P)
                if part == 0:
                    dve.wait_ge(z_sig, 16 * n + 16)
                    rev = slice(None, None, -1) if d else slice(None)
                    for m in range(KT):
                        send_step(dve.tensor_tensor_scan(D1[:, m, rev], ones[:, rev], sig[:, m, rev], 0.0, ALU.mult, ALU.add))
                elif part == 1:
                    dve.wait_ge(dst, steps[0])
                    mid, end = P // 2, (P - 1 if d == 0 else 0)
                    dve.tensor_copy(lmid, D1[:, :, mid]).then_inc(lmid_r, 1)
                    dve.tensor_tensor(lend, D1[:, :, end], D1[:, :, mid], ALU.subtract).then_inc(lmid_r, 1)
                    dve.wait_ge(lmid_r, 2 * n + 2)
                    send_step(dve.tensor_tensor(D1, D1, bc(lmid, 2, [P, KT, P]), ALU.subtract))
                elif part == 2:
                    dve.wait_ge(dst, steps[0])
                    dve.tensor_tensor(D0, D1, sig, ALU.subtract).then_inc(d0_r, 1)
                    send_step(dve.tensor_tensor(BT, kkT[:, :, tok], icl, ALU.mult))
                elif part == 3:
                    for m in range(KT):
                        send_step(dve.tensor_scalar(KTl[:, m, :], icl[:, m, :], ka_cols[:, m:m + 1], omka[:, m:m + 1], ALU.mult, ALU.add))
                    dve.wait_ge(dst, steps[0])
                    send_step(dve.tensor_tensor(KTl, KTl, kT[:, :, tok], ALU.mult))
                elif part == 4:
                    dve.wait_ge(dst, steps[0])
                    if lat:
                        dve.wait_ge(d0_r, n + 1)
                        dve.tensor_tensor(sig, KTl, rT[:, :, P * (c - 2):P * (c - 1)], ALU.mult).then_inc(prod_r, 1)
                else:
                    dve.wait_ge(dst, steps[0])
                    dve.wait_ge(e_r, 5 * n + 5)
                    send_step(dve.scalar_tensor_tensor(out=AT, in0=kkT[:, :, tok], scalar=-1.0, in1=D0, op0=ALU.mult, op1=ALU.mult))
                    send_step(dve.tensor_tensor(BT, BT, E2, ALU.mult))
                    if lat:
                        send_step(dve.tensor_tensor(RT, rT[:, :, P * (c - 2):P * (c - 1)], D1, ALU.mult))
                        dve.wait_ge(prod_r, nl + 1)
                    dve.wait_ge(dst, steps[0])
                    dve.tensor_tensor(KTl, KTl, E2, ALU.mult).then_inc(til_r, 1)

            for part in range(6):
                prepare(0, part)
            for n, (d, c) in enumerate(STEPS):
                lat, last, first = c >= 2, n % 4 == 3, n % 4 == 0
                more = n + 1 < len(STEPS)
                nl, ns = lat_before(n), handed_before(n)
                dve.wait_ge(e_r, 5 * n + 2)
                if first:
                    dve.memset(S, 0.0).then_inc(s_mid, 1)
                else:
                    dve.tensor_tensor(S, S, bc(smid, 2, [P, KT, P]), ALU.mult).then_inc(s_mid, 1)

                def masked(dest, b, mask, q):
                    dve.wait_ge(pr_mm, q)
                    dve.tensor_tensor(dest, bank(b).rearrange("p (a t) -> p a t", t=P), bc(mask, 1, [P, 4, P]), ALU.mult).then_inc(pr_ev, 1)

                base = 8 * n + 8 * nl
                for g in range(4):
                    masked(buf1[:, 4 * g:4 * g + 4, :], g, strict[:, d, :], base + g + 1)
                if lat:
                    for g in range(4):
                        masked(buf2[:, 4 * g:4 * g + 4, :], 4 + g, incl[:, d, :], base + 4 + g + 1)
                    dve.wait_ge(y1_mm, 2 * nl + 2)
                    if d == 0:
                        dve.tensor_copy(Yacc[:, c - 2, :], psum[:, 1024:2048]).then_inc(y1_ev, 1)
                    else:
                        dve.tensor_tensor(Yacc[:, c - 2, :], Yacc[:, c - 2, :], psum[:, 1024:2048], ALU.add).then_inc(y1_ev, 1)
                base += 8 if lat else 4
                for g in range(4):
                    masked(buf1[:, 4 * g:4 * g + 4, :], 4 + g, strict[:, d, :], base + g + 1)
                if lat:
                    for g in range(4):
                        masked(buf2[:, 4 * g:4 * g + 4, :], g, incl[:, d, :], base + 4 + g + 1)
                base_nt = base
                for g in range(4):
                    hd = slice(4 * g, 4 * g + 4)
                    dve.wait_ge(pr_ev, base_nt + g + 1)
                    link(dve.tensor_tensor(XT[:, hd, :], buf1[:, hd, :], bc(merge_mask[:, 7 * (1 - d), :], 1, [P, 4, P]), ALU.mult))
                    dve.tensor_tensor(XT[:, hd, :], XT[:, hd, :], bc(ident, 1, [P, 4, P]), ALU.add).then_inc(xt2_r, 1)
                if lat:
                    dve.wait_ge(bon_mm, nl + 1)
                    dve.tensor_tensor(bonus[:, c - 2, :], bonus[:, c - 2, :], bank(6)[:, 0:16], ALU.add).then_inc(bon_ev, 1)
                for l in range(5):
                    for g in range(4):
                        hd = slice(4 * g, 4 * g + 4)
                        dve.wait_ge(t1_mm, 24 * n + 4 * l + g + 1)
                        dve.tensor_tensor(T1[:, hd, :], bank(2 * g).rearrange("p (a t) -> p a t", t=P),
                                          bc(merge_mask[:, 7 * d + 1 + l, :], 1, [P, 4, P]), ALU.mult).then_inc(t1_ev, 1)
                    for g in range(4):
                        hd = slice(4 * g, 4 * g + 4)
                        dve.wait_ge(x_mm, 24 * n + 4 * l + g + 1)
                        if l == 0:
                            dve.wait_ge(tp_ev, 24 * n + g + 1)
                        dve.tensor_tensor(X[:, hd, :], X[:, hd, :], bank(2 * g + 1).rearrange("p (a t) -> p a t", t=P), ALU.add).then_inc(x_ev, 1)
                    if more:
                        prepare(n + 1, l)
                    elif l < 3:
                        y_norm(1, l)
                    else:
                        y_bonus(l - 3)
                pre, post = halves(d)
                for g in range(4):
                    hd = slice(4 * g, 4 * g + 4)
                    dve.wait_ge(t1_mm, 24 * n + 20 + g + 1)
                    dve.tensor_copy(T1[post, hd, pre], bank(2 * g)[post, :].rearrange("p (a t) -> p a t", t=P)[:, :, pre]).then_inc(t1_ev, 1)
                for g in range(4):
                    hd = slice(4 * g, 4 * g + 4)
                    dve.wait_ge(x_mm, 24 * n + 20 + g + 1)
                    dve.wait_ge(tp_ev, 24 * n + 20 + g + 1)
                    dve.tensor_tensor(XT[pre, hd, post], XT[pre, hd, post],
                                      bank(2 * g + 1)[pre, :].rearrange("p (a t) -> p a t", t=P)[:, :, post], ALU.add).then_inc(x_ev, 1)
                if more:
                    prepare(n + 1, 5)
                else:
                    y_norm(1, 3)
                    y_norm(1, 4)
                if not last:
                    tmp = Btok.rearrange("p (k t) -> p k t", t=P)
                    dve.wait_ge(s_mm, 2 * ns + 2)
                    dve.wait_ge(s_mid, n + 1)
                    link(dve.tensor_tensor(tmp, psum[:, 3072:4096].rearrange("p (k t) -> p k t", t=P),
                                           bc(hones, 1, [P, KT, P]), ALU.mult))
                    link(dve.tensor_tensor(tmp, tmp, S, ALU.add))
                    dve.tensor_tensor(S, tmp, bc(send[n % 2], 2, [P, KT, P]), ALU.mult).then_inc(s_ev, 1)
                    dve.wait_ge(s_ev, ns + 1)
                if lat:
                    dve.wait_ge(y_mm, 2 * nl + 2)
                    dve.wait_ge(y1_ev, nl + 1)
                    dve.tensor_tensor(Yacc[:, c - 2, :], Yacc[:, c - 2, :], psum[:, 2048:3072], ALU.add).then_inc(y_ev, 1)

            for part in range(5):
                y_norm(0, part)
            for b in range(4):
                dve.wait_ge(y_T, b + 1)
                dve.wait_ge(g_ev, 1)
                dve.tensor_tensor(ygT[:, 2 * b:2 * b + 2, :], bank(b).rearrange("p (a t) -> p a t", t=T),
                                  gT[:, 2 * b:2 * b + 2, :], ALU.mult).then_inc(yg_r, 1)

            def residual(src, gate, s, q0, done):
                for m in range(KT):
                    dve.wait_ge(s, q0 + (m // 2 * 2 + 2 if done else 1))
                    dve.scalar_tensor_tensor(out=xT[:, m, :], in0=src(m), scalar=gate[:, m:m + 1], in1=xT[:, m, :],
                                             op0=ALU.mult, op1=ALU.add).then_inc(x_tile, 1)

            halfbank = lambda b0: (lambda m: bank(b0 + m // 2)[:, T * (m % 2):T * (m % 2) + T])
            residual(halfbank(4), modc[:, 0, 16:24, 0], o_mm, 0, True)

            def router(l):
                dve.wait_ge(small_in, 32)
                dve.wait_ge(sc_r, l + 1)
                dve.wait_ge(cst, CONSTS[0])
                R = route
                M, wts = R[:, 384:416], R[:, 416:448]
                sc3 = R[:, 0:32].rearrange("p (t e) -> p t e", e=16)
                b = R[:, 32:64]
                b3 = b.rearrange("p (t e) -> p t e", e=16)
                v = b.rearrange("p (g e) -> p g e", e=4)
                hi, lo = R[:, 64:80].rearrange("p (g e) -> p g e", e=2), R[:, 80:96].rearrange("p (g e) -> p g e", e=2)
                top, sec, gsc = R[:, 96:104], R[:, 104:112], R[:, 112:120]
                link(dve.tensor_tensor(b3, sc3, bc(rbias, 1, [P, 2, 16]), ALU.add))
                send_step(dve.tensor_tensor(hi, v[:, :, 0:2], v[:, :, 2:4], ALU.max))
                link(dve.tensor_tensor(lo, v[:, :, 0:2], v[:, :, 2:4], ALU.min))
                send_step(dve.tensor_tensor(top, hi[:, :, 0], hi[:, :, 1], ALU.max))
                send_step(dve.tensor_tensor(sec, hi[:, :, 0], hi[:, :, 1], ALU.min))
                link(dve.tensor_tensor(gsc, lo[:, :, 0], lo[:, :, 1], ALU.max))
                link(dve.tensor_tensor(sec, sec, gsc, ALU.max))
                link(dve.tensor_tensor(gsc, top, sec, ALU.add))

                def chosen(val, groups, few, dest):
                    n = groups
                    one = R[:, 128:128 + 16 * n].rearrange("p (g i j) -> p g i j", i=4, j=4)
                    two = R[:, 256:256 + 16 * n].rearrange("p (g i j) -> p g i j", i=4, j=4)
                    vj, vi = bc(val, 2, [P, n, 4, 4]), bc(val, 3, [P, n, 4, 4])
                    send_step(dve.tensor_tensor(one, vj, vi, ALU.is_gt))
                    link(dve.tensor_tensor(two, vj, vi, ALU.is_equal))
                    flat = two.rearrange("p g i j -> p g (i j)")
                    link(dve.tensor_tensor(flat, flat, bc(tie, 1, [P, n, 16]), ALU.mult))
                    link(dve.tensor_tensor(one, one, two, ALU.add))
                    link(dve.tensor_reduce(dest, one, AX.X, ALU.add))
                    link(dve.tensor_scalar(dest, dest, few - 0.5, None, ALU.is_lt))

                sel_e = M.rearrange("p (g e) -> p g e", e=4)
                sel_g = R[:, 96:104].rearrange("p (t g) -> p t g", g=4)
                chosen(gsc.rearrange("p (t g) -> p t g", g=4), 2, 1, sel_g)
                chosen(v, 8, 2, sel_e)
                dve.tensor_tensor(sel_e, sel_e, bc(R[:, 96:104], 2, [P, 8, 4]), ALU.mult).then_inc(m_r, 1)
                dve.wait_ge(m_r, l + 1)
                w3, rk = wts.rearrange("p (t e) -> p t e", e=16), R[:, 448:480]
                link(dve.tensor_tensor(wts, M, R[:, 0:32], ALU.mult))
                link(dve.tensor_reduce(R[:, 104:106], w3, AX.X, ALU.add))
                link(dve.reciprocal(R[:, 106:108], R[:, 104:106]))
                link(dve.tensor_tensor(w3, w3, bc(R[:, 106:108], 2, [P, 2, 16]), ALU.mult))
                dve.wait_ge(rank_mm, l + 1)
                Rk = R[:, 128:160]
                link(dve.tensor_copy(R[:, 128:176], bank(3)[:, 0:48]))
                link(dve.scalar_tensor_tensor(out=rk, in0=Rk, scalar=1.0, in1=M, op0=ALU.add, op1=ALU.mult))
                link(dve.tensor_scalar(rk, rk, -1.0, None, ALU.add))

            def plan_further(l):
                R = route
                M, wts = R[:, 384:416], R[:, 416:448]
                Rk, cnt, extra, cum = R[:, 128:160], R[:, 160:176], R[:, 176:192], R[:, 192:208]
                link(dve.tensor_scalar(extra, cnt, float(SLOTS), None, ALU.is_gt))
                for n in range(2 * SLOTS, T, SLOTS):
                    link(dve.scalar_tensor_tensor(out=extra, in0=cnt, scalar=float(n), in1=extra, op0=ALU.is_gt, op1=ALU.add))
                link(dve.tensor_tensor_scan(cum, ones[:, 0:16], extra, 0.0, ALU.mult, ALU.add))
                four, lots = R[:, 208:212], R[:, 212:220]
                link(dve.tensor_tensor(four, cum[:, 15:16].broadcast_to([P, MORE]), iota[:, 0:2 * MORE:2], ALU.is_gt))
                link(dve.tensor_reduce(R[:, 220:221], four, AX.X, ALU.add))
                by_lot = R[:, 256:384].rearrange("p (v e) -> p v e", e=EXPERTS)
                link(dve.tensor_tensor(by_lot, bc(cum, 1, [P, 2 * MORE, EXPERTS]), bc(iota[:, 0:2 * MORE], 2, [P, 2 * MORE, EXPERTS]), ALU.is_le))
                link(dve.tensor_reduce(lots, by_lot, AX.X, ALU.add))
                link(dve.tensor_scalar(lots, lots, float(EXPERTS - 1), None, ALU.min))
                dve.tensor_copy(plan[:, l, 0:1], R[:, 220:221]).then_inc(plan_r, 1)
                dve.tensor_copy(plan[:, l, 1:9], lots).then_inc(plan_r, 1)
                start, past = R[:, 160:176], R[:, 224:256]
                far = Rk.rearrange("p (t e) -> p t e", e=16)
                link(dve.tensor_tensor(start, cum, extra, ALU.subtract))
                link(dve.tensor_scalar(start, start, float(SLOTS), 1.0 - SLOTS, ALU.mult, ALU.add))
                link(dve.tensor_scalar(past, Rk, SLOTS - 0.5, None, ALU.is_gt))
                link(dve.tensor_tensor(past, past, M, ALU.mult))
                link(dve.tensor_tensor(far, far, bc(start, 1, [P, 2, 16]), ALU.add))
                link(dve.tensor_tensor(Rk, Rk, past, ALU.mult))
                placeA, placeB, gateA, gateB = R[:, 480:482], R[:, 482:484], R[:, 484:486], R[:, 486:488]
                link(dve.tensor_reduce(placeA, far, AX.X, ALU.max))
                link(dve.tensor_reduce(placeB, far, AX.X, ALU.add))
                link(dve.tensor_tensor(placeB, placeB, placeA, ALU.subtract))
                for pl, gt in ((placeA, gateA), (placeB, gateB)):
                    p3 = past.rearrange("p (t e) -> p t e", e=16)
                    link(dve.tensor_tensor(p3, far, bc(pl, 2, [P, 2, 16]), ALU.is_equal))
                    link(dve.tensor_tensor(past, past, wts, ALU.mult))
                    link(dve.tensor_reduce(gt, p3, AX.X, ALU.add))
                link(dve.tensor_scalar(R[:, 480:484], R[:, 480:484], -1.0, None, ALU.add))

            def choose(Q):
                rk, wts = route[:, 448:480], route[:, 416:448]
                for t in range(NT):
                    e_s = lambda v: v[:, t, :].rearrange("p (e s) -> p e s", s=SLOTS)
                    dve.tensor_tensor(e_s(pick), bc(rk[:, 16 * t:16 * t + 16], 2, [P, EXPERTS, SLOTS]),
                                      bc(iota[:, 0:SLOTS], 1, [P, EXPERTS, SLOTS]), ALU.is_equal).then_inc(Q.picked, 1)
                    dve.wait_ge(Q.picked, 2 * t + 1)
                    dve.tensor_tensor(e_s(gpick), e_s(pick), bc(wts[:, 16 * t:16 * t + 16], 2, [P, EXPERTS, SLOTS]),
                                      ALU.mult).then_inc(Q.picked, 1)

            def choose_further(Q, i):
                place, gate = [route[:, 480 + 2 * x:482 + 2 * x] for x in range(2)], [route[:, 484 + 2 * x:486 + 2 * x] for x in range(2)]
                done = 4

                def then(ins):
                    nonlocal done
                    done += 1
                    ins.then_inc(Q.picked, 1)
                    dve.wait_ge(Q.picked, i * 11 + done)

                for t in range(NT):
                    A_, B_ = place[0][:, t:t + 1], place[1][:, t:t + 1]
                    p1, g1, g2 = pick[:, t, 0:P], gpick[:, t, 0:P], gpick[:, t, P:2 * P]
                    then(dve.tensor_scalar(p1, iota, A_, None, ALU.is_equal))
                    then(dve.scalar_tensor_tensor(out=p1, in0=iota, scalar=B_, in1=p1, op0=ALU.is_equal, op1=ALU.add))
                    then(dve.tensor_scalar(g1, iota, A_, gate[0][:, t:t + 1], ALU.is_equal, ALU.mult))
                    then(dve.tensor_scalar(g2, iota, B_, gate[1][:, t:t + 1], ALU.is_equal, ALU.mult))
                    then(dve.tensor_tensor(g1, g1, g2, ALU.add))
                then(dve.tensor_scalar(route[:, 480:484], route[:, 480:484], -float(P), None, ALU.add))

            def pair(Q, q):
                dve.wait_ge(Q.silu, q + 1)
                dve.wait_ge(Q.up, q + 1)
                dve.tensor_tensor(he, sg, bank(5), ALU.mult).then_inc(Q.hidden, 1)
                dve.wait_ge(Q.down, q + 1)
                dve.tensor_copy(ye, psum[:, 3072:4096]).then_inc(Q.out, 1)

            def moe(l):
                Q = moe_s[l]
                choose(Q)
                plan_further(l)
                with dve.Fori(0, PAIRS) as i:
                    pair(Q, i)
                n_more = further(dve, l)
                with dve.Fori(0, MORE) as i:
                    with dve.If(n_more > i):
                        choose_further(Q, i)
                        pair(Q, i + PAIRS)
                for m in range(KT):
                    dve.wait_ge(Q.scattered, n_more + PAIRS)
                    dve.scalar_tensor_tensor(out=xT[:, m, :], in0=halfbank(0)(m), scalar=modc[:, l, 40 + m:41 + m, 0], in1=xT[:, m, :],
                                             op0=ALU.mult, op1=ALU.add).then_inc(x_tile, 1)

            norm(2, gs[:, 2, :])
            router(0)
            moe(0)
            mods(1, (0, 16), ((3, 8, 0, n1_cols[1]),), 4)
            norm(3, gs[:, 3, :])
            dve.wait_ge(gm_in, 64)
            for q in range(8):
                u, t = q // 2, q % 2
                dve.wait_ge(v_pj, q + 1)
                dve.tensor_tensor(vtok[:, t, 512 * u:512 * u + 512], bank(q), brow[:, 0, 512 * u:512 * u + 512], ALU.add).then_inc(v_add, 1)
            for t in range(2):
                for u in range(4):
                    dve.wait_ge(v_gl, 2 * u + t + 1)
                    send_step(dve.bn_stats(stat[:, t, u, :], vtok[:, t, 512 * u:512 * u + 512]))
                dve.wait_ge(dst, steps[0])
                dve.bn_aggr(mv[:, t, :], stat[:, t, :, :]).then_inc(v_ln0, 1)
            dve.wait_ge(v_sd, 1)
            dve.wait_ge(v_ln0, 2)
            link(dve.reciprocal(rstd, rstd))
            for t in range(2):
                link(dve.tensor_scalar(vtok[:, t, :], vtok[:, t, :], mv[:, t, 0:1], rstd[:, t:t + 1], ALU.subtract, ALU.mult))
                link(dve.tensor_tensor(vtok[:, t, :], vtok[:, t, :], brow[:, 1, :], ALU.mult))
                dve.tensor_tensor(vtok[:, t, :], vtok[:, t, :], brow[:, 2, :], ALU.add).then_inc(v_ln, 1)
            mods(1, (16, 48), ((4, 32, 0, n2_cols[1]),), 5)
            for g in range(VG):
                dve.wait_ge(sp_mm, g // 2 * 2 + 2)
                dve.wait_ge(u_gl, g + 1)
                dve.tensor_tensor(uT[:, g, :], uT[:, g, :], bank(4 + g // 2 % 4)[:, T * (g % 2):T * (g % 2) + T], ALU.mult).then_inc(sp_ev, 1)
            residual(halfbank(0), modc[:, 1, 16:24, 0], go_mm, 3, False)
            norm(4, gs[:, 4, :])
            router(1)
            moe(1)
            norm(5, fin_cols)
            for j in range(2):
                dve.wait_ge(f_T, j + 1)
                dve.tensor_copy(tok_out[:, 1, 512 * j:512 * j + 512], psum[:, 2048 + 512 * j:2560 + 512 * j]).then_inc(f_ev, 1)

        @block.tensor
        def _(pe):
            def product(dest, lhs, rhs, k):
                for i in range(k):
                    mm = pe.matmul(dest, lhs(i), rhs(i), start=(i == 0), stop=(i == k - 1))
                return mm

            def mod_unit(l, u):
                n = mod_at(l, u)
                landed(pe, n)
                if u >= 2:
                    pe.wait_ge(mod_row, 12 * l + u - 1)
                for k in range(KT):
                    at = slice(32 * (k % 4), 32 * (k % 4) + 32)
                    mm = pe.matmul(bank(5 + u % 2)[at, :], silc[:, k, :], ring[n % RING][:, 512 * k:512 * k + 512],
                                   start=(k < 4), stop=(k >= 4))
                mm.then_inc(mod_done, 1)

            def mod_turn(l, u):
                pe.wait_ge(mod_row, 12 * l + u + 1)
                for m in range(4):
                    j = 4 * u + m
                    mm = pe.matmul(bank(7)[:, 2 * j:2 * j + 2], (modrow0, modrow1)[l][:, u % 2, P * m:P * m + P], modsel,
                                   start=True, stop=True)
                mm.then_inc(mod_cols, 1)

            pe.wait_ge(cst, CONSTS[0])

            def norm(q, sqb):
                for k in range(KT):
                    pe.wait_ge(n_sq, 8 * q + max(k + 1, 2))
                    mm = pe.matmul(bank(0)[:, 0:T], ones, sqb[:, k, :], start=(k == 0), stop=(k == KT - 1))
                mm.then_inc(n_ss, 1)

            pe.wait_ge(c_in, 32)
            pe.transpose(bank(4)[:, 0:16], crow, ident[0:16, 0:16]).then_inc(c_T, 1)
            pe.wait_ge(sil_ready, 2)
            pe.wait_ge(dst, 1)
            for u in range(EARLY):
                mod_unit(0, u)
                if u:
                    mod_turn(0, u - 1)
            mod_turn(0, EARLY - 1)
            pe.wait_ge(rows_in, 16 * 13)
            for i in range(3):
                n = (P, 96, 48)[i]
                pe.transpose(bank(0)[:, P * i:P * i + n], prow[0:n, i, :], ident[0:n, 0:n]).then_inc(rows_T, 1)
            pe.wait_ge(cols_ready, 3)
            pe.wait_ge(x_in, 32)
            for b in range(8):
                if b >= 4:
                    pe.wait_ge(xT_ready, b - 3)
                for a in range(2):
                    for t in range(2):
                        k = 2 * (b % 4) + a
                        pe.transpose(bank(b % 4)[:, T * a + P * t:T * a + P * t + P],
                                     xtok[:, 2 * (b // 4) + t, P * k:P * k + P], ident).then_inc(x_T, 1)
            mod_unit(0, 4)
            pe.wait_ge(xT_ready, 8)
            norm(0, sq0)
            pe.wait_ge(mods_r, 2)
            mod_turn(0, 4)
            mod_unit(0, 5)
            pe.wait_ge(n_rt, 1)
            norm(1, sq0)
            for u in range(6, FIRST_MODS):
                mod_turn(0, u - 1)
                mod_unit(0, u)
            pe.wait_ge(n_rt, 2)

            def modulation1(us):
                for u in us:
                    mod_unit(1, u)
                    if u > us[0]:
                        mod_turn(1, u - 1)
                mod_turn(1, us[-1])

            def slot(n):
                pe.wait_ge(pslot[n % 2], 16 * (n // 2 + 1))
                return slots2[n % 2].rearrange("p (k f) -> p k f", f=512)

            def kk_sum(m):
                pe.wait_ge(kk_sq, m + 1)
                if m == 0:
                    pe.wait_ge(mods_r, 3)
                if m:
                    pe.wait_ge(kk_mx, m)
                pe.matmul(bank(7), hones, kk_tmp[m % 2], start=True, stop=True).then_inc(kk_ss, 1)

            q = 0
            for m in range(8):
                if m % 4 == 0:
                    w = slot(m // 4)
                if q >= 7:
                    pe.wait_ge(pj_ev, q - 6)
                for k in range(KT):
                    if m == 0:
                        pe.wait_ge(xj_ready, k + 1)
                    mm = pe.matmul(bank(q % 7), w[:, k, P * (m % 4):P * (m % 4) + P], xj[0][:, k, :], start=(k == 0), stop=(k == KT - 1))
                mm.then_inc(pj_mm, 1)
                if 1 <= m < 4:
                    mod_turn(0, FIRST_MODS - 2 + m)
                    mod_unit(0, FIRST_MODS - 1 + m)
                if m == 3:
                    mod_turn(0, 11)
                q += 1
            pe.wait_ge(xj_ready, 16)
            for hf in range(2):
                w = slot(2 + hf)
                for t in range(4):
                    pe.wait_ge(pj_ev, q - 6)
                    product(bank(q % 7), lambda k: xj[1][:, k, P * t:P * t + P], lambda k: w[:, k, :], KT).then_inc(pj_mm, 1)
                    q += 1
                    kk_sum(q - 9)
            pe.wait_ge(xj_ready, 24)
            for m in range(8):
                if m % 4 == 0:
                    w = slot(4 + m // 4)
                pe.wait_ge(pj_ev, q - 6)
                product(bank(q % 7)[:, 0:T], lambda k: w[:, k, P * (m % 4):P * (m % 4) + P], lambda k: xj[0][:, k, T:2 * T], KT).then_inc(pj_mm, 1)
                q += 1
            pe.wait_ge(lora1_in, 80)
            for i in range(3):
                pe.wait_ge(xj_ready, 32 + 8 * i)
                pe.wait_ge(pj_ev, q - 6)
                src = xj[(1, 0, 1)[i]]
                lo = T if i == 2 else 0
                product(bank(q % 7)[:, 0:2 * T - lo], lambda k: lora1[:, i, k, :], lambda k: src[:, k, lo:2 * T], KT).then_inc(pj_mm, 1)
                q += 1
            pe.wait_ge(pj_ev, q)
            pe.wait_ge(kk_ready, 1)
            pe.wait_ge(lora2_in, 80)

            def place(h):
                return 8 * (h // 8) + 4 * (h % 2) + h % 8 // 2

            def rows_of(h):
                return slice(64 * (h % 2), 64 * (h % 2) + 64)

            def low_rank(n):
                d, c = STEPS[n]
                rows = slice(64 * d, 64 * d + 64)
                for i, src in ((1, loa), (0, tanw)):
                    for m in range(8):
                        mm = pe.matmul(bank(4 * i + 1 + 2 * (m // 4))[:, P * (m % 4):P * (m % 4) + P], lora2[rows, i, P * m:P * m + P],
                                       src[rows, P * c:P * c + P], start=True, stop=True)
                        if m % 4 == 3:
                            mm.then_inc(z_mm, 1)

            low_rank(0)
            for n, (d, c) in enumerate(STEPS):
                lat, last, first = c >= 2, n % 4 == 3, n % 4 == 0
                more = n + 1 < len(STEPS)
                nl, ns = lat_before(n), handed_before(n)
                if n:
                    pe.wait_ge(u_ev, 2 * n)
                else:
                    pe.wait_ge(z_sig, 16)
                pe.wait_ge(til_r, n + 1)

                def pairs(left, right, b0):
                    for g in range(4):
                        for a in range(4):
                            h = 8 * (g // 2) + 2 * a + g % 2
                            mm = pe.matmul(bank(b0 + g)[:, P * a:P * a + P], left[rows_of(h), h // 2, :],
                                           right[rows_of(h), h // 2, :], start=True, stop=True)
                        mm.then_inc(pr_mm, 1)

                def by_head(at, m, left, right, with_state, done):
                    if with_state is not None:
                        pe.matmul(psum[:, at + P * m:at + P * m + P], with_state[:, m, :], S[:, m, :], start=True, stop=False,
                                  skip_group_check=True)
                    for h in (2 * m, 2 * m + 1):
                        mm = pe.matmul(psum[:, at + 64 * h:at + 64 * h + 64], left[:, place(h), :], right[:, 64 * h:64 * h + 64],
                                       start=with_state is None, stop=True, skip_group_check=with_state is not None)
                    if m % 4 == 3:
                        mm.then_inc(done, 1)

                base = 8 * n + 8 * nl
                pairs(KTl, AT, 0)
                if nl:
                    pe.wait_ge(y_ev, nl)
                if ns:
                    pe.wait_ge(s_ev, ns)
                if not last:
                    for j, src in enumerate((BT, BT, KTl, KTl)):
                        for m in range(4):
                            mm = pe.transpose(bank(4 + j)[:, P * m:P * m + P], src[:, 4 * (j % 2) + m, :], ident)
                        mm.then_inc(bk_T, 1)
                    pe.wait_ge(bk_tok, 4 * (ns + 1))
                if lat:
                    pairs(KTl, RT, 4)
                pe.wait_ge(pr_ev, base + 4)
                pe.wait_ge(s_mid, n + 1)
                for m in range(8):
                    by_head(0, m, buf1, V[:, c, :], None if first else AT, w1_mm)
                if lat:
                    pe.wait_ge(pr_ev, base + 8)
                    for m in range(8):
                        by_head(1024, m, buf2, V[:, c, :], RT, y1_mm)
                base += 8 if lat else 4
                pairs(BT, AT, 4)
                pe.wait_ge(w1_ev, n + 1)
                if lat:
                    pe.wait_ge(y1_ev, nl + 1)
                    pairs(BT, RT, 0)
                pe.wait_ge(pr_ev, base + 4)
                if lat:
                    pe.wait_ge(prod_r, nl + 1)
                    for m in range(8):
                        mm = pe.matmul(bank(6)[:, 2 * m:2 * m + 2], sig[:, m, :], rksel[:, m, :], start=True, stop=True)
                    mm.then_inc(bon_mm, 1)
                    pe.wait_ge(pr_ev, base + 8)
                if more:
                    low_rank(n + 1)

                def turn(src, i, g):
                    for a in range(4):
                        mm = pe.transpose(bank(2 * g)[:, P * a:P * a + P], src[:, 4 * g + a, :], ident)
                    mm.then_inc(tp_mm, 1)

                for g in range(4):
                    pe.wait_ge(xt2_r, 4 * n + g + 1)
                    if lat and g == 3:
                        pe.wait_ge(bon_ev, nl + 1)
                    turn(XT, 0, g)
                for l in range(5):
                    for g in range(4):
                        pe.wait_ge(tp_ev, 24 * n + 4 * l + g + 1)
                        for a in range(4):
                            h = 4 * g + a
                            mm = pe.matmul(bank(2 * g)[:, P * a:P * a + P], buf1[:, h, :], X[:, h, :], start=True, stop=True)
                        mm.then_inc(t1_mm, 1)
                    if l == 0 and more:
                        pe.wait_ge(z_sig, 16 * (n + 1) + 16)
                    for g in range(4):
                        pe.wait_ge(t1_ev, 24 * n + 4 * l + g + 1)
                        for a in range(4):
                            h = 4 * g + a
                            mm = pe.matmul(bank(2 * g + 1)[:, P * a:P * a + P], XT[:, h, :], T1[:, h, :], start=True, stop=True)
                        mm.then_inc(x_mm, 1)
                    for g in range(4):
                        pe.wait_ge(x_ev, 24 * n + 4 * l + g + 1)
                        turn(X, l + 1, g)
                pre, post = halves(d)
                for g in range(4):
                    pe.wait_ge(tp_ev, 24 * n + 20 + g + 1)
                    for a in range(4):
                        h = 4 * g + a
                        mm = pe.matmul(bank(2 * g)[post, P * a + pre.start:P * a + pre.stop], buf1[pre, h, post], X[pre, h, pre],
                                       start=True, stop=True)
                    mm.then_inc(t1_mm, 1)
                for g in range(4):
                    pe.wait_ge(t1_ev, 24 * n + 20 + g + 1)
                    for a in range(4):
                        h = 4 * g + a
                        mm = pe.matmul(bank(2 * g + 1)[pre, P * a + post.start:P * a + post.stop], T1[post, h, pre], XT[post, h, post],
                                       start=True, stop=True)
                    mm.then_inc(x_mm, 1)
                for hf in range(2):
                    for g in (2 * hf, 2 * hf + 1):
                        pe.wait_ge(x_ev, 24 * n + 20 + g + 1)
                        for a in range(4):
                            h = 8 * hf + 2 * a + g % 2
                            mm = pe.matmul(psum[:, 1024 + 64 * h:1024 + 64 * h + 64], XT[:, place(h), :], W[:, 64 * h:64 * h + 64],
                                           start=True, stop=True)
                    mm.then_inc(u_mm, 1)
                if not last:
                    for m in range(8):
                        ch = slice(P * m, P * m + P)
                        if m % 4 == 0:
                            pe.wait_ge(u_ev, 2 * n + m // 4 + 1)
                        pe.matmul(psum[:, 3072 + P * m:3072 + P * m + P], Btok[:, ch], U[:, ch], start=True, stop=False)
                        mm = pe.matmul(psum[:, 3072 + P * m:3072 + P * m + P], Ktok[:, ch], V[:, c, ch], start=False, stop=True)
                        if m % 4 == 3:
                            mm.then_inc(s_mm, 1)
                if lat:
                    pe.wait_ge(u_ev, 2 * n + 2)
                    for m in range(8):
                        by_head(2048, m, buf2, U, None, y_mm)

            pe.wait_ge(y_ev, 4)
            pe.wait_ge(s_ev, 6)
            for m in range(8):
                mm = pe.matmul(psum[:, 2048 + T * m:2048 + T * m + T], lora2[:, 2, P * m:P * m + P], sigg, start=True, stop=True)
                if m % 2 == 1:
                    mm.then_inc(g_mm, 1)
            pe.wait_ge(u_ev, 16)
            for t in (1, 0):
                pe.wait_ge(y_r, 2 - t)
                for k in range(KT):
                    mm = pe.transpose(bank(k // 2)[:, T * (k % 2) + P * t:T * (k % 2) + P * t + P], Yacc[:, t, P * k:P * k + P], ident)
                    if t == 0 and k % 2 == 1:
                        mm.then_inc(y_T, 1)
            pe.wait_ge(wo_in, 32)
            pe.wait_ge(yg_r, 4)
            for m in range(8):
                w = wo[m // 4].rearrange("p (k f) -> p k f", f=512)
                product(bank(4 + m // 2)[:, T * (m % 2):T * (m % 2) + T], lambda k: w[:, k, P * (m % 4):P * (m % 4) + P],
                        lambda k: ygT[:, k, :], KT).then_inc(o_mm, 1)

            def router(l, q):
                pe.wait_ge(small_in, 32)
                for k in range(KT):
                    pe.wait_ge(n_h, 8 * q + k + 1)
                    for t in range(2):
                        mm = pe.matmul(bank(1)[:, 16 * t:16 * t + 16], h2T[:, k, P * t:P * t + P], wr[:, k, :],
                                       start=(k == 0 and t == 0), stop=(k == KT - 1), skip_group_check=True)
                mm.then_inc(lg_mm, 1)
                for b in range(4):
                    for a in range(4):
                        mm = pe.transpose(bank(4 + b)[:, P * a:P * a + P],
                                          h2T[:, 4 * (b % 2) + a, P * (b // 2):P * (b // 2) + P], ident)
                    mm.then_inc(ht_mm, 1)
                pe.wait_ge(m_r, l + 1)
                M = [route[:, 384 + 16 * t:400 + 16 * t] for t in range(2)]
                R = bank(3)
                pe.matmul(R[:, 0:16], before, M[0], start=True, stop=True)
                for dest, first in ((R[:, 16:32], before), (R[:, 32:48], ones)):
                    pe.matmul(dest, first, M[1], start=True, stop=False)
                    mm = pe.matmul(dest, ones, M[0], start=False, stop=True)
                mm.then_inc(rank_mm, 1)

            def turn_gates(Q):
                pe.wait_ge(Q.picked, 4)
                for b in range(4):
                    for a in range(2):
                        for t in range(NT):
                            i = 2 * b + a
                            mm = pe.transpose(bank(4 + b)[:, T * a + P * t:T * a + P * t + P],
                                              gpick[:, t, P * i:P * i + P], ident)
                    mm.then_inc(Q.turned, 1)

            def gather(Q, i, given):
                pe.wait_ge(Q.given, given)
                for k in range(KT):
                    for t in range(NT):
                        mm = pe.matmul(psum[:, 2048 + P * k:2048 + P * k + P], h2tok[:, t, P * k:P * k + P],
                                       pick[:, t, 0:P] if i is None else pick[:, t, bass.ds(i * P, P)], start=(t == 0), stop=(t == NT - 1))
                mm.then_inc(Q.gathered, 1)

            def scatter(Q, q, i, opening=False):
                pe.wait_ge(Q.out, q + 1)
                for m in range(KT):
                    mm = pe.matmul(bank(m // 2)[:, T * (m % 2):T * (m % 2) + T], ye[:, P * m:P * m + P], giveT[:, i, :],
                                   start=(opening and m % 2 == 0), stop=False, skip_group_check=True)
                mm.then_inc(Q.scattered, 1)

            FIRST, SECOND = 0, 1

            def expert_pair(l, Q, q, weights):
                w = [ring[(U_EX[l] + n) % RING] for n in range(6)]
                if q is SECOND:
                    w[0:2] = ahead
                pe.wait_ge(Q.staged, q + 1)
                for j, done in enumerate((Q.gate, Q.up)):
                    weights(j)
                    for k in range(KT):
                        for e in range(2):
                            mm = pe.matmul(bank(4 + j)[SLOTS * e:SLOTS * e + SLOTS, :], xs[:, k, SLOTS * e:SLOTS * e + SLOTS],
                                           w[2 * j + e][:, FFN * k:FFN * k + FFN], start=(k == 0), stop=(k == KT - 1))
                    mm.then_inc(done, 1)
                pe.wait_ge(Q.hidden, q + 1)
                for k in range(FT):
                    mm = pe.transpose(bank(6)[:, P * k:P * k + P], he[:, P * k:P * k + P], ident)
                mm.then_inc(Q.hidden_turned, 1)
                weights(2)
                pe.wait_ge(Q.hidden_ready, q + 1)
                for hf in range(2):
                    for k in range(FT):
                        for e in range(2):
                            mm = pe.matmul(bank(6 + hf)[SLOTS * e:SLOTS * e + SLOTS, :], heT[:, k, SLOTS * e:SLOTS * e + SLOTS],
                                           w[4 + e][:, D * k + 512 * hf:D * k + 512 * hf + 512],
                                           start=(k == 0), stop=(k == FT - 1))
                mm.then_inc(Q.down, 1)

            def moe(l):
                def weights(i):
                    def wait(j):
                        if i is SECOND and j == 0:
                            pe.wait_ge(ahead_in, 32 * (l + 1))
                            return
                        for e in range(2):
                            n = U_EX[l] + 2 * j + e
                            pe.wait_ge(loaded[n % RING], i * 16 + landings(n) - (16 if j == 0 and i is not FIRST else 0))
                    return wait

                Q = moe_s[l]
                pe.wait_ge(ht_r, 4 * (l + 1))
                turn_gates(Q)
                gather(Q, 0, 4)
                expert_pair(l, Q, FIRST, weights(FIRST))
                gather(Q, 1, 4)
                scatter(Q, 0, 0, opening=True)
                expert_pair(l, Q, SECOND, weights(SECOND))
                with pe.Fori(2, PAIRS) as i:
                    gather(Q, i, 4)
                    scatter(Q, i - 1, i - 1)
                    expert_pair(l, Q, i, weights(i))
                scatter(Q, PAIRS - 1, PAIRS - 1)
                n_more = further(pe, l)
                with pe.Fori(0, MORE) as i:
                    with pe.If(n_more > i):
                        pe.wait_ge(Q.picked, i * 11 + 15)
                        for t in range(NT):
                            mm = pe.transpose(bank(4)[:, P * t:P * t + P], gpick[:, t, 0:P], ident)
                        mm.then_inc(Q.turned, 1)
                        gather(Q, None, i + 5)
                        expert_pair(l, Q, i + PAIRS, lambda j: pe.wait_ge(more_in[l], i * 96 + 96))
                        scatter(Q, i + PAIRS, 0)

            norm(2, sq)
            router(0, 2)
            moe(0)
            modulation1(range(EARLY))
            norm(3, sq)
            pe.wait_ge(n_rt, 4)
            pe.wait_ge(x_tile, 16)
            for m in range(16):
                n = U_WIN + m // 4
                landed(pe, n)
                w = ring[n % RING].rearrange("p (k f) -> p k f", f=512)
                for k in range(KT):
                    if m == 0:
                        pe.wait_ge(n_h, 24 + k + 1)
                    mm = pe.matmul(bank(m // 2)[:, T * (m % 2):T * (m % 2) + T], w[:, k, P * (m % 4):P * (m % 4) + P], h2T[:, k, :],
                                   start=(k == 0), stop=(k == KT - 1))
                mm.then_inc(u_pj, 1)
            for q in range(8):
                u, t = q // 2, q % 2
                n = U_WIN + 4 + u
                landed(pe, n)
                pe.wait_ge(u_gl, 2 * q + 2)
                w = ring[n % RING].rearrange("p (k f) -> p k f", f=512)
                product(bank(q), lambda k: h2T[:, k, P * t:P * t + P], lambda k: w[:, k, :], KT).then_inc(v_pj, 1)
            landed(pe, U_WS)
            wsr = ring[U_WS % RING][:, 0:VG * P].rearrange("p (g j) -> p g j", j=P)
            for b in range(4):
                pe.wait_ge(v_add, b + 1)
                for a in range(4):
                    mm = pe.transpose(bank(b)[:, P * a:P * a + P], wsr[:, 4 * b + a, :], ident)
                mm.then_inc(ws_tr, 1)
            pe.wait_ge(v_add, 8)
            modulation1(range(EARLY, 12))
            pe.wait_ge(ws_ev, 4)
            pe.wait_ge(v_ln, 2)
            for g in range(VG):
                if g >= 8:
                    pe.wait_ge(sp_ev, g // 2 * 2 - 6)
                if g == 6:
                    pe.wait_ge(mods_r, 5)
                for t in range(2):
                    dest = bank(4 + g // 2 % 4)[:, T * (g % 2) + P * t:T * (g % 2) + P * t + P]
                    pe.matmul(dest, vtok[:, t, P * g:P * g + P], wsT[:, g, :], start=True, stop=False)
                    mm = pe.matmul(dest, ones[0:1, :], bsrow[0:1, P * g:P * g + P], start=False, stop=True)
                mm.then_inc(sp_mm, 1)
            for u in range(4):
                n = U_WOUT + u
                landed(pe, n)
                pe.wait_ge(sp_ev, 4 * u + 4)
                w = ring[n % RING].rearrange("p (k f) -> p k f", f=D)
                for m in range(KT):
                    for k in range(4):
                        mm = pe.matmul(bank(m // 2)[:, T * (m % 2):T * (m % 2) + T], w[:, k, P * m:P * m + P],
                                       uT[:, 4 * u + k, :], start=(u == 0 and k == 0 and m % 2 == 0), stop=False,
                                       skip_group_check=True)
                mm.then_inc(go_mm, 1)
            norm(4, sq)
            router(1, 4)
            moe(1)
            norm(5, sq)
            for j in range(2):
                for k in range(4 * j, 4 * j + 4):
                    pe.wait_ge(n_h, 40 + k + 1)
                    for t in range(2):
                        mm = pe.transpose(psum[:, 1024 + 1024 * t + P * k:1024 + 1024 * t + P * k + P],
                                          h2T[:, k, P * t:P * t + P], ident)
                mm.then_inc(f_T, 1)


_INS = ["x", "c", "ctx", "c_ctx", "w_mod", "b_mod", "norm1_g", "norm2_g", "rw_mu", "rw_wr", "rw_wk", "rw_wv", "rw_wo",
        "rw_w0", "rw_w1", "rw_w2", "rw_a0", "rw_a1", "rw_a2", "rw_g1", "rw_g2", "rw_kk", "rw_ka", "rw_rk", "rw_lnx_g",
        "rw_lnx_b", "sg_w_in", "sg_b_in", "sg_ln_g", "sg_ln_b", "sg_w_s", "sg_b_s", "sg_w_out", "w_router",
        "router_bias", "ex_w_gate", "ex_w_up", "ex_w_down", "final_g"]


def kernel(**inputs):
    import numpy as np
    import concourse.bacc as bacc
    from concourse.bass_utils import run_bass_kernel_spmd as run

    nc = bacc.Bacc("TRN2", target_bir_lowering=False, num_devices=1)
    arrays, aps = {}, {}
    for name in _INS:
        a = np.ascontiguousarray(inputs[name])
        arrays[f"in_{name}"] = a
        aps[name] = nc.dram_tensor(f"in_{name}", a.shape, mybir.dt.from_np(a.dtype), kind="ExternalInput").ap()
    out = nc.dram_tensor("out_0", (1, T, D), F32, kind="ExternalOutput").ap()
    build(nc, aps, out)
    return run(nc, [arrays], core_ids=[0]).results[0]["out_0"]
```
